# Optimizing a Trainium2 kernel written in Bass

```python
import math
import jax
import jax.numpy as jnp
from jax import lax
import numpy as np

D_MODEL = 2048
BATCH = 1
SEQ = 256
DEPTH = 2

MIX_WIDTH = D_MODEL
N_MIXERS = 4
GROUP_WIDTH = MIX_WIDTH // N_MIXERS
FN_HEADS = 4
FN_HEAD_DIM = GROUP_WIDTH // FN_HEADS
S5_GROUP_CH = 16
S5_GROUPS = GROUP_WIDTH // S5_GROUP_CH
S5_STATE = 64
HEAD_DIM = 128
ATT_HEADS = GROUP_WIDTH // HEAD_DIM
KV_HEADS = ATT_HEADS // 2
Q_BLOCK = 128
GRID_W = 64
ROPE_THETA = 10000.0
AXIS_ROT_DIM = HEAD_DIM // 2
RW_HEAD_DIM = 64
RW_HEADS = GROUP_WIDTH // RW_HEAD_DIM
RW_DECAY_LORA = 32
RW_AICL_LORA = 32
RW_GATE_LORA = 96
RW_GN_EPS = 64e-5
PEER_HEADS = 8
PEER_KEY_DIM = 128
PEER_HALF = PEER_KEY_DIM // 2
PEER_N_KEYS = 128
PEER_EXPERTS = PEER_N_KEYS * PEER_N_KEYS
PEER_TOPK = 16
PEER_CHUNK = 128
NORM_EPS = 1e-6

COL_SIZES = (GROUP_WIDTH, GROUP_WIDTH, ATT_HEADS * HEAD_DIM, KV_HEADS * HEAD_DIM,
             KV_HEADS * HEAD_DIM, GROUP_WIDTH, GROUP_WIDTH, GROUP_WIDTH, GROUP_WIDTH)
PROJ_WIDTH = sum(COL_SIZES)
SPLIT_POINTS = tuple(sum(COL_SIZES[:i + 1]) for i in range(len(COL_SIZES) - 1))

kernel_name = 'hymba_style_hybrid_encoder_peer'

def rms_norm(x, gain):
    xf = x.astype(jnp.float32)
    y = xf * lax.rsqrt(jnp.mean(xf * xf, axis=-1, keepdims=True) + NORM_EPS)
    return (y * gain.astype(jnp.float32)).astype(x.dtype)

def fourier_mix(u, w_f):
    bn, s, _ = u.shape
    uh = u.astype(jnp.float32).reshape(bn, s, FN_HEADS, FN_HEAD_DIM)
    f = jnp.fft.fft2(uh, axes=(1, 3), norm='ortho').real
    return f.reshape(bn, s, GROUP_WIDTH).astype(u.dtype) @ w_f

def _ssm_combine(e1, e2):
    a1, b1 = e1
    a2, b2 = e2
    return a1 * a2, a2 * b1 + b2

def s5_mix(u, lam_re, lam_im, log_step, b_re, b_im, c_re, c_im, d_skip, w_glu):
    f32 = jnp.float32
    bn, s, _ = u.shape
    uf = u.astype(f32).reshape(bn, s, S5_GROUPS, S5_GROUP_CH)
    uc = uf.astype(jnp.complex64)
    ys = []
    for d in range(2):
        lam = lax.complex(lam_re[d].astype(f32), lam_im[d].astype(f32))
        step = jnp.exp(log_step[d].astype(f32))[:, None]
        lam_bar = jnp.exp(lam * step)
        bmat = lax.complex(b_re[d].astype(f32), b_im[d].astype(f32))
        b_bar = ((lam_bar - 1.0) / lam)[..., None] * bmat
        bu = jnp.einsum('gph,bsgh->bsgp', b_bar, uc)
        a = jnp.broadcast_to(lam_bar, bu.shape)
        _, states = lax.associative_scan(_ssm_combine, (a, bu), reverse=(d == 1), axis=1)
        cmat = lax.complex(c_re[d].astype(f32), c_im[d].astype(f32))
        ys.append(jnp.einsum('ghp,bsgp->bsgh', cmat, states).real)
    y = ys[0] + ys[1] + d_skip.astype(f32) * uf
    y = jax.nn.gelu(y.reshape(bn, s, GROUP_WIDTH)).astype(u.dtype)
    return y * jax.nn.sigmoid(y @ w_glu)

def axial_rope_tables(seq_len):
    rows = seq_len // GRID_W
    row_id = jnp.repeat(jnp.arange(rows), GRID_W).astype(jnp.float32)
    col_id = jnp.tile(jnp.arange(GRID_W), rows).astype(jnp.float32)
    inv = ROPE_THETA ** (-jnp.arange(0, AXIS_ROT_DIM, 2, dtype=jnp.float32) / AXIS_ROT_DIM)
    ang = jnp.concatenate([row_id[:, None] * inv, col_id[:, None] * inv], axis=-1)
    return jnp.cos(ang), jnp.sin(ang)

def apply_rope(x, cos, sin):
    xf = x.astype(jnp.float32)
    half = HEAD_DIM // 2
    x1, x2 = xf[..., :half], xf[..., half:]
    c = cos[None, :, None, :]
    s = sin[None, :, None, :]
    return jnp.concatenate([x1 * c - x2 * s, x1 * s + x2 * c], axis=-1).astype(x.dtype)

def block_attention(q, k, v):
    bn, s, _, _ = q.shape
    rep = ATT_HEADS // KV_HEADS
    nb = s // Q_BLOCK
    qb = q.reshape(bn, nb, Q_BLOCK, KV_HEADS, rep, HEAD_DIM).transpose(1, 0, 2, 3, 4, 5)
    scale = HEAD_DIM ** -0.5

    def one_block(qblk):
        sc = jnp.einsum('bqgrd,bkgd->bgrqk', qblk, k, preferred_element_type=jnp.float32) * scale
        p = jax.nn.softmax(sc, axis=-1).astype(v.dtype)
        return jnp.einsum('bgrqk,bkgd->bqgrd', p, v)

    o = lax.map(one_block, qb)
    return o.transpose(1, 0, 2, 3, 4, 5).reshape(bn, s, ATT_HEADS * HEAD_DIM)

def attention_mix(q, k, v, q_gain, k_gain, cos, sin):
    bn, s, _ = q.shape
    q = q.reshape(bn, s, ATT_HEADS, HEAD_DIM)
    k = k.reshape(bn, s, KV_HEADS, HEAD_DIM)
    v = v.reshape(bn, s, KV_HEADS, HEAD_DIM)
    q = apply_rope(rms_norm(q, q_gain), cos, sin)
    k = apply_rope(rms_norm(k, k_gain), cos, sin)
    return block_attention(q, k, v)

def centred_shift(x, mu):
    prev = jnp.pad(x[:, :-1], ((0, 0), (1, 0), (0, 0)))
    nxt = jnp.pad(x[:, 1:], ((0, 0), (0, 1), (0, 0)))
    return x + (prev - x) * mu[0] + (nxt - x) * mu[1]

def rwkv_scan(r, w, k, v, kk, b, reverse):
    bn, _, h, n = r.shape

    def step(state, inp):
        r_t, w_t, k_t, v_t, kk_t, b_t = inp
        sa = jnp.einsum('bhvk,bhk->bhv', state, -kk_t)
        state = (state * w_t[:, :, None, :] + sa[..., None] * b_t[:, :, None, :]
                 + v_t[..., None] * k_t[:, :, None, :])
        return state, jnp.einsum('bhvk,bhk->bhv', state, r_t)

    s0 = jnp.zeros((bn, h, n, n), jnp.float32)
    xs = tuple(jnp.moveaxis(t, 1, 0) for t in (r, w, k, v, kk, b))
    _, ys = lax.scan(step, s0, xs, reverse=reverse)
    return jnp.moveaxis(ys, 0, 1)

def rwkv7_mix(r, k, v, z, mu, w0, w1, w2, a0, a1, a2, g1, g2, k_k, k_a, r_k, ln_w, ln_b):
    f32 = jnp.float32
    bn, s, c = r.shape
    r = centred_shift(r, mu[0])
    k = centred_shift(k, mu[1])
    v = centred_shift(v, mu[2])
    z = centred_shift(z, mu[3])

    def heads(t):
        return t.astype(f32).reshape(bn, s, RW_HEADS, RW_HEAD_DIM)

    g = jax.nn.sigmoid(z @ g1) @ g2
    kk = heads(k * k_k)
    kk = kk * lax.rsqrt(jnp.sum(kk * kk, axis=-1, keepdims=True) + 1e-12)
    rh = heads(r)
    vh = heads(v)
    ys = []
    bonuses = []
    for d in range(2):
        w_log = -jax.nn.softplus(-(w0[d] + jnp.tanh(z @ w1[d]) @ w2[d])) - 0.5
        decay = heads(jnp.exp(-jnp.exp(w_log.astype(f32))))
        a = jax.nn.sigmoid(a0[d] + (z @ a1[d]) @ a2[d])
        kd = heads(k * (1.0 + (a - 1.0) * k_a))
        ys.append(rwkv_scan(rh, decay, kd, vh, kk, kk * heads(a), reverse=(d == 1)))
        bonuses.append(jnp.sum(rh * kd * r_k.astype(f32), axis=-1, keepdims=True) * vh)
    y = ys[0] + ys[1]
    mean = jnp.mean(y, axis=-1, keepdims=True)
    var = jnp.mean(jnp.square(y - mean), axis=-1, keepdims=True)
    yn = ((y - mean) * lax.rsqrt(var + RW_GN_EPS)).reshape(bn, s, c)
    yn = yn * ln_w.astype(f32) + ln_b.astype(f32)
    out = (yn + (bonuses[0] + bonuses[1]).reshape(bn, s, c)) * g.astype(f32)
    return out.astype(r.dtype)

def peer_ffn(h, w_query, sub_keys, expert_u, expert_v):
    bn, s, d = h.shape
    xt = h.reshape(bn * s // PEER_CHUNK, PEER_CHUNK, d)
    kk2 = PEER_TOPK * PEER_TOPK

    def chunk(xc):
        q = (xc @ w_query).reshape(PEER_CHUNK, PEER_HEADS, 2, PEER_HALF)
        sc = jnp.einsum('chpd,hpkd->chpk', q, sub_keys, preferred_element_type=jnp.float32)
        s1, i1 = lax.top_k(sc[:, :, 0], PEER_TOPK)
        s2, i2 = lax.top_k(sc[:, :, 1], PEER_TOPK)
        cand_s = (s1[..., :, None] + s2[..., None, :]).reshape(PEER_CHUNK, PEER_HEADS, kk2)
        cand_i = (i1[..., :, None] * PEER_N_KEYS + i2[..., None, :]).reshape(PEER_CHUNK, PEER_HEADS, kk2)
        top_s, pos = lax.top_k(cand_s, PEER_TOPK)
        idx = jnp.take_along_axis(cand_i, pos, axis=-1)
        gate = jax.nn.softmax(top_s, axis=-1)
        u = jnp.take(expert_u, idx, axis=0)
        act = jax.nn.gelu(jnp.einsum('chkd,cd->chk', u, xc, preferred_element_type=jnp.float32),
                          approximate=False)
        vsel = jnp.take(expert_v, idx, axis=0)
        return jnp.einsum('chk,chkd->cd', (gate * act).astype(xc.dtype), vsel)

    return lax.map(chunk, xt).reshape(bn, s, d)

def setup_inputs(seed: int = 0) -> dict:
    key = jax.random.key(seed)
    keys = list(jax.random.split(key, 48))
    f32 = jnp.float32
    L = DEPTH
    G, P, GW = S5_GROUPS, S5_STATE, GROUP_WIDTH

    def nrm(shape, scale):
        return scale * jax.random.normal(keys.pop(), shape, f32)

    def gain(shape):
        return 1.0 + nrm(shape, 0.02)

    w0_base = -6.5 + 5.0 * jnp.linspace(0.0, 1.0, GW, dtype=f32) ** 0.9
    return {
        'x': nrm((BATCH, SEQ, D_MODEL), 1.0),
        'norm_mix': gain((L, D_MODEL)),
        'w_in': nrm((L, D_MODEL, PROJ_WIDTH), D_MODEL ** -0.5),
        'fourier_w': nrm((L, GW, GW), GW ** -0.5),
        's5_lam_re': -0.5 + nrm((L, 2, G, P), 0.01),
        's5_lam_im': jnp.pi * jnp.arange(P, dtype=f32) + nrm((L, 2, G, P), 0.01),
        's5_log_step': jax.random.uniform(keys.pop(), (L, 2, G), f32,
                                          minval=math.log(1e-3), maxval=math.log(1e-1)),
        's5_b_re': nrm((L, 2, G, P, S5_GROUP_CH), (2 * S5_GROUP_CH) ** -0.5),
        's5_b_im': nrm((L, 2, G, P, S5_GROUP_CH), (2 * S5_GROUP_CH) ** -0.5),
        's5_c_re': nrm((L, 2, G, S5_GROUP_CH, P), P ** -0.5),
        's5_c_im': nrm((L, 2, G, S5_GROUP_CH, P), P ** -0.5),
        's5_d': nrm((L, G, S5_GROUP_CH), 1.0),
        's5_w_glu': nrm((L, GW, GW), GW ** -0.5),
        'attn_q_norm': gain((L, HEAD_DIM)),
        'attn_k_norm': gain((L, HEAD_DIM)),
        'rwkv_mu': jax.random.uniform(keys.pop(), (L, 4, 2, GW), f32, minval=0.0, maxval=0.5),
        'rwkv_w0': w0_base + nrm((L, 2, GW), 0.1),
        'rwkv_w1': nrm((L, 2, GW, RW_DECAY_LORA), GW ** -0.5),
        'rwkv_w2': nrm((L, 2, RW_DECAY_LORA, GW), 0.1 * RW_DECAY_LORA ** -0.5),
        'rwkv_a0': nrm((L, 2, GW), 0.1),
        'rwkv_a1': nrm((L, 2, GW, RW_AICL_LORA), GW ** -0.5),
        'rwkv_a2': nrm((L, 2, RW_AICL_LORA, GW), RW_AICL_LORA ** -0.5),
        'rwkv_g1': nrm((L, GW, RW_GATE_LORA), GW ** -0.5),
        'rwkv_g2': nrm((L, RW_GATE_LORA, GW), RW_GATE_LORA ** -0.5),
        'rwkv_k_k': 0.85 + nrm((L, GW), 0.02),
        'rwkv_k_a': gain((L, GW)),
        'rwkv_r_k': nrm((L, RW_HEADS, RW_HEAD_DIM), 0.1),
        'rwkv_ln_w': gain((L, GW)),
        'rwkv_ln_b': nrm((L, GW), 0.02),
        'branch_norm': gain((L, MIX_WIDTH)),
        'w_out': nrm((L, MIX_WIDTH, D_MODEL), MIX_WIDTH ** -0.5),
        'norm_ffn': gain((L, D_MODEL)),
        'peer_w_query': nrm((L, D_MODEL, PEER_HEADS * PEER_KEY_DIM), D_MODEL ** -0.5),
        'peer_sub_keys': nrm((L, PEER_HEADS, 2, PEER_N_KEYS, PEER_HALF), PEER_HALF ** -0.5),
        'peer_u': nrm((L, PEER_EXPERTS, D_MODEL), D_MODEL ** -0.5),
        'peer_v': nrm((L, PEER_EXPERTS, D_MODEL), PEER_HEADS ** -0.5),
    }

def reference(x, norm_mix, w_in, fourier_w, s5_lam_re, s5_lam_im, s5_log_step, s5_b_re, s5_b_im,
              s5_c_re, s5_c_im, s5_d, s5_w_glu, attn_q_norm, attn_k_norm, rwkv_mu, rwkv_w0,
              rwkv_w1, rwkv_w2, rwkv_a0, rwkv_a1, rwkv_a2, rwkv_g1, rwkv_g2, rwkv_k_k, rwkv_k_a,
              rwkv_r_k, rwkv_ln_w, rwkv_ln_b, branch_norm, w_out, norm_ffn, peer_w_query,
              peer_sub_keys, peer_u, peer_v):
    bn, s, _ = x.shape
    cos, sin = axial_rope_tables(s)
    for l in range(DEPTH):
        h = rms_norm(x, norm_mix[l])
        proj = h @ w_in[l]
        pa, pb, pq, pk, pv, rr, rk, rv, rz = jnp.split(proj, SPLIT_POINTS, axis=-1)
        ya = fourier_mix(pa, fourier_w[l])
        yb = s5_mix(pb, s5_lam_re[l], s5_lam_im[l], s5_log_step[l], s5_b_re[l], s5_b_im[l],
                    s5_c_re[l], s5_c_im[l], s5_d[l], s5_w_glu[l])
        yc = attention_mix(pq, pk, pv, attn_q_norm[l], attn_k_norm[l], cos, sin)
        yd = rwkv7_mix(rr, rk, rv, rz, rwkv_mu[l], rwkv_w0[l], rwkv_w1[l], rwkv_w2[l],
                       rwkv_a0[l], rwkv_a1[l], rwkv_a2[l], rwkv_g1[l], rwkv_g2[l],
                       rwkv_k_k[l], rwkv_k_a[l], rwkv_r_k[l], rwkv_ln_w[l], rwkv_ln_b[l])
        ycat = jnp.stack([ya, yb, yc.astype(ya.dtype), yd.astype(ya.dtype)], axis=2)
        ycat = rms_norm(ycat, branch_norm[l].reshape(N_MIXERS, GROUP_WIDTH))
        x = x + ycat.reshape(bn, s, MIX_WIDTH) @ w_out[l]
        x = x + peer_ffn(rms_norm(x, norm_ffn[l]), peer_w_query[l], peer_sub_keys[l],
                         peer_u[l], peer_v[l])
    return x


_drawn_inputs = setup_inputs


def setup_inputs(seed=0):
    import zlib

    import numpy as np

    out = dict(_drawn_inputs(seed))
    spreads = {}
    factors = {'s5_lam_re': 8.0,
     'attn_q_norm': 3.114,
     'attn_k_norm': 3.223,
     'rwkv_w1': 4.982,
     'rwkv_w2': 4.577,
     'rwkv_k_k': 2.823,
     'rwkv_ln_w': 3.018}
    for name, (base, spread) in spreads.items():
        noise = np.random.default_rng([zlib.crc32(name.encode()), seed]).standard_normal(out[name].shape)
        drawn = base * np.exp(spread * noise) if base else spread * noise
        out[name] = jnp.asarray(drawn.astype(out[name].dtype))
    for name, factor in factors.items():
        out[name] = (out[name] * factor).astype(out[name].dtype)
    return out
```

```python
import math
from contextlib import ExitStack

import numpy as np

import concourse.bass as bass
from concourse import mybir

P = 128
F32 = mybir.dt.float32
U32 = mybir.dt.uint32
ALU = mybir.AluOpType
ACT = mybir.ActivationFunctionType
AX = mybir.AxisListType

DEPTH, SEQ, D = 2, 256, 2048
TB = SEQ // P
KT = D // P
GW = 512
GT = GW // P
PROJ = 4096
PT = PROJ // P
NORM_EPS = 1e-6
HEAD = 128
SCALE = HEAD ** -0.5
S5P, S5C, S5G = 64, 16, 32
CH = 32
NCH = SEQ // CH
CPB = P // CH
RH = 64
PEER_H, KEYS, TOPK = 8, 128, 16
EXPERTS = KEYS * KEYS
RING = 8
HALF_K = 8
WRING = 3

T_A, T_B, T_Q, T_K, T_V, T_R, T_RK, T_RV, T_RZ = 0, 4, 8, 12, 14, 16, 20, 24, 28

ROWS = {}
for _name, _n in (("norm_mix", 16), ("norm_ffn", 16), ("mu", 32), ("w0", 8), ("a0", 8), ("k_k", 4), ("k_a", 4),
                  ("r_k", 4), ("ln_w", 4), ("ln_b", 4), ("branch", 16), ("s5_d", 4), ("q_norm", 1), ("k_norm", 1)):
    ROWS[_name] = (sum(n for _, n in ROWS.values()), _n)
NROWS = sum(n for _, n in ROWS.values())
assert NROWS <= P


def constants():
    p = np.arange(P)[:, None]
    q = np.arange(P)[None, :]
    parts = {"ident": p == q, "ones": np.ones((P, P)), "heads": p // RH == q // RH}
    half = HEAD // 2
    parts["rot"] = np.where(p == q + half, -1.0, 0.0) + np.where(p == q - half, 1.0, 0.0)
    t = np.arange(SEQ)
    inv = 10000.0 ** (-np.arange(0, half, 2, dtype=np.float32) / half)
    ang = np.concatenate([(t // 64)[:, None] * inv, (t % 64)[:, None] * inv], axis=-1).astype(np.float32)
    parts["cos"] = np.tile(np.cos(ang).T, (2, 1))
    parts["sin"] = np.tile(np.sin(ang).T, (2, 1))
    ch = 2 * np.pi * p * q / P
    s = 1 / math.sqrt(SEQ * P)
    parts["dft_ch"] = np.concatenate([np.cos(ch), np.sin(ch)], 1) * s
    sq = np.concatenate([2 * np.pi * (p + b * P) * t[None, :] / SEQ for b in range(TB)], 1).reshape(P, TB, SEQ)
    parts["dft_seq"] = np.concatenate([np.cos(sq), -np.sin(sq)], 2).reshape(P, TB * 2 * SEQ)
    s16, s32 = p // 16 == q // 16, p // CH == q // CH
    parts["m16U"], parts["m16L"] = s16 & (q > p), s16 & (q < p)
    parts["mXU"], parts["mXL"] = s32 & ~s16 & (q > p), s32 & ~s16 & (q < p)
    parts["m32U"], parts["m32L"] = s32 & (q > p), s32 & (q < p)
    parts["m32Ui"], parts["m32Li"] = s32 & (q >= p), s32 & (q <= p)
    parts["ident64"] = (p % RH) == np.arange(RH)[None, :]
    parts["iota16"] = np.tile(np.arange(16)[None, :], (P, 1))
    parts["even"] = (p // S5C) % 2 == 0
    parts["odd"] = (p // S5C) % 2 == 1
    parts["eps"] = np.full((P, 1), NORM_EPS)
    parts["eps_kk"] = np.full((P, 1), 1e-12)
    parts["eps_gn"] = np.full((P, 1), 64e-5)
    where, at = {}, 0
    for k, v in parts.items():
        where[k] = (at, at + v.shape[1])
        at += v.shape[1]
    return np.concatenate([np.asarray(v, np.float64) for v in parts.values()], 1).astype(np.float32), where


class Steps:

    def __init__(self, engine, own):
        self.engine, self.own, self.count = engine, own, {}

    def __call__(self, instruction, sem=None, wait=True):
        sem = self.own if sem is None else sem
        instruction.then_inc(sem, 1)
        self.count[sem.name] = self.count.get(sem.name, 0) + 1
        if wait:
            self.engine.wait_ge(sem, self.count[sem.name])


def build(nc, t, out):
    _, where = constants()
    whole = ExitStack()
    with whole:
        first_sem = []

        def sem(name):
            s = whole.enter_context(nc.semaphore(name))
            first_sem.append(s)
            return s

        def sb(stack, name, shape, dt=F32):
            return stack.enter_context(nc.sbuf_tensor(name, shape, dt))

        def ps(stack, name, shape, dt=F32):
            return stack.enter_context(nc.psum_tensor(name, shape, dt))

        x = sb(whole, "x", [P, TB, D])
        consts = sb(whole, "consts", [P, where["eps_gn"][1]])
        pcol = sb(whole, "pcol", [P, NROWS])
        mus = sb(whole, "mus", [P, 16])
        layer_base = sb(whole, "layer_base", [P, 1])

        def c(name, a=None, b=None):
            lo, hi = where[name]
            return consts[:, lo if a is None else lo + a:hi if b is None else lo + b]

        def col(name, i=0, n=1):
            at = ROWS[name][0] + i
            return pcol[:, at:at + n]

        loaded, base_set, stored = sem("loaded"), sem("base_set"), sem("stored")
        with nc.Block() as block:
            @block.sync
            def _(sp):
                sp.dma_start(consts[:], t["consts"]).then_inc(loaded, 16)
                sp.dma_start(x[:], t["x"][0].rearrange("(b p) d -> p b d", p=P)).then_inc(loaded, 16)
                sp.wait_ge(loaded, 32)

            @block.vector
            def _(dve):
                dve.memset(layer_base[:], 0.0).then_inc(base_set, 1)
                dve.wait_ge(base_set, 1)

        row_in = [sem(f"row_in{i}") for i in range(RING)]
        kept = len(first_sem)
        with nc.Fori(0, DEPTH) as layer:
            rw = ExitStack()
            ycT = sb(rw, "ycT", [P, 16, SEQ])
            rwT = sb(rw, "rwT", [P, 16, SEQ])
            mix = ExitStack()
            mixT = sb(mix, "mixT", [P, 16, SEQ])
            tab = ExitStack()
            s5 = {"cos": sb(tab, "s5cos", [P, 32, SEQ]), "sin": sb(tab, "s5sin", [P, 32, SEQ]),
                  "v": sb(tab, "s5v", [P, 24, 32])}
            project(nc, t, layer, sem, sb, ps, c, col, x, pcol, mus, mixT, rwT, s5)
            attend(nc, t, layer, sem, sb, ps, c, col, mixT, ycT)
            s5_branch(nc, t, layer, sem, sb, ps, c, col, mixT, ycT, s5)
            tab.close()
            mix.close()
            rwkv(nc, t, layer, sem, sb, ps, c, col, mus, rwT, ycT)
            route_kept = ExitStack()
            h2 = sb(route_kept, "h2", [P, TB, D])
            index = sb(route_kept, "index", [P, TB, PEER_H, TOPK], U32)
            gate = sb(route_kept, "gate", [P, TB, PEER_H, TOPK])
            route(nc, t, layer, sem, sb, ps, c, col, x, ycT, h2, index, gate, layer_base)
            experts(nc, t, layer, sem, sb, row_in, x, h2, index, gate)
            route_kept.close()
            rw.close()
            with nc.Block() as block:
                @block.sync
                def _(sp):
                    for s in first_sem[kept:]:
                        sp.sem_clear(s)

        with nc.Block() as block:
            @block.sync
            def _(sp):
                sp.dma_start(out[0].rearrange("(b p) d -> p b d", p=P), x[:]).then_inc(stored, 16)
                sp.wait_ge(stored, 16)


def project(nc, t, layer, sem, sb, ps, c, col, x, pcol, mus, mixT, rwT, s5):
    rows_in, slab_in = sem("pj_rows_in"), [sem(f"pj_slab_in{i}") for i in range(WRING)]
    rows_T, cols_ready = sem("pj_rows_T"), sem("pj_cols_ready")
    h_ready, hT_mm, hT_ready = sem("pj_h_ready"), sem("pj_hT_mm"), sem("pj_hT_ready")
    rms_ready, slab_used, proj_mm, proj_out = sem("pj_rms"), sem("pj_slab_used"), sem("pj_mm"), sem("pj_out")
    ls_ready, s5_act = sem("pj_ls_ready"), sem("pj_s5_act")
    s5_arg = sem("pj_s5_arg")
    dve_own, act_own = sem("pj_dve"), sem("pj_act")
    with ExitStack() as st:
        rows = sb(st, "pj_rows", [P, P])
        srow = sb(st, "pj_srow", [96, P])
        ls2 = sb(st, "pj_ls2", [96, 2])
        h = sb(st, "pj_h", [P, D])
        hT = sb(st, "pj_hT", [P, KT, SEQ])
        slab = sb(st, "pj_slab", [P, 2, HALF_K, GW])
        ssq = sb(st, "pj_ssq", [P, 8])
        tmp = h[:].rearrange("p (a n) -> p a n", a=2)
        bank = ps(st, "pj_bank", [P, 8, 512])
        ROW_SRC = [("norm_mix", t["norm_mix"]), ("norm_ffn", t["norm_ffn"]), ("mu", t["rwkv_mu"]), ("w0", t["rwkv_w0"]),
                   ("a0", t["rwkv_a0"]), ("k_k", t["rwkv_k_k"]), ("k_a", t["rwkv_k_a"]), ("r_k", t["rwkv_r_k"]),
                   ("ln_w", t["rwkv_ln_w"]), ("ln_b", t["rwkv_ln_b"]), ("branch", t["branch_norm"]),
                   ("s5_d", t["s5_d"]), ("q_norm", t["attn_q_norm"]), ("k_norm", t["attn_k_norm"])]
        NS = 2
        N_SLABS = PROJ // GW * 2

        with nc.Block() as block:
            @block.sync
            def _(sp):
                for name, src in ROW_SRC:
                    a, n = ROWS[name]
                    v = src[layer]
                    v = {1: lambda v: v, 2: lambda v: v.rearrange("a b -> (a b)"),
                         3: lambda v: v.rearrange("a b c -> (a b c)")}[len(v.shape)](v)
                    sp.dma_start(rows[a:a + n, :], v.rearrange("(n p) -> n p", p=P)).then_inc(rows_in, 16)
                for i, name in enumerate(("s5_lam_re", "s5_lam_im")):
                    sp.dma_start(srow[32 * i:32 * i + 32, :],
                                 t[name][layer].rearrange("d (g e) p -> (d g) (e p)", e=2)).then_inc(rows_in, 16)
                sp.dma_start(ls2[64:96, :], t["s5_log_step"][layer].rearrange("d (g e) -> (d g) e", e=2))\
                    .then_inc(rows_in, 16)
                for n in range(N_SLABS):
                    g, kh = divmod(n, 2)
                    if n >= NS:
                        sp.wait_ge(proj_mm if kh else slab_used, g)
                    sp.dma_start(slab[:, n % NS], t["w_in"][layer][
                        kh * HALF_K * P:(kh + 1) * HALF_K * P, g * GW:(g + 1) * GW].rearrange("(k p) n -> p k n", p=P))\
                        .then_inc(slab_in[n % NS], 16)

            @block.scalar
            def _(act):
                do = Steps(act, act_own)
                for b in range(TB):
                    do(nc.scalar.activation(s5["cos"][:, 0:8, :].rearrange("p a n -> p (a n)"), x[:, b, :], ACT.Square,
                                            accum_out=ssq[:, b:b + 1]))
                    do(nc.scalar.activation(ssq[:, 2 + b:3 + b], ssq[:, b:b + 1], ACT.Sqrt, scale=1.0 / D, bias=c("eps")),
                       rms_ready)
                act.wait_ge(s5_arg, 1)
                v = s5["v"]
                do(nc.scalar.activation(v[:, 3], v[:, 2], ACT.Exp), s5_act)
                act.wait_ge(s5_arg, 2)
                do(nc.scalar.activation(v[:, 6], v[:, 4], ACT.Exp), s5_act)
                do(nc.scalar.activation(v[:, 8], v[:, 7], ACT.Sin), s5_act)
                do(nc.scalar.activation(v[:, 10], v[:, 9], ACT.Sin), s5_act)
                for g in range(PROJ // GW):
                    act.wait_ge(proj_mm, g + 1)
                    dst = mixT[:, 4 * g:4 * g + 4] if g < 4 else rwT[:, 4 * g - 16:4 * g - 12]
                    b = 2 * (g % 4)
                    do(nc.scalar.copy(dst, bank[:, b:b + 2, :].rearrange("p b (m s) -> p (b m) s", m=2)), proj_out)

            @block.tensor
            def _(pe):
                pe.wait_ge(rows_in, 17 * 16)
                nc.tensor.transpose(bank[:, 7, 0:NROWS], rows[0:NROWS, :], c("ident")[0:NROWS, 0:NROWS])
                pe.wait_ge(ls_ready, 1)
                nc.tensor.transpose(bank[:, 7, 256:352], srow[:, :], c("ident")[0:96, 0:96]).then_inc(rows_T, 1)
                for b in range(TB):
                    pe.wait_ge(h_ready, b + 1)
                    for k in range(KT):
                        if b == 1 and k == 12:
                            pe.wait_ge(cols_ready, 2)
                        mm = nc.tensor.transpose(bank[:, 4 * b + k // 4, k % 4 * P:k % 4 * P + P], h[:, k * P:k * P + P],
                                                 c("ident"))
                        if k % 4 == 3:
                            mm.then_inc(hT_mm, 1)
                for n in range(N_SLABS):
                    g, kh = divmod(n, 2)
                    pe.wait_ge(slab_in[n % NS], 16 * (n // NS + 1))
                    if kh == 0:
                        pe.wait_ge(hT_ready, 8)
                        if g >= 4:
                            pe.wait_ge(proj_out, g - 3)
                    for m in range(4):
                        for k in range(HALF_K):
                            mm = nc.tensor.matmul(bank[:, 2 * (g % 4) + m // 2, m % 2 * SEQ:m % 2 * SEQ + SEQ],
                                                  slab[:, n % NS, k, m * P:m * P + P], hT[:, kh * HALF_K + k, :],
                                                  start=(kh == 0 and k == 0 and m % 2 == 0),
                                                  stop=(kh == 1 and k == HALF_K - 1), skip_group_check=True)
                    mm.then_inc(proj_mm if kh else slab_used, 1)

            @block.vector
            def _(dve):
                do = Steps(dve, dve_own)
                V = nc.vector
                dve.wait_ge(rows_in, 17 * 16)
                do(V.tensor_copy(srow[64:96, :].rearrange("q (e p) -> q e p", e=2),
                                 ls2[64:96, :].unsqueeze(2).to_broadcast([32, 2, S5P])), ls_ready)
                dve.wait_ge(rows_T, 1)
                do(V.tensor_copy(pcol[:], bank[:, 7, 0:NROWS]), cols_ready)
                v = s5["v"]
                do(V.tensor_copy(v[:, 0:3], bank[:, 7, 256:352].rearrange("p (a b) -> p a b", a=3)), cols_ready)
                mu = col("mu", 0, 32).rearrange("p (i s g) -> p i s g", i=4, s=2)
                m4 = mus[:].rearrange("p (i g) -> p i g", i=4)
                do(V.tensor_tensor(m4, mu[:, :, 0, :], mu[:, :, 1, :], ALU.add))
                do(V.tensor_scalar(mus[:], mus[:], -1.0, 1.0, ALU.mult, ALU.add))
                for b in range(TB):
                    dve.wait_ge(rms_ready, b + 1)
                    do(V.reciprocal(ssq[:, 4 + b:5 + b], ssq[:, 2 + b:3 + b]))
                    do(V.tensor_scalar(h[:], x[:, b, :], ssq[:, 4 + b:5 + b], None, ALU.mult), h_ready)
                    for q in range(4):
                        dve.wait_ge(hT_mm, 4 * b + q + 1)
                        do(V.tensor_tensor(hT[:, 4 * q:4 * q + 4, b * P:b * P + P],
                                           bank[:, 4 * b + q, :].rearrange("p (k s) -> p k s", k=4),
                                           col("norm_mix", 4 * q, 4).unsqueeze(2).to_broadcast([P, 4, P]), ALU.mult), hT_ready)
                    if b == 0:
                        do(V.tensor_copy(v[:, 23], v[:, 2]), s5_arg)
                dve.wait_ge(s5_act, 1)
                re, im, step = v[:, 0], v[:, 1], v[:, 3]
                do(V.tensor_tensor(v[:, 4], re, step, ALU.mult))
                do(V.tensor_tensor(v[:, 5], im, step, ALU.mult))
                big = 1.5 * 2.0 ** 23
                do(V.tensor_scalar(v[:, 11], v[:, 5], 1.0 / (2 * math.pi), big, ALU.mult, ALU.add))
                do(V.tensor_scalar(v[:, 11], v[:, 11], big, None, ALU.subtract))
                do(V.scalar_tensor_tensor(v[:, 12], v[:, 11], -6.28125, v[:, 5], ALU.mult, ALU.add))
                do(V.scalar_tensor_tensor(v[:, 12], v[:, 11], -(2 * math.pi - 6.28125), v[:, 12], ALU.mult, ALU.add))
                do(V.tensor_scalar(v[:, 7], v[:, 12], 3.1415925, -3.1415925, ALU.min, ALU.max))
                do(V.scalar_tensor_tensor(v[:, 12], v[:, 7], -1.0, v[:, 7], ALU.mult, ALU.max))
                do(V.tensor_scalar(v[:, 9], v[:, 12], -1.0, math.pi / 2, ALU.mult, ALU.add), s5_arg)
                dve.wait_ge(s5_act, 4)
                rho, sn, cs = v[:, 6], v[:, 8], v[:, 10]
                do(V.tensor_tensor(v[:, 11], rho, cs, ALU.mult))
                do(V.tensor_scalar(v[:, 11], v[:, 11], -1.0, None, ALU.add))
                do(V.tensor_tensor(v[:, 12], rho, sn, ALU.mult))
                do(V.tensor_tensor(v[:, 13], re, re, ALU.mult))
                do(V.tensor_tensor(v[:, 14], im, im, ALU.mult))
                do(V.tensor_tensor(v[:, 13], v[:, 13], v[:, 14], ALU.add))
                do(V.reciprocal(v[:, 13], v[:, 13]))
                do(V.tensor_tensor(v[:, 14], v[:, 11], re, ALU.mult))
                do(V.tensor_tensor(v[:, 15], v[:, 12], im, ALU.mult))
                do(V.tensor_tensor(v[:, 14], v[:, 14], v[:, 15], ALU.add))
                do(V.tensor_tensor(v[:, 16], v[:, 14], v[:, 13], ALU.mult))
                do(V.tensor_tensor(v[:, 14], v[:, 12], re, ALU.mult))
                do(V.tensor_tensor(v[:, 15], v[:, 11], im, ALU.mult))
                do(V.tensor_tensor(v[:, 14], v[:, 14], v[:, 15], ALU.subtract))
                do(V.tensor_tensor(v[:, 17], v[:, 14], v[:, 13], ALU.mult))
                Ec, Es = s5["cos"], s5["sin"]
                do(V.memset(Ec[:, :, 0:1], 1.0))
                do(V.memset(Es[:, :, 0:1], 0.0))
                wr, wi, wr2, wi2 = v[:, 18], v[:, 19], v[:, 20], v[:, 21]
                do(V.tensor_copy(wr, cs))
                do(V.tensor_copy(wi, sn))
                n = 1
                while n < SEQ:
                    gq = min(32, 1024 // n)
                    for g in range(0, 32, gq):
                        a = tmp[:, 0, 0:gq * n].rearrange("p (g n) -> p g n", g=gq)
                        b_ = tmp[:, 1, 0:gq * n].rearrange("p (g n) -> p g n", g=gq)
                        br = wr[:, g:g + gq].unsqueeze(2).to_broadcast([P, gq, n])
                        bi = wi[:, g:g + gq].unsqueeze(2).to_broadcast([P, gq, n])
                        lo_c, lo_s = Ec[:, g:g + gq, 0:n], Es[:, g:g + gq, 0:n]
                        do(V.tensor_tensor(a, lo_c, br, ALU.mult), wait=False)
                        do(V.tensor_tensor(b_, lo_s, bi, ALU.mult))
                        do(V.tensor_tensor(Ec[:, g:g + gq, n:2 * n], a, b_, ALU.subtract))
                        do(V.tensor_tensor(a, lo_s, br, ALU.mult), wait=False)
                        do(V.tensor_tensor(b_, lo_c, bi, ALU.mult))
                        do(V.tensor_tensor(Es[:, g:g + gq, n:2 * n], a, b_, ALU.add))
                    do(V.tensor_tensor(v[:, 22], wi, wi, ALU.mult), wait=False)
                    do(V.tensor_tensor(wr2, wr, wr, ALU.mult))
                    do(V.scalar_tensor_tensor(wi2, wr, 2.0, wi, ALU.mult, ALU.mult))
                    do(V.tensor_tensor(wr, wr2, v[:, 22], ALU.subtract), wait=False)
                    do(V.tensor_copy(wi, wi2))
                    n *= 2


def attend(nc, t, layer, sem, sb, ps, c, col, mixT, ycT):
    w_in, unit_mm, unit_out = sem("at_w_in"), sem("at_mm"), sem("at_out")
    sq_ready, rstd_ready, qn_ready, rope_ready = sem("at_sq"), sem("at_rstd"), sem("at_qn"), sem("at_rope")
    root_ready, max_ready, exp_ready, prob_ready = sem("at_root"), sem("at_max"), sem("at_exp"), sem("at_prob")
    dve_own, act_own = sem("at_dve"), sem("at_act")
    with ExitStack() as st:
        wf = sb(st, "at_wf", [P, GT, GW])
        arena = sb(st, "at_arena", [P, 4096])
        Z = arena[:, 0:2048].rearrange("p (h b n) -> p h b n", h=4, b=TB)
        S = arena[:, 0:2048].rearrange("p (h b n) -> p h b n", h=4, b=TB)
        fT = arena[:, 2048:3072].rearrange("p (h n) -> p h n", h=4)
        PT_ = arena[:, 2048:4096].rearrange("p (h k n) -> p h k n", h=4, k=TB)
        qk = sb(st, "at_qk", [P, 6, SEQ])
        qa = sb(st, "at_qa", [P, 6, SEQ])
        qb = sb(st, "at_qb", [P, 6, SEQ])
        vt = sb(st, "at_v", [P, TB, 2, P])
        Pr = sb(st, "at_p", [P, 4, TB, SEQ])
        st8 = sb(st, "at_stat", [P, 4, 8])
        bank = ps(st, "at_bank", [P, 4, 512])
        f6 = lambda a: a.rearrange("p h n -> p (h n)")

        with nc.Block() as block:
            @block.sync
            def _(sp):
                sp.dma_start(wf[:], t["fourier_w"][layer].rearrange("(k p) n -> p k n", p=P)).then_inc(w_in, 16)

            @block.tensor
            def _(pe):
                unit = [0]

                def begin():
                    if unit[0] >= 4:
                        pe.wait_ge(unit_out, unit[0] - 3)
                    return bank[:, unit[0] % 4, :]

                def end(mm):
                    mm.then_inc(unit_mm, 1)
                    unit[0] += 1

                mmul = nc.tensor.matmul
                for h in range(4):
                    o = begin()
                    for b in range(TB):
                        mm = mmul(o[:, b * 256:b * 256 + 256], mixT[:, T_A + h, b * P:b * P + P], c("dft_ch"),
                                  start=(b == 0), stop=True, skip_group_check=True)
                    end(mm)
                pe.wait_ge(unit_out, 4)
                for hp in range(2):
                    o = begin()
                    for e in range(2):
                        for b in range(TB):
                            for part in range(2):
                                at = (b * 2 + part) * SEQ
                                mm = mmul(o[:, e * 256:e * 256 + 256], Z[:, 2 * hp + e, b, part * P:part * P + P],
                                          c("dft_seq", at, at + SEQ), start=(e == 0 and b == 0 and part == 0),
                                          stop=(b == 1 and part == 1), skip_group_check=True)
                    end(mm)
                pe.wait_ge(w_in, 16)
                pe.wait_ge(unit_out, 6)
                for mp in range(2):
                    o = begin()
                    for e in range(2):
                        for k in range(GT):
                            m = 2 * mp + e
                            mm = mmul(o[:, e * 256:e * 256 + 256], wf[:, k, m * P:m * P + P], fT[:, k, :],
                                      start=(e == 0 and k == 0), stop=(k == GT - 1), skip_group_check=True)
                    end(mm)
                pe.wait_ge(sq_ready, 1)
                for g in range(3):
                    o = begin()
                    end(mmul(o, c("ones"), f6(qb)[:, g * 512:g * 512 + 512], start=True, stop=True))
                pe.wait_ge(qn_ready, 1)
                for g in range(3):
                    o = begin()
                    end(mmul(o, c("rot"), f6(qk)[:, g * 512:g * 512 + 512], start=True, stop=True))
                o = begin()
                for g in range(2):
                    for b in range(TB):
                        at = (b * 2 + g) * P
                        mm = nc.tensor.transpose(o[:, at:at + P], mixT[:, T_V + g, b * P:b * P + P], c("ident"))
                end(mm)
                pe.wait_ge(rope_ready, 1)
                for h in range(4):
                    o = begin()
                    for b in range(TB):
                        mm = mmul(o[:, b * 256:b * 256 + 256], qa[:, h, b * P:b * P + P], qa[:, 4 + h // 2, :],
                                  start=(b == 0), stop=True, skip_group_check=True)
                    end(mm)
                pe.wait_ge(prob_ready, 1)
                for h in range(4):
                    o = begin()
                    for k in range(TB):
                        for b in range(TB):
                            at = k * 256 + b * P
                            mm = nc.tensor.transpose(o[:, at:at + P], Pr[:, h, b, k * P:k * P + P], c("ident"))
                    end(mm)
                pe.wait_ge(unit_out, unit[0])
                for hp in range(2):
                    o = begin()
                    for e in range(2):
                        h = 2 * hp + e
                        for k in range(TB):
                            mm = mmul(o[:, e * 256:e * 256 + 256], vt[:, k, h // 2, :], PT_[:, h, k, :],
                                      start=(e == 0 and k == 0), stop=(k == 1), skip_group_check=True)
                    end(mm)

            @block.scalar
            def _(act):
                do = Steps(act, act_own)
                unit = [0]

                def take(dst, func=ACT.Copy, **kw):
                    act.wait_ge(unit_mm, unit[0] + 1)
                    src = bank[:, unit[0] % 4, :]
                    unit[0] += 1
                    do(nc.scalar.activation(dst, src, func, **kw), unit_out)

                for h in range(4):
                    take(Z[:, h].rearrange("p b n -> p (b n)"))
                for hp in range(2):
                    take(f6(fT[:, 2 * hp:2 * hp + 2]))
                for mp in range(2):
                    take(f6(ycT[:, 2 * mp:2 * mp + 2]))
                for g in range(3):
                    take(f6(qa)[:, g * 512:g * 512 + 512], ACT.Sqrt, scale=1.0 / HEAD, bias=c("eps"))
                act.wait_ge(qn_ready, 1)
                for g in range(3):
                    take(f6(qb)[:, g * 512:g * 512 + 512])
                take(vt[:].rearrange("p b g n -> p (b g n)"))
                for h in range(4):
                    take(S[:, h].rearrange("p b n -> p (b n)"))
                act.wait_ge(max_ready, 1)
                for h in range(4):
                    for b in range(TB):
                        i = 2 * h + b
                        do(nc.scalar.activation(Pr[:, h, b, :], S[:, h, b, :], ACT.Exp, scale=SCALE,
                                                bias=st8[:, 1, i:i + 1], accum_out=st8[:, 2, i:i + 1]), exp_ready)
                for h in range(4):
                    take(PT_[:, h].rearrange("p k n -> p (k n)"))
                for hp in range(2):
                    take(f6(ycT[:, 8 + 2 * hp:10 + 2 * hp]))

            @block.vector
            def _(dve):
                do = Steps(dve, dve_own)
                V = nc.vector
                do(V.tensor_tensor(qb[:], mixT[:, T_Q:T_Q + 6, :], mixT[:, T_Q:T_Q + 6, :], ALU.mult), sq_ready)
                dve.wait_ge(unit_out, 11)
                do(V.reciprocal(qa[:], qa[:]))
                for i in range(6):
                    do(V.scalar_tensor_tensor(qk[:, i, :], mixT[:, T_Q + i, :], col("q_norm" if i < 4 else "k_norm"),
                                              qa[:, i, :], ALU.mult, ALU.mult))
                do(V.tensor_tensor(qa[:], qk[:], c("cos").unsqueeze(1).to_broadcast([P, 6, SEQ]), ALU.mult), qn_ready)
                dve.wait_ge(unit_out, 14)
                do(V.tensor_tensor(qb[:], qb[:], c("sin").unsqueeze(1).to_broadcast([P, 6, SEQ]), ALU.mult))
                do(V.tensor_tensor(qa[:], qa[:], qb[:], ALU.add), rope_ready)
                dve.wait_ge(unit_out, 19)
                do(V.tensor_reduce(st8[:, 0], S.rearrange("p h b n -> p (h b) n"), AX.X, ALU.max))
                do(V.tensor_scalar(st8[:, 1], st8[:, 0], -SCALE, None, ALU.mult), max_ready)
                dve.wait_ge(exp_ready, 8)
                do(V.reciprocal(st8[:, 3], st8[:, 2]))
                p8 = Pr[:].rearrange("p h b n -> p (h b) n")
                do(V.tensor_tensor(p8, p8, st8[:, 3].unsqueeze(2).to_broadcast([P, 8, SEQ]), ALU.mult), prob_ready)


def s5_branch(nc, t, layer, sem, sb, ps, c, col, mixT, ycT, s5):
    raw_in, exp_ready, unit_mm, unit_out = sem("s5_raw_in"), sem("s5_exp"), sem("s5_mm"), sem("s5_out")
    c_ready, bu_mm, bu_used, x_ready, y_mm = sem("s5_c"), sem("s5_bu_mm"), sem("s5_bu_used"), sem("s5_x"), sem("s5_y_mm")
    pre_ready, gelu_ready, dve_own, act_own = sem("s5_pre"), sem("s5_gelu"), sem("s5_dve"), sem("s5_act")
    with ExitStack() as st:
        wglu = sb(st, "s5_wglu", [P, GT, GW])
        raw = sb(st, "s5_raw", [P, 4, 512])
        work = sb(st, "s5_work", [P, 6, 1024])
        BT = sb(st, "s5_BT", [P, 2, 8, P])
        CT = sb(st, "s5_CT", [P, 2, 8, P])
        y = sb(st, "s5_y", [P, GT, SEQ])
        bu = ps(st, "s5_bu", [P, 4, 512])
        bank = ps(st, "s5_bank", [P, 3, 512])
        yb = ps(st, "s5_yb", [P, 512])
        bexp = [work[:, i].rearrange("p (q n) -> p q n", q=32) for i in range(2)]
        cexp = [work[:, 2 + i].rearrange("p (q n) -> p q n", q=8) for i in range(2)]
        order = [(ct, d) for ct in range(GT) for d in range(2)]

        with nc.Block() as block:
            @block.sync
            def _(sp):
                for i, name in enumerate(("s5_b_re", "s5_b_im")):
                    sp.dma_start(raw[:, i].rearrange("p (q h) -> p q h", q=32),
                                 t[name][layer].rearrange("d (g e) p h -> (e p) (d g) h", e=2)).then_inc(raw_in, 16)
                for i, name in enumerate(("s5_c_re", "s5_c_im")):
                    sp.dma_start(raw[:, 2 + i].rearrange("p (q n) -> p q n", q=8),
                                 t[name][layer].rearrange("d (q g) h p -> (g h) (d q) p", q=GT)).then_inc(raw_in, 16)
                sp.dma_start(wglu[:], t["s5_w_glu"][layer].rearrange("(k p) n -> p k n", p=P)).then_inc(raw_in, 16)

            @block.tensor
            def _(pe):
                unit = [0]
                pe.wait_ge(raw_in, 80)
                pe.wait_ge(exp_ready, 8)
                for which in range(2):
                    for part in range(2):
                        for d in range(2):
                            if unit[0] >= 3:
                                pe.wait_ge(unit_out, unit[0] - 2)
                            for q in range(4):
                                j = d * 4 + q
                                src = bexp[part][:, 4 * j:4 * j + 4, :].rearrange("p a b -> p (a b)") if which == 0 \
                                    else cexp[part][:, j, :]
                                mm = nc.tensor.transpose(bank[:, unit[0] % 3, q * P:q * P + P], src, c("ident"))
                            mm.then_inc(unit_mm, 1)
                            unit[0] += 1
                pe.wait_ge(unit_out, 8)
                for i in range(len(order) + 1):
                    if i < len(order):
                        ct, d = order[i]
                        if i:
                            pe.wait_ge(bu_used, i)
                        for j in range(4):
                            for part in range(2):
                                mm = nc.tensor.matmul(bu[:, j, part * SEQ:part * SEQ + SEQ],
                                                      BT[32 * j:32 * j + 32, part, d * 4 + ct, :],
                                                      mixT[32 * j:32 * j + 32, T_B + ct, :],
                                                      start=(part == 0), stop=True, skip_group_check=True)
                        mm.then_inc(bu_mm, 1)
                    if i:
                        ct, d = order[i - 1]
                        pe.wait_ge(x_ready, i)
                        pe.wait_ge(c_ready, 1)
                        if ct and d == 0:
                            pe.wait_ge(pre_ready, ct)
                        for j in range(4):
                            for part in range(2):
                                mm = nc.tensor.matmul(yb[32 * j:32 * j + 32, 0:SEQ],
                                                      CT[:, part, d * 4 + ct, 32 * j:32 * j + 32],
                                                      work[:, part, j * SEQ:j * SEQ + SEQ],
                                                      start=(d == 0 and part == 0), stop=(d == 1 and part == 1),
                                                      skip_group_check=True)
                        mm.then_inc(y_mm, 1)
                pe.wait_ge(gelu_ready, GT)
                for mp in range(2):
                    for e in range(2):
                        m = 2 * mp + e
                        for k in range(GT):
                            mm = nc.tensor.matmul(bank[:, mp, e * 256:e * 256 + 256], wglu[:, k, m * P:m * P + P],
                                                  y[:, k, :], start=(e == 0 and k == 0), stop=(k == GT - 1),
                                                  skip_group_check=True)
                    mm.then_inc(unit_mm, 1)

            @block.scalar
            def _(act):
                do = Steps(act, act_own)
                for u in range(8):
                    act.wait_ge(unit_mm, u + 1)
                    which, part, d = u // 4, u // 2 % 2, u % 2
                    dst = (BT, CT)[which][:, part, 4 * d:4 * d + 4, :].rearrange("p q n -> p (q n)")
                    do(nc.scalar.copy(dst, bank[:, u % 3, :]), unit_out)
                for ct in range(GT):
                    act.wait_ge(pre_ready, ct + 1)
                    do(nc.scalar.activation(y[:, ct, :], y[:, ct, :], ACT.Gelu_apprx_tanh), gelu_ready)
                for mp in range(2):
                    act.wait_ge(unit_mm, 9 + mp)
                    do(nc.scalar.activation(raw[:, mp, :], bank[:, mp, :], ACT.Sigmoid), unit_out)

            @block.vector
            def _(dve):
                do = Steps(dve, dve_own)
                V = nc.vector
                for i in range(2):
                    do(V.memset(work[:, i, :], 0.0))
                dve.wait_ge(raw_in, 80)
                for i in range(2):
                    r = raw[:, i].rearrange("p (q h) -> p q h", q=32)
                    do(V.tensor_copy(bexp[i][0:64, :, 0:16], r[0:64]), exp_ready, wait=False)
                    do(V.tensor_copy(bexp[i][64:128, :, 16:32], r[64:128]), exp_ready, wait=False)
                    r = raw[:, 2 + i].rearrange("p (q n) -> p q n", q=8)
                    do(V.tensor_scalar(cexp[i][:, :, 0:64], r, c("even"), None, ALU.mult), exp_ready, wait=False)
                    do(V.tensor_scalar(cexp[i][:, :, 64:128], r, c("odd"), None, ALU.mult), exp_ready, wait=False)
                dve.wait_ge(unit_out, 8)
                v = s5["v"]
                cr = CT[:, 0].rearrange("p q (j n) -> p (q j) n", j=4)
                ci = CT[:, 1].rearrange("p q (j n) -> p (q j) n", j=4)
                kr = v[:, 16].unsqueeze(2).to_broadcast([P, 32, 32])
                ki = v[:, 17].unsqueeze(2).to_broadcast([P, 32, 32])
                w = [work[:, i].rearrange("p (q n) -> p q n", q=32) for i in range(6)]
                do(V.tensor_tensor(w[0], cr, kr, ALU.mult), wait=False)
                do(V.tensor_tensor(w[1], ci, ki, ALU.mult), wait=False)
                do(V.tensor_tensor(w[2], cr, ki, ALU.mult), wait=False)
                do(V.tensor_tensor(w[3], ci, kr, ALU.mult))
                do(V.tensor_tensor(cr, w[0], w[1], ALU.subtract), wait=False)
                do(V.scalar_tensor_tensor(ci, w[2], -1.0, w[3], ALU.mult, ALU.subtract), c_ready)
                for i, (ct, d) in enumerate(order):
                    q0 = d * 16 + ct * 4
                    e = slice(None, None, -1) if d else slice(None)
                    tc, ts = s5["cos"][:, q0:q0 + 4, e], s5["sin"][:, q0:q0 + 4, e]
                    f = [work[:, k].rearrange("p (j s) -> p j s", j=4) for k in range(6)]
                    re, im = bu[:, :, 0:SEQ], bu[:, :, SEQ:2 * SEQ]
                    if i:
                        dve.wait_ge(y_mm, i)
                    dve.wait_ge(bu_mm, i + 1)
                    do(V.tensor_tensor(f[2], re, tc, ALU.mult), wait=False)
                    do(V.tensor_tensor(f[3], im, ts, ALU.mult), wait=False)
                    do(V.tensor_tensor(f[4], im, tc, ALU.mult), wait=False)
                    do(V.tensor_tensor(f[5], re, ts, ALU.mult), bu_used)
                    do(V.tensor_tensor(f[0], f[2], f[3], ALU.add), wait=False)
                    do(V.tensor_tensor(f[1], f[4], f[5], ALU.subtract))
                    for part in range(2):
                        for j in range(4):
                            do(V.tensor_tensor_scan(f[2 + part][:, j, e], v[:, 6, q0 + j:q0 + j + 1].to_broadcast([P, SEQ]),
                                                    f[part][:, j, e], 0.0, ALU.mult, ALU.add), wait=(part == 1 and j == 3))
                    do(V.tensor_tensor(f[4], f[2], tc, ALU.mult), wait=False)
                    do(V.tensor_tensor(f[5], f[3], ts, ALU.mult))
                    do(V.tensor_tensor(f[0], f[4], f[5], ALU.subtract))
                    do(V.tensor_tensor(f[4], f[2], ts, ALU.mult), wait=False)
                    do(V.tensor_tensor(f[5], f[3], tc, ALU.mult))
                    do(V.tensor_tensor(f[1], f[4], f[5], ALU.add), x_ready)
                    if d == 1:
                        dve.wait_ge(y_mm, i + 1)
                        do(V.scalar_tensor_tensor(y[:, ct, :], mixT[:, T_B + ct, :], col("s5_d", ct), yb[:, 0:SEQ],
                                                  ALU.mult, ALU.add), pre_ready)
                dve.wait_ge(unit_out, 10)
                do(V.tensor_tensor(ycT[:, 4:8, :].rearrange("p k s -> p (k s)"), y[:].rearrange("p k s -> p (k s)"),
                                   raw[:, 0:2, :].rearrange("p k s -> p (k s)"), ALU.mult))


def rwkv(nc, t, layer, sem, sb, ps, c, col, mus, rwT, ycT):
    both = lambda *names: [f"{n}{d}" for n in names for d in range(2)]
    PE_EV = (["up", "kk", "bonus", "trV", "trA", "trB", "trK"]
             + both("pair") + both("nn") + both("vp") + both("sq2") + both("sq4") + both("ap1") + both("sq8")
             + both("ap2") + both("ap4") + both("ap8") + both("no") + both("aq1") + both("aq2") + both("aq4") + both("aq8")
             + both("qy") + both("gh"))
    ACT_EV = (["up", "kkroot", "trV", "trA", "trB", "trK"] + both("vp") + both("sq2") + both("sq4") + both("sq8")
              + both("no") + both("gh"))
    DVE_EV = (["sq", "bonusin", "bonus", "prep"] + both("pair") + both("nn") + both("ap1") + both("ap2") + both("ap4")
              + both("ap8") + both("aq1") + both("aq2") + both("aq4") + both("aq8") + both("qy") + both("gh"))

    def at(events, i, name, first=0):
        return first + i * len(events) + events.index(name) + 1

    w_in, low_mm, low_out, z_ready = sem("rw_w_in"), sem("rw_low_mm"), sem("rw_low_out"), sem("rw_z_ready")
    pe_ev, act_ev, dve_ev = sem("rw_pe"), sem("rw_act"), sem("rw_dve")
    state_mm, state_ready, y_ready = sem("rw_state_mm"), sem("rw_state"), sem("rw_y_ready")
    stat_mm, root_ready, sqd_ready = sem("rw_stat_mm"), sem("rw_root"), sem("rw_sqd")
    dve_own, act_own = sem("rw_dve_own"), sem("rw_act_own")
    Q = 2 * GT
    with ExitStack() as st:
        w1 = sb(st, "rw_w1", [P, GT, P])
        g1 = sb(st, "rw_g1", [P, GT, 96])
        w2 = sb(st, "rw_w2", [P, GW])
        g2 = sb(st, "rw_g2", [96, GW])
        low = sb(st, "rw_low", [P, SEQ])
        lowg = sb(st, "rw_lowg", [96, SEQ])
        zs = sb(st, "rw_zs", [P, GT, SEQ])
        diag = zs[:].rearrange("p a s -> p (a s)").rearrange("p (d n k) -> p d n k", d=2, n=NCH)
        keep = sb(st, "rw_keep", [P, GT])
        sr, sk, sv, kk = [sb(st, f"rw_{n}", [P, SEQ]) for n in ("sr", "sk", "sv", "kkn")]
        kq = sb(st, "rw_kq", [P, SEQ])
        dec, aa, kd, kb, Pc, IP, Pe, D1, BH, KH = [sb(st, f"rw_{n}", [P, 2, SEQ]) for n in
                                                   ("dec", "aa", "kd", "kb", "pc", "ip", "pe", "d1", "bh", "kh")]
        wend, BTc, KTc = dec, aa, Pc
        pend = sb(st, "rw_pend", [P, 2, NCH])
        AR = sb(st, "rw_ar", [P, 2, TB, 2, P])
        R = sb(st, "rw_r", [P, 2, 4, P])
        mats = {n: sb(st, f"rw_{n}", [P, 2, 4, P]) for n in ("NT", "NTo", "Rb", "Aak", "Rk", "N", "N2T", "N2", "N4T")}
        mats["N4"], mats["N8T"] = mats["N"], mats["Aak"]
        Yo = mats["N2"]
        Bt = sb(st, "rw_bt", [P, 2, TB, P])
        Kt = sb(st, "rw_kt", [P, 2, TB, P])
        Vt = sb(st, "rw_vt", [P, TB, P])
        G = sb(st, "rw_G", [P, NCH, Q, RH])
        H = sb(st, "rw_H", [P, NCH, Q, RH])
        QT = sb(st, "rw_QT", [P, Q, SEQ])
        yin = sb(st, "rw_yin", [P, GT, SEQ])
        bonus = sb(st, "rw_bonus", [P, GT, SEQ])
        gt = sb(st, "rw_gt", [P, GT, SEQ])
        S = sb(st, "rw_S", [P, 2, Q, RH])
        bank = ps(st, "rw_bank", [P, 8, 512])
        flat = lambda a: a.rearrange("p a s -> p (a s)")
        big = lambda a, i: a[:].rearrange("p n q k -> p (n q k)")[:, i * 1024:i * 1024 + 1024]
        dlt, sqd = big(G, 0), big(G, 1)
        ACT_BANK = {"vp": 2, "no": 2}
        AP_BANK = {"ap1": 1, "ap2": 2, "ap4": 3, "ap8": 1, "aq1": 3, "aq2": 1, "aq4": 2, "aq8": 3}
        AP_MAT = {"1": "NT", "2": "N2T", "4": "N4T", "8": "N8T"}

        with nc.Block() as block:
            @block.sync
            def _(sp):
                for d in range(2):
                    sp.dma_start(w1[:, :, 32 * d:32 * d + 32], t["rwkv_w1"][layer, d].rearrange("(k p) n -> p k n", p=P))\
                        .then_inc(w_in, 16)
                    sp.dma_start(w1[:, :, 64 + 32 * d:96 + 32 * d],
                                 t["rwkv_a1"][layer, d].rearrange("(k p) n -> p k n", p=P)).then_inc(w_in, 16)
                    sp.dma_start(w2[32 * d:32 * d + 32, :], t["rwkv_w2"][layer, d]).then_inc(w_in, 16)
                    sp.dma_start(w2[64 + 32 * d:96 + 32 * d, :], t["rwkv_a2"][layer, d]).then_inc(w_in, 16)
                sp.dma_start(g1[:], t["rwkv_g1"][layer].rearrange("(k p) n -> p k n", p=P)).then_inc(w_in, 16)
                sp.dma_start(g2[:], t["rwkv_g2"][layer]).then_inc(w_in, 16)

            @block.tensor
            def _(pe):
                mmul, tr = nc.tensor.matmul, nc.tensor.transpose
                pe.wait_ge(w_in, 160)
                pe.wait_ge(z_ready, 1)
                for k in range(GT):
                    mmul(bank[:, 0, 0:SEQ], w1[:, k, :], zs[:, k, :], start=(k == 0), stop=(k == GT - 1))
                for k in range(GT):
                    mm = mmul(bank[0:96, 1, 0:SEQ], g1[:, k, :], zs[:, k, :], start=(k == 0), stop=(k == GT - 1))
                mm.then_inc(low_mm, 1)
                pe.wait_ge(low_out, 3)
                for i in range(GT):
                    dve = lambda name: pe.wait_ge(dve_ev, at(DVE_EV, i, name))
                    act = lambda name: pe.wait_ge(act_ev, at(ACT_EV, i, name))
                    ev = lambda mm: mm.then_inc(pe_ev, 1)
                    if i:
                        pe.wait_ge(dve_ev, at(DVE_EV, i - 1, "gh1"))
                        pe.wait_ge(act_ev, at(ACT_EV, i - 1, "gh1"))
                    for u in range(4):
                        mmul(bank[:, u, 0:SEQ], w2[32 * u:32 * u + 32, i * P:i * P + P], low[32 * u:32 * u + 32, :],
                             start=True, stop=True)
                    ev(mmul(bank[:, 4, 0:SEQ], g2[:, i * P:i * P + P], lowg[:], start=True, stop=True))
                    dve("sq")
                    ev(mmul(bank[:, 5, 0:SEQ], c("heads"), kq[:], start=True, stop=True))
                    dve("bonusin")
                    ev(mmul(bank[:, 6, 0:SEQ], c("heads"), kq[:], start=True, stop=True))
                    for b in range(TB):
                        mm = tr(bank[:, 7, b * P:b * P + P], sv[:, b * P:b * P + P], c("ident"))
                    ev(mm)
                    dve("prep")
                    act("up")
                    for n, src in enumerate((lambda d, b: AR[:, d, b, 0, :], lambda d, b: BTc[:, d, b * P:b * P + P],
                                             lambda d, b: KTc[:, d, b * P:b * P + P])):
                        for d in range(2):
                            for b in range(TB):
                                mm = tr(bank[:, n, (2 * d + b) * P:(2 * d + b + 1) * P], src(d, b), c("ident"))
                        ev(mm)
                    act("trK")
                    dve("bonus")
                    for d in range(2):
                        for left, base in ((BH, 0), (KH, 2)):
                            for b in range(TB):
                                for e in range(2):
                                    r = slice(RH * e, RH * e + RH)
                                    mm = mmul(bank[:, 4 * d + base + e, b * 256:b * 256 + 256], left[r, d, b * P:b * P + P],
                                              AR[r, d, b, :, :].rearrange("p a s -> p (a s)"), start=(b == 0), stop=True,
                                              skip_group_check=True)
                        ev(mm)
                    for d in range(2):
                        dve(f"pair{d}")
                        for b in range(TB):
                            for e in range(2):
                                r = slice(RH * e, RH * e + RH)
                                mm = mmul(bank[:, 4 * d + e, b * P:b * P + P], AR[r, d, b, 0, :], BH[r, d, b * P:b * P + P],
                                          start=(b == 0), stop=True, skip_group_check=True)
                        ev(mm)
                    for d in range(2):
                        for j in range(4):
                            e, b = divmod(j, 2)
                            mm = mmul(bank[:, 4 * d + 2, j * RH:j * RH + RH], mats["Aak"][:, d, j, :],
                                      Vt[:, b, e * RH:e * RH + RH], start=(j == 0), stop=True, skip_group_check=True)
                        ev(mm)

                    def product(d, b, left, right):
                        for j in range(4):
                            mm = mmul(bank[:, 4 * d + b, j * P:j * P + P], left[:, d, j, :], right[:, d, j, :],
                                      start=(j == 0), stop=True, skip_group_check=True)
                        return mm

                    for d in range(2):
                        dve(f"nn{d}")
                        product(d, 0, mats["N"], mats["NT"])
                        ev(product(d, 1, mats["NT"], mats["N"]))
                    for d in range(2):
                        act(f"sq2{d}")
                        product(d, 2, mats["N2"], mats["N2T"])
                        ev(product(d, 3, mats["N2T"], mats["N2"]))
                    for d in range(2):
                        act(f"vp{d}")
                        ev(product(d, AP_BANK["ap1"], mats["NT"], R))
                    for d in range(2):
                        act(f"sq4{d}")
                        ev(product(d, 0, mats["N4"], mats["N4T"]))
                    for name, after in (("ap2", "ap1"), ("ap4", "ap2"), ("ap8", "ap4")):
                        for d in range(2):
                            dve(f"{after}{d}")
                            if name == "ap8":
                                act(f"sq8{d}")
                            ev(product(d, AP_BANK[name], mats[AP_MAT[name[2]]], R))
                    for d in range(2):
                        dve(f"ap8{d}")
                        ev(product(d, 2, mats["NTo"], R))
                    for name, after in (("aq1", None), ("aq2", "aq1"), ("aq4", "aq2"), ("aq8", "aq4")):
                        for d in range(2):
                            if after:
                                dve(f"{after}{d}")
                            else:
                                act(f"no{d}")
                            ev(product(d, AP_BANK[name], mats[AP_MAT[name[2]]], Yo))
                    for d in range(2):
                        dve(f"aq8{d}")
                        for b in range(TB):
                            for e in range(2):
                                j, rows = 2 * e + b, slice(RH * e, RH * e + RH)
                                mmul(bank[rows, 4 * d, b * P:b * P + P], R[:, d, j, RH:P], mats["Rb"][:, d, j, :],
                                     start=(b == 0), stop=True, skip_group_check=True)
                                mmul(bank[rows, 4 * d, 256 + b * P:384 + b * P], R[:, d, j, 0:RH], mats["Rb"][:, d, j, :],
                                     start=False, stop=False, skip_group_check=True)
                                mm = mmul(bank[rows, 4 * d, 256 + b * P:384 + b * P], Vt[:, b, e * RH:e * RH + RH],
                                          mats["Rk"][:, d, j, :], start=False, stop=True, skip_group_check=True)
                        ev(mm)
                    for d in range(2):
                        dve(f"qy{d}")
                        for b in range(TB):
                            for e in range(2):
                                for q in range(CPB):
                                    j, rows, k = 2 * e + b, slice(RH * e, RH * e + RH), slice(CH * q, CH * q + CH)
                                    o = bank[rows, 4 * d + q, b * P:b * P + P]
                                    hd = slice(RH * e, RH * e + RH)
                                    mmul(o[:, 0:RH], R[k, d, j, RH:P], Bt[k, d, b, hd], start=(b == 0), stop=True,
                                         skip_group_check=True)
                                    mmul(o[:, RH:P], Bt[k, d, b, hd], R[k, d, j, 0:RH], start=False, stop=False,
                                         skip_group_check=True)
                                    mm = mmul(o[:, RH:P], Kt[k, d, b, hd], Vt[k, b, hd], start=False, stop=True,
                                              skip_group_check=True)
                        ev(mm)
                pe.wait_ge(dve_ev, at(DVE_EV, GT - 1, "gh1"))
                pe.wait_ge(act_ev, at(ACT_EV, GT - 1, "gh1"))
                for n in range(NCH):
                    pe.wait_ge(state_ready, n + 1)
                    for q in range(Q):
                        i, d = divmod(q, 2)
                        ch = n if d == 0 else NCH - 1 - n
                        at_ = i % 2 * SEQ + ch * CH
                        for e in range(2):
                            r = slice(RH * e, RH * e + RH)
                            mm = mmul(bank[r, 2 * d + i // 2, at_:at_ + CH], S[r, n % 2, q, :], QT[r, q, ch * CH:ch * CH + CH],
                                      start=(n == 0 and i % 2 == 0), stop=True, skip_group_check=True)
                    if n < NCH - 1:
                        for q in range(Q):
                            for e in range(2):
                                r = slice(RH * e, RH * e + RH)
                                mm = mmul(bank[r, 4 + n % 2, q * RH:q * RH + RH], G[r, n, q, :], S[r, n % 2, q, :],
                                          start=(q == 0), stop=True, skip_group_check=True)
                    mm.then_inc(state_mm, 1)
                pe.wait_ge(y_ready, 1)
                for g in range(2):
                    mm = mmul(bank[:, 6 + g, :], c("heads"), flat(yin[:])[:, g * 512:g * 512 + 512], start=True, stop=True)
                mm.then_inc(stat_mm, 1)
                pe.wait_ge(sqd_ready, 1)
                for g in range(2):
                    mm = mmul(bank[:, 4 + g, :], c("heads"), sqd[:, g * 512:g * 512 + 512], start=True, stop=True)
                mm.then_inc(stat_mm, 1)

            @block.scalar
            def _(act):
                do = Steps(act, act_own)
                A = nc.scalar
                act.wait_ge(low_mm, 1)
                do(A.activation(low[0:64, :], bank[0:64, 0, 0:SEQ], ACT.Tanh), low_out)
                do(A.copy(low[64:128, :], bank[64:128, 0, 0:SEQ]), low_out)
                do(A.activation(lowg[:], bank[0:96, 1, 0:SEQ], ACT.Sigmoid), low_out)
                for i in range(GT):
                    pe = lambda name: act.wait_ge(pe_ev, at(PE_EV, i, name))
                    pe("up")
                    if i:
                        act.wait_ge(pe_ev, at(PE_EV, i - 1, "gh1"))
                    for d in range(2):
                        do(A.activation(dec[:, d, :], bank[:, d, 0:SEQ], ACT.Sigmoid, bias=col("w0", 4 * d + i)))
                        do(A.activation(aa[:, d, :], bank[:, 2 + d, 0:SEQ], ACT.Sigmoid, bias=col("a0", 4 * d + i)))
                    do(A.copy(gt[:, i, :], bank[:, 4, 0:SEQ]))
                    do(A.activation(flat(dec[:]), flat(dec[:]), ACT.Exp, scale=-math.exp(-0.5)), act_ev)
                    pe("kk")
                    do(A.activation(kk[:], bank[:, 5, 0:SEQ], ACT.Sqrt, bias=c("eps_kk")), act_ev)
                    pe("trV")
                    do(A.copy(flat(Vt[:]), bank[:, 7, 0:256]), act_ev)
                    pe("trA")
                    src = bank[:, 0, :].rearrange("p (d b e k) -> p d b e k", d=2, b=TB, e=2)
                    for d in range(2):
                        dst = R[:, d, :, RH:P].rearrange("p (e b) k -> p b e k", e=2)
                        if d == 0:
                            do(A.copy(dst, src[:, d]))
                        else:
                            do(A.copy(dst, src[:, d]), act_ev)
                    pe("trB")
                    do(A.copy(Bt[:].rearrange("p d b k -> p (d b k)"), bank[:, 1, :]), act_ev)
                    pe("trK")
                    do(A.copy(Kt[:].rearrange("p d b k -> p (d b k)"), bank[:, 2, :]), act_ev)
                    for d in range(2):
                        pe(f"vp{d}")
                        do(A.copy(R[:, d, :, 0:RH], bank[:, 4 * d + 2, 0:256].rearrange("p (j k) -> p j k", j=4)), act_ev)
                    jk = lambda a, d: a[:, d].rearrange("p j k -> p (j k)")
                    for name, lo, hi, b0 in (("sq2", "N2T", "N2", 0), ("sq4", "N4T", None, 2), ("sq8", "N8T", None, 0)):
                        for d in range(2):
                            pe(f"{name}{d}")
                            if name == "sq4":
                                do(A.copy(jk(mats["N4"], d), bank[:, 4 * d + 3, :]))
                            if hi:
                                do(A.copy(jk(mats[hi], d), bank[:, 4 * d + b0 + 1, :]))
                            do(A.copy(jk(mats[lo], d), bank[:, 4 * d + b0, :]), act_ev)
                    for d in range(2):
                        pe(f"no{d}")
                        do(A.copy(jk(Yo, d), bank[:, 4 * d + 2, :]), act_ev)
                    for d in range(2):
                        act.wait_ge(dve_ev, at(DVE_EV, i, f"gh{d}"))
                        dst = H[:, ::-1, 2 * i + d, :] if d else H[:, :, 2 * i + d, :]
                        src = bank[:, 4 * d:4 * d + 4, 0:256].rearrange("p q (b n) -> p b q n", b=TB)[:, :, :, RH:P]
                        do(A.copy(dst.rearrange("p (b q) k -> p b q k", b=TB), src), act_ev)
                act.wait_ge(stat_mm, 2)
                do(A.activation(sqd, bank[:, 4:6, :].rearrange("p b n -> p (b n)"), ACT.Sqrt, scale=1.0 / RH,
                                bias=c("eps_gn")), root_ready)

            @block.vector
            def _(dve):
                do = Steps(dve, dve_own)
                V = nc.vector

                def shift(dst, kind, i):
                    src = rwT[:, 4 * kind + i, :]
                    do(V.tensor_scalar(dst, src, mus[:, 4 * kind + i:4 * kind + i + 1], None, ALU.mult))
                    do(V.scalar_tensor_tensor(dst[:, 1:], src[:, :-1], col("mu", 8 * kind + i), dst[:, 1:], ALU.mult, ALU.add))
                    do(V.scalar_tensor_tensor(dst[:, :-1], src[:, 1:], col("mu", 8 * kind + 4 + i), dst[:, :-1],
                                              ALU.mult, ALU.add))

                for i in range(GT):
                    shift(zs[:, i, :], 3, i)
                do(V.tensor_scalar(keep[:], col("k_a", 0, 4), -1.0, 1.0, ALU.mult, ALU.add), z_ready)
                do(V.memset(D1[:], 0.0))
                do(V.memset(Pe[:], 1.0))
                for i in range(GT):
                    pe = lambda name: dve.wait_ge(pe_ev, at(PE_EV, i, name))
                    act = lambda name: dve.wait_ge(act_ev, at(ACT_EV, i, name))
                    if i:
                        dve.wait_ge(pe_ev, at(PE_EV, i - 1, "gh1"))
                    shift(sr[:], 0, i)
                    shift(sk[:], 1, i)
                    shift(sv[:], 2, i)
                    do(V.tensor_scalar(sk[:], sk[:], 1.0, None, ALU.mult))
                    do(V.scalar_tensor_tensor(kq[:], sk[:], col("k_k", i), sk[:], ALU.mult, ALU.mult))
                    do(V.tensor_scalar(kq[:], kq[:], col("k_k", i), None, ALU.mult), dve_ev)
                    act("kkroot")
                    do(V.reciprocal(kk[:], kk[:]))
                    do(V.scalar_tensor_tensor(kk[:], sk[:], col("k_k", i), kk[:], ALU.mult, ALU.mult))
                    on2 = lambda a: a.unsqueeze(1).to_broadcast([P, 2, SEQ])
                    do(V.tensor_tensor(kb[:], aa[:], on2(kk[:]), ALU.mult))
                    do(V.tensor_scalar(kd[:], aa[:], col("k_a", i), keep[:, i:i + 1], ALU.mult, ALU.add))
                    do(V.tensor_tensor(kd[:], kd[:], on2(sk[:]), ALU.mult))
                    do(V.tensor_tensor(kq[:], kd[:, 0, :], kd[:, 1, :], ALU.add))
                    do(V.scalar_tensor_tensor(kq[:], sr[:], col("r_k", i), kq[:], ALU.mult, ALU.mult), dve_ev)
                    pe("bonus")
                    do(V.tensor_tensor(bonus[:, i, :], bank[:, 6, 0:SEQ], sv[:], ALU.mult), dve_ev)
                    for d in range(2):
                        s0 = CH - 1 if d else 0
                        do(V.tensor_copy(D1[:, d, s0::CH], dec[:, d, s0::CH]))
                        do(V.memset(dec[:, d, s0::CH], 0.0))
                        o = slice(None, None, -1) if d else slice(None)
                        do(V.tensor_tensor_scan(Pc[:, d, o], dec[:, d, o], D1[:, d, o], 0.0, ALU.mult, ALU.add))
                    do(V.reciprocal(IP[:], Pc[:]))
                    n32 = lambda a: a.rearrange("p (n s) -> p n s", s=CH)
                    do(V.tensor_copy(n32(Pe[:, 0, :])[:, :, 1:], n32(Pc[:, 0, :])[:, :, :-1]))
                    do(V.tensor_copy(n32(Pe[:, 1, :])[:, :, :-1], n32(Pc[:, 1, :])[:, :, 1:]))
                    do(V.tensor_copy(pend[:, 0, :], Pc[:, 0, CH - 1::CH]))
                    do(V.tensor_copy(pend[:, 1, :], Pc[:, 1, 0::CH]))
                    s2 = lambda a: a.rearrange("p (b s) -> p b s", b=TB)
                    for d in range(2):
                        do(V.scalar_tensor_tensor(AR[:, d, :, 0, :], s2(Pe[:, d, :]), -1.0, s2(kk[:]), ALU.mult, ALU.mult))
                        do(V.tensor_tensor(AR[:, d, :, 1, :], s2(Pc[:, d, :]), s2(sr[:]), ALU.mult))
                    do(V.tensor_tensor(KH[:], kd[:], IP[:], ALU.mult))
                    do(V.tensor_tensor(BH[:], kb[:], IP[:], ALU.mult))
                    nn = lambda a: flat(a[:]).rearrange("p (n s) -> p n s", s=CH)
                    do(V.tensor_tensor(nn(wend), nn(IP), flat(pend[:]).unsqueeze(2).to_broadcast([P, 16, CH]), ALU.mult))
                    do(V.tensor_tensor(BTc[:], kb[:], wend[:], ALU.mult))
                    do(V.tensor_tensor(KTc[:], kd[:], wend[:], ALU.mult), dve_ev)
                    m4 = lambda m: c(m).unsqueeze(1).unsqueeze(1).to_broadcast([P, 2, TB, P])
                    eb = lambda a, d: a[:, d].rearrange("p (e b) k -> p e b k", e=2)
                    for d in range(2):
                        pe(f"pair{d}")
                        w = "UL"[d]
                        for n, (dst, base, half, mask) in enumerate((("NT", 0, 0, "m16" + w), ("NTo", 0, 1, "mX" + w),
                                                                     ("Rb", 0, 2, "m32" + w + "i"), ("Aak", 2, 0, "m32" + w),
                                                                     ("Rk", 2, 2, "m32" + w + "i"))):
                            lo = P if half == 2 else 0
                            src = bank[:, 4 * d + base:4 * d + base + 2, :].rearrange("p e (b k) -> p e b k", b=TB)
                            ins = V.tensor_tensor(eb(mats[dst], d), src[:, :, :, lo:lo + P], m4(mask), ALU.mult)
                            do(ins, dve_ev if n == 4 else None)
                    for d in range(2):
                        pe(f"nn{d}")
                        src = bank[:, 4 * d:4 * d + 2, 0:256].rearrange("p e (b k) -> p e b k", b=TB)
                        do(V.tensor_tensor(eb(mats["N"], d), src, m4("m16" + "LU"[d]), ALU.mult), dve_ev)
                    jk = lambda a, d: a[:, d].rearrange("p j k -> p (j k)")
                    for name in ("ap1", "ap2", "ap4", "ap8"):
                        for d in range(2):
                            pe(f"{name}{d}")
                            do(V.tensor_tensor(jk(R, d), bank[:, 4 * d + AP_BANK[name], :], jk(R, d), ALU.add), dve_ev)
                    for name in ("aq1", "aq2", "aq4", "aq8"):
                        for d in range(2):
                            pe(f"{name}{d}")
                            last = name == "aq8"
                            do(V.tensor_tensor(jk(Yo, d), bank[:, 4 * d + AP_BANK[name], :], jk(Yo, d), ALU.add),
                               None if last else dve_ev)
                            if last:
                                do(V.tensor_tensor(jk(R, d), jk(R, d), jk(Yo, d), ALU.add), dve_ev)
                    for d in range(2):
                        pe(f"qy{d}")
                        do(V.tensor_tensor(s2(QT[:, 2 * i + d, :]), s2(bank[:, 4 * d, 0:SEQ]), AR[:, d, :, 1, :], ALU.add))
                        if d == 0:
                            do(V.tensor_copy(yin[:, i, :], bank[:, 4 * d, 256:512]), dve_ev)
                        else:
                            do(V.tensor_tensor(yin[:, i, :], bank[:, 4 * d, 256:512], yin[:, i, :], ALU.add), dve_ev)
                    for d in range(2):
                        do(V.tensor_tensor(diag[:, d], c("ident64").unsqueeze(1).to_broadcast([P, NCH, RH]),
                                           pend[:, d, :].unsqueeze(2).to_broadcast([P, NCH, RH]), ALU.mult))
                    for d in range(2):
                        pe(f"gh{d}")
                        dst = G[:, ::-1, 2 * i + d, :] if d else G[:, :, 2 * i + d, :]
                        src = bank[:, 4 * d:4 * d + 4, 0:256].rearrange("p q (b n) -> p b q n", b=TB)[:, :, :, 0:RH]
                        do(V.tensor_tensor(dst.rearrange("p (b q) k -> p b q k", b=TB), src,
                                           diag[:, d].rearrange("p (b q) k -> p b q k", b=TB), ALU.add), dve_ev)
                do(V.memset(S[:, 0], 0.0), state_ready)
                dve.wait_ge(act_ev, at(ACT_EV, GT - 1, "gh1"))
                for n in range(NCH - 1):
                    dve.wait_ge(state_mm, n + 1)
                    do(V.tensor_tensor(S[:, (n + 1) % 2].rearrange("p q k -> p (q k)"), bank[:, 4 + n % 2, :],
                                       H[:, n].rearrange("p q k -> p (q k)"), ALU.add), state_ready)
                dve.wait_ge(state_mm, NCH)
                y2 = flat(yin[:]).rearrange("p (b n) -> p b n", b=2)
                do(V.tensor_tensor(y2, bank[:, 0:2, :], y2, ALU.add))
                do(V.tensor_tensor(y2, bank[:, 2:4, :], y2, ALU.add), y_ready)
                dve.wait_ge(stat_mm, 1)
                do(V.scalar_tensor_tensor(dlt.rearrange("p (b n) -> p b n", b=2), bank[:, 6:8, :], -1.0 / RH, y2,
                                          ALU.mult, ALU.add))
                do(V.tensor_tensor(sqd, dlt, dlt, ALU.mult), sqd_ready)
                dve.wait_ge(root_ready, 1)
                do(V.reciprocal(sqd, sqd))
                do(V.tensor_tensor(dlt, dlt, sqd, ALU.mult))
                for i in range(GT):
                    y = dlt[:, i * SEQ:i * SEQ + SEQ]
                    do(V.tensor_scalar(y, y, col("ln_w", i), col("ln_b", i), ALU.mult, ALU.add))
                do(V.tensor_tensor(dlt, dlt, flat(bonus[:]), ALU.add))
                do(V.tensor_tensor(flat(ycT[:, 12:16, :]), dlt, flat(gt[:]), ALU.mult))


def route(nc, t, layer, sem, sb, ps, c, col, x, ycT, h2, index, gate, layer_base):
    slab_in, piece_mm = [sem(f"rt_slab_in{i}") for i in range(WRING)], sem("rt_piece_mm")
    small_in, sq_ready, norm_mm, root_ready = sem("rt_small_in"), sem("rt_sq"), sem("rt_norm_mm"), sem("rt_root")
    ycn_ready, x_added, rms_ready, h2_ready, h2_mm = sem("rt_ycn"), sem("rt_x"), sem("rt_rms"), sem("rt_h2"), sem("rt_h2_mm")
    hT_ready, sk_mm, sk_out, q_out, score_mm, score_out = (sem("rt_hT"), sem("rt_sk_mm"), sem("rt_sk_out"), sem("rt_q_out"),
                                                           sem("rt_score_mm"), sem("rt_score_out"))
    top_ready, exp_ready, dve_own, act_own = sem("rt_top"), sem("rt_exp"), sem("rt_dve"), sem("rt_act")
    with ExitStack() as st:
        slab = sb(st, "rt_slab", [P, 2, HALF_K, GW])
        sq = sb(st, "rt_sq_b", [P, KT, SEQ])
        hT = sb(st, "rt_hT_b", [P, KT, SEQ])
        rstd = sb(st, "rt_rstd", [P, 4, SEQ])
        gain = sb(st, "rt_gain", [P, D])
        qT = sb(st, "rt_qT", [P, PEER_H, SEQ])
        sk = sb(st, "rt_sk", [P, PEER_H, 2, KEYS // 2])
        skT = sb(st, "rt_skT", [P, PEER_H, KEYS])
        score = sb(st, "rt_score", [P, TB, 2, PEER_H, KEYS])
        ssq = sb(st, "rt_ssq", [P, 8])
        left = sb(st, "rt_left", [P, 256])
        top_v = sb(st, "rt_top_v", [P, 2, PEER_H, TOPK])
        top_i = sb(st, "rt_top_i", [P, 2, PEER_H, TOPK], U32)
        top_f = sb(st, "rt_top_f", [P, 2, PEER_H, TOPK])
        best = sb(st, "rt_best", [P, PEER_H, TOPK])
        pos = sb(st, "rt_pos", [P, PEER_H, TOPK], U32)
        half_u = sb(st, "rt_half_u", [P, 2, PEER_H, TOPK], U32)
        half_f = sb(st, "rt_half_f", [P, 2, PEER_H, TOPK])
        pick = sb(st, "rt_pick", [P, 2, PEER_H, TOPK])
        tot = sb(st, "rt_tot", [P, PEER_H])
        cand = sq[:, 0:8, :]
        hot = sq[:, 8:16, :].rearrange("p a s -> p (a s)").rearrange("p (h s k) -> p h s k", h=PEER_H, s=TOPK)
        bank = ps(st, "rt_bank", [P, 8, 512])
        NS = 2
        pieces = [("w_out", n, kh) for n in range(4) for kh in range(2)] + \
                 [("peer_w_query", n, kh) for n in range(2) for kh in range(2)]

        with nc.Block() as block:
            @block.sync
            def _(sp):
                for n, (name, g, kh) in enumerate(pieces):
                    if n >= NS:
                        sp.wait_ge(piece_mm, n - NS + 1)
                    sp.dma_start(slab[:, n % NS], t[name][layer][kh * HALF_K * P:(kh + 1) * HALF_K * P, g * GW:(g + 1) * GW]
                                 .rearrange("(k p) n -> p k n", p=P)).then_inc(slab_in[n % NS], 16)
                    if n == 1:
                        sp.dma_start(sk[:], t["peer_sub_keys"][layer].rearrange("h e k d -> k h e d")).then_inc(small_in, 16)
                        sp.dma_start(gain[:], t["norm_ffn"][layer].unsqueeze(0).to_broadcast([P, D])).then_inc(small_in, 16)

            @block.tensor
            def _(pe):
                mmul, tr = nc.tensor.matmul, nc.tensor.transpose
                pe.wait_ge(sq_ready, 1)
                for g in range(4):
                    for k in range(4):
                        mm = mmul(bank[:, g // 2, g % 2 * 256:g % 2 * 256 + 256], c("ones"), sq[:, 4 * g + k, :],
                                  start=(g % 2 == 0 and k == 0), stop=(k == 3), skip_group_check=True)
                mm.then_inc(norm_mm, 1)
                pe.wait_ge(small_in, 32)
                for h in range(PEER_H):
                    mm = tr(bank[:, 6 + h // 4, h % 4 * P:h % 4 * P + P], sk[:, h].rearrange("p e d -> p (e d)"), c("ident"))
                mm.then_inc(sk_mm, 1)
                pe.wait_ge(ycn_ready, KT)
                for n in range(8):
                    g, kh = divmod(n, 2)
                    pe.wait_ge(slab_in[n % NS], 16 * (n // NS + 1))
                    if kh == 0 and g >= 2:
                        pe.wait_ge(x_added, 2 * (g - 1))
                    for b in range(TB):
                        for k in range(HALF_K):
                            mm = mmul(bank[:, 2 + 2 * (g % 2) + b, :], sq[:, kh * HALF_K + k, b * P:b * P + P],
                                      slab[:, n % NS, k, :], start=(kh == 0 and k == 0), stop=(kh == 1 and k == 7),
                                      skip_group_check=True)
                    mm.then_inc(piece_mm, 1)
                pe.wait_ge(sk_out, 2)
                pe.wait_ge(x_added, 8)
                for b in range(TB):
                    pe.wait_ge(h2_ready, b + 1)
                    for k in range(KT):
                        mm = tr(bank[:, 4 * b + k // 4, k % 4 * P:k % 4 * P + P], h2[:, b, k * P:k * P + P], c("ident"))
                        if k % 4 == 3:
                            mm.then_inc(h2_mm, 1)
                pe.wait_ge(hT_ready, 8)
                for n in range(8, 12):
                    g, kh = divmod(n - 8, 2)
                    pe.wait_ge(slab_in[n % NS], 16 * (n // NS + 1))
                    for m in range(4):
                        for k in range(HALF_K):
                            mm = mmul(bank[:, 2 * g + m // 2, m % 2 * SEQ:m % 2 * SEQ + SEQ], slab[:, n % NS, k, m * P:m * P + P],
                                      hT[:, kh * HALF_K + k, :], start=(kh == 0 and k == 0 and m % 2 == 0),
                                      stop=(kh == 1 and k == 7), skip_group_check=True)
                    mm.then_inc(piece_mm, 1)
                pe.wait_ge(q_out, 4)
                for b in range(TB):
                    for e in range(2):
                        for hg in range(2):
                            for h in range(4 * hg, 4 * hg + 4):
                                r = slice(64 * e, 64 * e + 64)
                                mm = mmul(bank[:, 4 * b + 2 * e + hg, h % 4 * P:h % 4 * P + P], qT[r, h, b * P:b * P + P],
                                          skT[r, h, :], start=(h % 4 == 0), stop=True, skip_group_check=True)
                            mm.then_inc(score_mm, 1)

            @block.scalar
            def _(act):
                do = Steps(act, act_own)
                A = nc.scalar
                act.wait_ge(norm_mm, 1)
                do(A.activation(rstd[:].rearrange("p g s -> p (g s)"), bank[:, 0:2, :].rearrange("p b n -> p (b n)"), ACT.Sqrt,
                                scale=1.0 / GW, bias=c("eps")), root_ready)
                act.wait_ge(sk_mm, 1)
                for g in range(2):
                    do(A.copy(skT[:, 4 * g:4 * g + 4].rearrange("p h k -> p (h k)"), bank[:, 6 + g, :]), sk_out)
                act.wait_ge(x_added, 8)
                for b in range(TB):
                    do(A.activation(sq[:, 0:8].rearrange("p k s -> p (k s)"), x[:, b, :], ACT.Square,
                                    accum_out=ssq[:, b:b + 1]))
                    do(A.activation(ssq[:, 2 + b:3 + b], ssq[:, b:b + 1], ACT.Sqrt, scale=1.0 / D, bias=c("eps")), rms_ready)
                for u in range(4):
                    act.wait_ge(piece_mm, 8 + 2 * (u // 2) + 2)
                    do(A.copy(qT[:, 2 * u:2 * u + 2].rearrange("p m s -> p (m s)"), bank[:, u, :]), q_out)
                for b in range(TB):
                    for e in range(2):
                        for hg in range(2):
                            u = 4 * b + 2 * e + hg
                            act.wait_ge(score_mm, u + 1)
                            do(A.copy(score[:, b, e, 4 * hg:4 * hg + 4].rearrange("p h k -> p (h k)"), bank[:, u, :]), score_out)
                for b in range(TB):
                    act.wait_ge(top_ready, b + 1)
                    g = gate[:, b].rearrange("p h s -> p (h s)")
                    do(A.activation(g, g, ACT.Exp), exp_ready)

            @block.vector
            def _(dve):
                do = Steps(dve, dve_own)
                V = nc.vector
                do(V.tensor_tensor(sq[:], ycT[:], ycT[:], ALU.mult), sq_ready)
                dve.wait_ge(root_ready, 1)
                do(V.reciprocal(rstd[:], rstd[:]))
                for k in range(KT):
                    do(V.scalar_tensor_tensor(sq[:, k, :], ycT[:, k, :], col("branch", k), rstd[:, k // 4, :],
                                              ALU.mult, ALU.mult), ycn_ready)
                for g in range(4):
                    dve.wait_ge(piece_mm, 2 * g + 2)
                    for b in range(TB):
                        xs = x[:, b, g * GW:(g + 1) * GW]
                        do(V.tensor_tensor(xs, bank[:, 2 + 2 * (g % 2) + b, :], xs, ALU.add), x_added)
                for b in range(TB):
                    dve.wait_ge(rms_ready, b + 1)
                    do(V.reciprocal(ssq[:, 4 + b:5 + b], ssq[:, 2 + b:3 + b]))
                    do(V.tensor_scalar(h2[:, b, :], x[:, b, :], ssq[:, 4 + b:5 + b], None, ALU.mult), h2_ready)
                for b in range(TB):
                    for q in range(4):
                        dve.wait_ge(h2_mm, 4 * b + q + 1)
                        do(V.tensor_tensor(hT[:, 4 * q:4 * q + 4, b * P:b * P + P],
                                           bank[:, 4 * b + q, :].rearrange("p (k s) -> p k s", k=4),
                                           col("norm_ffn", 4 * q, 4).unsqueeze(2).to_broadcast([P, 4, P]), ALU.mult), hT_ready)
                dve.wait_ge(small_in, 32)
                for b in range(TB):
                    do(V.tensor_tensor(h2[:, b, :], h2[:, b, :], gain[:], ALU.mult))
                dve.wait_ge(score_out, 8)

                def top16(values, out_v, out_i):
                    rest = left[:, 0:values.shape[-1]]
                    do(V.max(out_v[:, 0:8], values))
                    do(V.max_index(out_i[:, 0:8], out_v[:, 0:8], values))
                    do(V.match_replace(rest, out_v[:, 0:8], values, -3.0e38))
                    do(V.max(out_v[:, 8:16], rest))
                    do(V.max_index(out_i[:, 8:16], out_v[:, 8:16], rest))

                all4 = [P, PEER_H, TOPK, TOPK]
                flat = lambda a: a.rearrange("p h s -> p (h s)")
                for b in range(TB):
                    for e in range(2):
                        for h in range(PEER_H):
                            top16(score[:, b, e, h, :], top_v[:, e, h, :], top_i[:, e, h, :])
                    do(V.tensor_copy(top_f[:], top_i[:]))
                    do(V.tensor_tensor(cand.rearrange("p h (i j) -> p h i j", i=TOPK),
                                       top_v[:, 0].unsqueeze(3).to_broadcast(all4), top_v[:, 1].unsqueeze(2).to_broadcast(all4),
                                       ALU.add))
                    for h in range(PEER_H):
                        top16(cand[:, h, :], best[:, h, :], pos[:, h, :])
                    do(V.tensor_scalar(half_u[:, 0], pos[:], 4, None, ALU.logical_shift_right))
                    do(V.tensor_scalar(half_u[:, 1], pos[:], 15, None, ALU.bitwise_and))
                    do(V.tensor_copy(half_f[:], half_u[:]))
                    for e in range(2):
                        do(V.tensor_tensor(hot, half_f[:, e].unsqueeze(3).to_broadcast(all4),
                                           c("iota16").unsqueeze(1).unsqueeze(1).to_broadcast(all4), ALU.is_equal))
                        do(V.tensor_tensor(hot, hot, top_f[:, e].unsqueeze(2).to_broadcast(all4), ALU.mult))
                        do(V.tensor_reduce(pick[:, e], hot, AX.X, ALU.add))
                    do(V.scalar_tensor_tensor(flat(pick[:, 0]), flat(pick[:, 0]), float(KEYS), flat(pick[:, 1]),
                                              ALU.mult, ALU.add))
                    do(V.tensor_scalar(flat(index[:, b]), flat(pick[:, 0]), layer_base[:], None, ALU.add))
                    do(V.tensor_tensor(gate[:, b], best[:], best[:, :, 0:1].to_broadcast([P, PEER_H, TOPK]), ALU.subtract),
                       top_ready)
                    dve.wait_ge(exp_ready, b + 1)
                    do(V.tensor_reduce(tot[:], gate[:, b], AX.X, ALU.add))
                    do(V.reciprocal(tot[:], tot[:]))
                    do(V.tensor_tensor(gate[:, b], gate[:, b], tot[:].unsqueeze(2).to_broadcast([P, PEER_H, TOPK]), ALU.mult))
                do(V.tensor_scalar(layer_base[:], layer_base[:], float(EXPERTS), None, ALU.add))


def experts(nc, t, layer, sem, sb, row_in, x, h2, index, gate):
    staged, place_free, dots, gelus, weights, place_taken = (sem("ex_staged"), sem("ex_place_free"), sem("ex_dots"),
                                                         sem("ex_gelus"), sem("ex_weights"), sem("ex_place_taken"))
    with ExitStack() as st:
        ring = sb(st, "ex_ring", [P, RING, D])
        rows = sb(st, "ex_rows", [P, 2, TOPK], U32)
        dot = sb(st, "ex_dot", [P, 2, TOPK])
        act_ = sb(st, "ex_act", [P, 2, TOPK])
        weight = sb(st, "ex_weight", [P, 2, TOPK])
        tables = [t[n].rearrange("l e d -> (l e) d") for n in ("peer_u", "peer_v")]
        PER = 2 * TOPK
        laps = PER // RING

        with nc.Block() as block:
            @block.gpsimd
            def _(pool):
                pool.sem_inc(place_free, RING)
                for b in range(TB):
                    with pool.Fori(0, PEER_H // 2) as pair:
                        for e in range(2):
                            head = pair * 2 + (b * PEER_H + e)
                            pool.wait_ge(place_free, head * PER + 1)
                            nc.gpsimd.tensor_copy(rows[:, e, :], index[:, b, bass.ds(pair * 2 + e, 1), :]).then_inc(staged, 1)
                            pool.wait_ge(staged, head + 1)
                            for s in range(PER):
                                pool.wait_ge(place_free, head * PER + s + 1)
                                pool.sem_inc(place_taken, 1)
                                nc.gpsimd.indirect_dma_start(
                                    out=ring[:, s % RING, :], out_offset=None, in_=tables[s // TOPK][:, :],
                                    in_offset=bass.IndirectOffsetOnAxis(ap=rows[:, e, s % TOPK:s % TOPK + 1], axis=0))\
                                    .then_inc(row_in[s % RING], 16)

            @block.scalar
            def _(act):
                for b in range(TB):
                    with act.Fori(0, PEER_H // 2) as pair:
                        for e in range(2):
                            head = pair * 2 + (b * PEER_H + e)
                            act.wait_ge(dots, head + 1)
                            nc.scalar.activation(act_[:, e, :], dot[:, e, :], ACT.Gelu).then_inc(gelus, 1)

            @block.vector
            def _(dve):
                V = nc.vector
                for b in range(TB):
                    with dve.Fori(0, PEER_H // 2) as pair:
                        for e in range(2):
                            head = pair * 2 + (b * PEER_H + e)
                            arrived = (layer * (TB * PEER_H) + head) * (16 * laps)
                            for s in range(TOPK):
                                dve.wait_ge(row_in[s % RING], arrived + 16 * (s // RING + 1))
                                ins = V.tensor_tensor_reduce(out=ring[:, s % RING, :], in0=ring[:, s % RING, :],
                                                             in1=h2[:, b, :], scale=1.0, scalar=0.0, op0=ALU.mult,
                                                             op1=ALU.add, accum_out=dot[:, e, s:s + 1])
                                ins.then_inc(place_free, 1)
                            dve.wait_ge(place_free, head * PER + TOPK + RING)
                            dve.sem_inc(dots, 1)
                            dve.wait_ge(gelus, head + 1)
                            V.tensor_tensor(weight[:, e, :], act_[:, e, :], gate[:, b, bass.ds(pair * 2 + e, 1), :], ALU.mult)\
                                .then_inc(weights, 1)
                            dve.wait_ge(weights, head + 1)
                            for s in range(TOPK, PER):
                                dve.wait_ge(row_in[s % RING], arrived + 16 * (s // RING + 1))
                                dve.wait_ge(place_free, head * PER + s + RING)
                                V.scalar_tensor_tensor(x[:, b, :], ring[:, s % RING, :],
                                                       weight[:, e, s - TOPK:s - TOPK + 1], x[:, b, :], ALU.mult, ALU.add)\
                                    .then_inc(place_free, 1)


_INS = ["x", "norm_mix", "w_in", "fourier_w", "s5_lam_re", "s5_lam_im", "s5_log_step", "s5_b_re", "s5_b_im", "s5_c_re",
        "s5_c_im", "s5_d", "s5_w_glu", "attn_q_norm", "attn_k_norm", "rwkv_mu", "rwkv_w0", "rwkv_w1", "rwkv_w2", "rwkv_a0",
        "rwkv_a1", "rwkv_a2", "rwkv_g1", "rwkv_g2", "rwkv_k_k", "rwkv_k_a", "rwkv_r_k", "rwkv_ln_w", "rwkv_ln_b",
        "branch_norm", "w_out", "norm_ffn", "peer_w_query", "peer_sub_keys", "peer_u", "peer_v"]


def kernel(**inputs):
    import concourse.bacc as bacc
    from concourse.bass_utils import run_bass_kernel_spmd

    nc = bacc.Bacc("TRN2", target_bir_lowering=False, num_devices=1)
    arrays = {f"in_{n}": np.ascontiguousarray(inputs[n]) for n in _INS}
    arrays["in_consts"] = constants()[0]
    t = {n[3:]: nc.dram_tensor(n, a.shape, mybir.dt.from_np(a.dtype), kind="ExternalInput").ap() for n, a in arrays.items()}
    out = nc.dram_tensor("out_x", (1, SEQ, D), F32, kind="ExternalOutput").ap()
    build(nc, t, out)
    r = run_bass_kernel_spmd(nc, [arrays], core_ids=[0])
    return r.results[0]["out_x"]
```

```python
import math
from contextlib import ExitStack

import numpy as np

import concourse.bass as bass
from concourse import mybir

P = 128
F32 = mybir.dt.float32
U32 = mybir.dt.uint32
ALU = mybir.AluOpType
ACT = mybir.ActivationFunctionType
AX = mybir.AxisListType

DEPTH, SEQ, D = 2, 256, 2048
TB = SEQ // P
KT = D // P
GW = 512
GT = GW // P
PROJ = 4096
PT = PROJ // P
NORM_EPS = 1e-6
HEAD = 128
SCALE = HEAD ** -0.5
S5P, S5C, S5G = 64, 16, 32
CH = 32
NCH = SEQ // CH
CPB = P // CH
RH = 64
PEER_H, KEYS, TOPK = 8, 128, 16
EXPERTS = KEYS * KEYS
RING = 8
HALF_K = 8
WRING = 3

T_A, T_B, T_Q, T_K, T_V, T_R, T_RK, T_RV, T_RZ = 0, 4, 8, 12, 14, 16, 20, 24, 28

ROWS = {}
for _name, _n in (("norm_mix", 16), ("norm_ffn", 16), ("mu", 32), ("w0", 8), ("a0", 8), ("k_k", 4), ("k_a", 4),
                  ("r_k", 4), ("ln_w", 4), ("ln_b", 4), ("branch", 16), ("s5_d", 4), ("q_norm", 1), ("k_norm", 1)):
    ROWS[_name] = (sum(n for _, n in ROWS.values()), _n)
NROWS = sum(n for _, n in ROWS.values())
assert NROWS <= P


def constants():
    p = np.arange(P)[:, None]
    q = np.arange(P)[None, :]
    parts = {"ident": p == q, "ones": np.ones((P, P)), "heads": p // RH == q // RH}
    half = HEAD // 2
    parts["rot"] = np.where(p == q + half, -1.0, 0.0) + np.where(p == q - half, 1.0, 0.0)
    t = np.arange(SEQ)
    inv = 10000.0 ** (-np.arange(0, half, 2, dtype=np.float32) / half)
    ang = np.concatenate([(t // 64)[:, None] * inv, (t % 64)[:, None] * inv], axis=-1).astype(np.float32)
    parts["cos"] = np.tile(np.cos(ang).T, (2, 1))
    parts["sin"] = np.tile(np.sin(ang).T, (2, 1))
    ch = 2 * np.pi * p * q / P
    s = 1 / math.sqrt(SEQ * P)
    parts["dft_ch"] = np.concatenate([np.cos(ch), np.sin(ch)], 1) * s
    sq = np.concatenate([2 * np.pi * (p + b * P) * t[None, :] / SEQ for b in range(TB)], 1).reshape(P, TB, SEQ)
    parts["dft_seq"] = np.concatenate([np.cos(sq), -np.sin(sq)], 2).reshape(P, TB * 2 * SEQ)
    s16, s32 = p // 16 == q // 16, p // CH == q // CH
    parts["m16U"], parts["m16L"] = s16 & (q > p), s16 & (q < p)
    parts["mXU"], parts["mXL"] = s32 & ~s16 & (q > p), s32 & ~s16 & (q < p)
    parts["m32U"], parts["m32L"] = s32 & (q > p), s32 & (q < p)
    parts["m32Ui"], parts["m32Li"] = s32 & (q >= p), s32 & (q <= p)
    parts["ident64"] = (p % RH) == np.arange(RH)[None, :]
    parts["iota16"] = np.tile(np.arange(16)[None, :], (P, 1))
    parts["even"] = (p // S5C) % 2 == 0
    parts["odd"] = (p // S5C) % 2 == 1
    parts["eps"] = np.full((P, 1), NORM_EPS)
    parts["eps_kk"] = np.full((P, 1), 1e-12)
    parts["eps_gn"] = np.full((P, 1), 64e-5)
    where, at = {}, 0
    for k, v in parts.items():
        where[k] = (at, at + v.shape[1])
        at += v.shape[1]
    return np.concatenate([np.asarray(v, np.float64) for v in parts.values()], 1).astype(np.float32), where


class Steps:

    def __init__(self, engine, own):
        self.engine, self.own, self.count = engine, own, {}

    def __call__(self, instruction, sem=None, wait=True):
        sem = self.own if sem is None else sem
        instruction.then_inc(sem, 1)
        self.count[sem.name] = self.count.get(sem.name, 0) + 1
        if wait:
            self.engine.wait_ge(sem, self.count[sem.name])


def build(nc, t, out):
    _, where = constants()
    whole = ExitStack()
    with whole:
        first_sem = []

        def sem(name):
            s = whole.enter_context(nc.semaphore(name))
            first_sem.append(s)
            return s

        def sb(stack, name, shape, dt=F32):
            return stack.enter_context(nc.sbuf_tensor(name, shape, dt))

        def ps(stack, name, shape, dt=F32):
            return stack.enter_context(nc.psum_tensor(name, shape, dt))

        x = sb(whole, "x", [P, TB, D])
        consts = sb(whole, "consts", [P, where["eps_gn"][1]])
        pcol = sb(whole, "pcol", [P, NROWS])
        mus = sb(whole, "mus", [P, 16])
        layer_base = sb(whole, "layer_base", [P, 1])

        def c(name, a=None, b=None):
            lo, hi = where[name]
            return consts[:, lo if a is None else lo + a:hi if b is None else lo + b]

        def col(name, i=0, n=1):
            at = ROWS[name][0] + i
            return pcol[:, at:at + n]

        loaded, base_set, stored = sem("loaded"), sem("base_set"), sem("stored")
        with nc.Block() as block:
            @block.sync
            def _(sp):
                sp.dma_start(consts[:], t["consts"]).then_inc(loaded, 16)
                sp.dma_start(x[:], t["x"][0].rearrange("(b p) d -> p b d", p=P)).then_inc(loaded, 16)
                sp.wait_ge(loaded, 32)

            @block.vector
            def _(dve):
                dve.memset(layer_base[:], 0.0).then_inc(base_set, 1)
                dve.wait_ge(base_set, 1)

        row_in = [sem(f"row_in{i}") for i in range(RING)]
        kept = len(first_sem)
        with nc.Fori(0, DEPTH) as layer:
            rw = ExitStack()
            ycT = sb(rw, "ycT", [P, 16, SEQ])
            projected = ExitStack()
            rwT = sb(projected, "rwT", [P, 16, SEQ])
            mix = ExitStack()
            mixT = sb(mix, "mixT", [P, 16, SEQ])
            tab = ExitStack()
            s5 = {"cos": sb(tab, "s5cos", [P, 32, SEQ]), "sin": sb(tab, "s5sin", [P, 32, SEQ]),
                  "v": sb(tab, "s5v", [P, 24, 32])}
            project(nc, t, layer, sem, sb, ps, c, col, x, pcol, mus, mixT, rwT, s5)
            attend(nc, t, layer, sem, sb, ps, c, col, mixT, ycT)
            s5_branch(nc, t, layer, sem, sb, ps, c, col, mixT, ycT, s5)
            tab.close()
            mix.close()
            rwkv(nc, t, layer, sem, sb, ps, c, col, mus, rwT, ycT)
            projected.close()
            route_kept = ExitStack()
            h2 = sb(route_kept, "h2", [P, TB, D])
            score = sb(route_kept, "score", [P, TB * PEER_H + 1, 2, KEYS])
            route(nc, t, layer, sem, sb, ps, c, col, x, ycT, h2, score)
            experts(nc, t, layer, sem, sb, c, row_in, x, h2, score, layer_base)
            route_kept.close()
            rw.close()
            with nc.Block() as block:
                @block.sync
                def _(sp):
                    for s in first_sem[kept:]:
                        sp.sem_clear(s)

        with nc.Block() as block:
            @block.sync
            def _(sp):
                sp.dma_start(out[0].rearrange("(b p) d -> p b d", p=P), x[:]).then_inc(stored, 16)
                sp.wait_ge(stored, 16)


def project(nc, t, layer, sem, sb, ps, c, col, x, pcol, mus, mixT, rwT, s5):
    rows_in, slab_in = sem("pj_rows_in"), [sem(f"pj_slab_in{i}") for i in range(WRING)]
    rows_T, cols_ready = sem("pj_rows_T"), sem("pj_cols_ready")
    h_ready, hT_mm, hT_ready = sem("pj_h_ready"), sem("pj_hT_mm"), sem("pj_hT_ready")
    rms_ready, slab_used, proj_mm, proj_out = sem("pj_rms"), sem("pj_slab_used"), sem("pj_mm"), sem("pj_out")
    ls_ready, s5_act = sem("pj_ls_ready"), sem("pj_s5_act")
    s5_arg = sem("pj_s5_arg")
    dve_own, act_own = sem("pj_dve"), sem("pj_act")
    with ExitStack() as st:
        rows = sb(st, "pj_rows", [P, P])
        srow = sb(st, "pj_srow", [96, P])
        ls2 = sb(st, "pj_ls2", [96, 2])
        h = sb(st, "pj_h", [P, D])
        hT = sb(st, "pj_hT", [P, KT, SEQ])
        slab = sb(st, "pj_slab", [P, 2, HALF_K, GW])
        ssq = sb(st, "pj_ssq", [P, 8])
        tmp = h[:].rearrange("p (a n) -> p a n", a=2)
        bank = ps(st, "pj_bank", [P, 8, 512])
        ROW_SRC = [("norm_mix", t["norm_mix"]), ("norm_ffn", t["norm_ffn"]), ("mu", t["rwkv_mu"]), ("w0", t["rwkv_w0"]),
                   ("a0", t["rwkv_a0"]), ("k_k", t["rwkv_k_k"]), ("k_a", t["rwkv_k_a"]), ("r_k", t["rwkv_r_k"]),
                   ("ln_w", t["rwkv_ln_w"]), ("ln_b", t["rwkv_ln_b"]), ("branch", t["branch_norm"]),
                   ("s5_d", t["s5_d"]), ("q_norm", t["attn_q_norm"]), ("k_norm", t["attn_k_norm"])]
        NS = 2
        N_SLABS = PROJ // GW * 2

        with nc.Block() as block:
            @block.sync
            def _(sp):
                for name, src in ROW_SRC:
                    a, n = ROWS[name]
                    v = src[layer]
                    v = {1: lambda v: v, 2: lambda v: v.rearrange("a b -> (a b)"),
                         3: lambda v: v.rearrange("a b c -> (a b c)")}[len(v.shape)](v)
                    sp.dma_start(rows[a:a + n, :], v.rearrange("(n p) -> n p", p=P)).then_inc(rows_in, 16)
                for i, name in enumerate(("s5_lam_re", "s5_lam_im")):
                    sp.dma_start(srow[32 * i:32 * i + 32, :],
                                 t[name][layer].rearrange("d (g e) p -> (d g) (e p)", e=2)).then_inc(rows_in, 16)
                sp.dma_start(ls2[64:96, :], t["s5_log_step"][layer].rearrange("d (g e) -> (d g) e", e=2))\
                    .then_inc(rows_in, 16)
                for n in range(N_SLABS):
                    g, kh = divmod(n, 2)
                    if n >= NS:
                        sp.wait_ge(proj_mm if kh else slab_used, g)
                    sp.dma_start(slab[:, n % NS], t["w_in"][layer][
                        kh * HALF_K * P:(kh + 1) * HALF_K * P, g * GW:(g + 1) * GW].rearrange("(k p) n -> p k n", p=P))\
                        .then_inc(slab_in[n % NS], 16)

            @block.scalar
            def _(act):
                do = Steps(act, act_own)
                for b in range(TB):
                    do(nc.scalar.activation(s5["cos"][:, 0:8, :].rearrange("p a n -> p (a n)"), x[:, b, :], ACT.Square,
                                            accum_out=ssq[:, b:b + 1]))
                    do(nc.scalar.activation(ssq[:, 2 + b:3 + b], ssq[:, b:b + 1], ACT.Sqrt, scale=1.0 / D, bias=c("eps")),
                       rms_ready)
                act.wait_ge(s5_arg, 1)
                v = s5["v"]
                do(nc.scalar.activation(v[:, 3], v[:, 2], ACT.Exp), s5_act)
                act.wait_ge(s5_arg, 2)
                do(nc.scalar.activation(v[:, 6], v[:, 4], ACT.Exp), s5_act)
                do(nc.scalar.activation(v[:, 8], v[:, 7], ACT.Sin), s5_act)
                do(nc.scalar.activation(v[:, 10], v[:, 9], ACT.Sin), s5_act)
                for g in range(PROJ // GW):
                    act.wait_ge(proj_mm, g + 1)
                    dst = mixT[:, 4 * g:4 * g + 4] if g < 4 else rwT[:, 4 * g - 16:4 * g - 12]
                    b = 2 * (g % 4)
                    do(nc.scalar.copy(dst, bank[:, b:b + 2, :].rearrange("p b (m s) -> p (b m) s", m=2)), proj_out)

            @block.tensor
            def _(pe):
                pe.wait_ge(rows_in, 17 * 16)
                nc.tensor.transpose(bank[:, 7, 0:NROWS], rows[0:NROWS, :], c("ident")[0:NROWS, 0:NROWS])
                pe.wait_ge(ls_ready, 1)
                nc.tensor.transpose(bank[:, 7, 256:352], srow[:, :], c("ident")[0:96, 0:96]).then_inc(rows_T, 1)
                for b in range(TB):
                    pe.wait_ge(h_ready, b + 1)
                    for k in range(KT):
                        if b == 1 and k == 12:
                            pe.wait_ge(cols_ready, 2)
                        mm = nc.tensor.transpose(bank[:, 4 * b + k // 4, k % 4 * P:k % 4 * P + P], h[:, k * P:k * P + P],
                                                 c("ident"))
                        if k % 4 == 3:
                            mm.then_inc(hT_mm, 1)
                for n in range(N_SLABS):
                    g, kh = divmod(n, 2)
                    pe.wait_ge(slab_in[n % NS], 16 * (n // NS + 1))
                    if kh == 0:
                        pe.wait_ge(hT_ready, 8)
                        if g >= 4:
                            pe.wait_ge(proj_out, g - 3)
                    for m in range(4):
                        for k in range(HALF_K):
                            mm = nc.tensor.matmul(bank[:, 2 * (g % 4) + m // 2, m % 2 * SEQ:m % 2 * SEQ + SEQ],
                                                  slab[:, n % NS, k, m * P:m * P + P], hT[:, kh * HALF_K + k, :],
                                                  start=(kh == 0 and k == 0 and m % 2 == 0),
                                                  stop=(kh == 1 and k == HALF_K - 1), skip_group_check=True)
                    mm.then_inc(proj_mm if kh else slab_used, 1)

            @block.vector
            def _(dve):
                do = Steps(dve, dve_own)
                V = nc.vector
                dve.wait_ge(rows_in, 17 * 16)
                do(V.tensor_copy(srow[64:96, :].rearrange("q (e p) -> q e p", e=2),
                                 ls2[64:96, :].unsqueeze(2).to_broadcast([32, 2, S5P])), ls_ready)
                dve.wait_ge(rows_T, 1)
                do(V.tensor_copy(pcol[:], bank[:, 7, 0:NROWS]), cols_ready)
                v = s5["v"]
                do(V.tensor_copy(v[:, 0:3], bank[:, 7, 256:352].rearrange("p (a b) -> p a b", a=3)), cols_ready)
                mu = col("mu", 0, 32).rearrange("p (i s g) -> p i s g", i=4, s=2)
                m4 = mus[:].rearrange("p (i g) -> p i g", i=4)
                do(V.tensor_tensor(m4, mu[:, :, 0, :], mu[:, :, 1, :], ALU.add))
                do(V.tensor_scalar(mus[:], mus[:], -1.0, 1.0, ALU.mult, ALU.add))
                for b in range(TB):
                    dve.wait_ge(rms_ready, b + 1)
                    do(V.reciprocal(ssq[:, 4 + b:5 + b], ssq[:, 2 + b:3 + b]))
                    do(V.tensor_scalar(h[:], x[:, b, :], ssq[:, 4 + b:5 + b], None, ALU.mult), h_ready)
                    for q in range(4):
                        dve.wait_ge(hT_mm, 4 * b + q + 1)
                        do(V.tensor_tensor(hT[:, 4 * q:4 * q + 4, b * P:b * P + P],
                                           bank[:, 4 * b + q, :].rearrange("p (k s) -> p k s", k=4),
                                           col("norm_mix", 4 * q, 4).unsqueeze(2).to_broadcast([P, 4, P]), ALU.mult), hT_ready)
                    if b == 0:
                        do(V.tensor_copy(v[:, 23], v[:, 2]), s5_arg)
                dve.wait_ge(s5_act, 1)
                re, im, step = v[:, 0], v[:, 1], v[:, 3]
                do(V.tensor_tensor(v[:, 4], re, step, ALU.mult))
                do(V.tensor_tensor(v[:, 5], im, step, ALU.mult))
                big = 1.5 * 2.0 ** 23
                do(V.tensor_scalar(v[:, 11], v[:, 5], 1.0 / (2 * math.pi), big, ALU.mult, ALU.add))
                do(V.tensor_scalar(v[:, 11], v[:, 11], big, None, ALU.subtract))
                do(V.scalar_tensor_tensor(v[:, 12], v[:, 11], -6.28125, v[:, 5], ALU.mult, ALU.add))
                do(V.scalar_tensor_tensor(v[:, 12], v[:, 11], -(2 * math.pi - 6.28125), v[:, 12], ALU.mult, ALU.add))
                do(V.tensor_scalar(v[:, 7], v[:, 12], 3.1415925, -3.1415925, ALU.min, ALU.max))
                do(V.scalar_tensor_tensor(v[:, 12], v[:, 7], -1.0, v[:, 7], ALU.mult, ALU.max))
                do(V.tensor_scalar(v[:, 9], v[:, 12], -1.0, math.pi / 2, ALU.mult, ALU.add), s5_arg)
                dve.wait_ge(s5_act, 4)
                rho, sn, cs = v[:, 6], v[:, 8], v[:, 10]
                do(V.tensor_tensor(v[:, 11], rho, cs, ALU.mult))
                do(V.tensor_scalar(v[:, 11], v[:, 11], -1.0, None, ALU.add))
                do(V.tensor_tensor(v[:, 12], rho, sn, ALU.mult))
                do(V.tensor_tensor(v[:, 13], re, re, ALU.mult))
                do(V.tensor_tensor(v[:, 14], im, im, ALU.mult))
                do(V.tensor_tensor(v[:, 13], v[:, 13], v[:, 14], ALU.add))
                do(V.reciprocal(v[:, 13], v[:, 13]))
                do(V.tensor_tensor(v[:, 14], v[:, 11], re, ALU.mult))
                do(V.tensor_tensor(v[:, 15], v[:, 12], im, ALU.mult))
                do(V.tensor_tensor(v[:, 14], v[:, 14], v[:, 15], ALU.add))
                do(V.tensor_tensor(v[:, 16], v[:, 14], v[:, 13], ALU.mult))
                do(V.tensor_tensor(v[:, 14], v[:, 12], re, ALU.mult))
                do(V.tensor_tensor(v[:, 15], v[:, 11], im, ALU.mult))
                do(V.tensor_tensor(v[:, 14], v[:, 14], v[:, 15], ALU.subtract))
                do(V.tensor_tensor(v[:, 17], v[:, 14], v[:, 13], ALU.mult))
                Ec, Es = s5["cos"], s5["sin"]
                do(V.memset(Ec[:, :, 0:1], 1.0))
                do(V.memset(Es[:, :, 0:1], 0.0))
                wr, wi, wr2, wi2 = v[:, 18], v[:, 19], v[:, 20], v[:, 21]
                do(V.tensor_copy(wr, cs))
                do(V.tensor_copy(wi, sn))
                n = 1
                while n < SEQ:
                    gq = min(32, 1024 // n)
                    for g in range(0, 32, gq):
                        a = tmp[:, 0, 0:gq * n].rearrange("p (g n) -> p g n", g=gq)
                        b_ = tmp[:, 1, 0:gq * n].rearrange("p (g n) -> p g n", g=gq)
                        br = wr[:, g:g + gq].unsqueeze(2).to_broadcast([P, gq, n])
                        bi = wi[:, g:g + gq].unsqueeze(2).to_broadcast([P, gq, n])
                        lo_c, lo_s = Ec[:, g:g + gq, 0:n], Es[:, g:g + gq, 0:n]
                        do(V.tensor_tensor(a, lo_c, br, ALU.mult), wait=False)
                        do(V.tensor_tensor(b_, lo_s, bi, ALU.mult))
                        do(V.tensor_tensor(Ec[:, g:g + gq, n:2 * n], a, b_, ALU.subtract))
                        do(V.tensor_tensor(a, lo_s, br, ALU.mult), wait=False)
                        do(V.tensor_tensor(b_, lo_c, bi, ALU.mult))
                        do(V.tensor_tensor(Es[:, g:g + gq, n:2 * n], a, b_, ALU.add))
                    do(V.tensor_tensor(v[:, 22], wi, wi, ALU.mult), wait=False)
                    do(V.tensor_tensor(wr2, wr, wr, ALU.mult))
                    do(V.scalar_tensor_tensor(wi2, wr, 2.0, wi, ALU.mult, ALU.mult))
                    do(V.tensor_tensor(wr, wr2, v[:, 22], ALU.subtract), wait=False)
                    do(V.tensor_copy(wi, wi2))
                    n *= 2


def attend(nc, t, layer, sem, sb, ps, c, col, mixT, ycT):
    w_in, unit_mm, unit_out = sem("at_w_in"), sem("at_mm"), sem("at_out")
    sq_ready, rstd_ready, qn_ready, rope_ready = sem("at_sq"), sem("at_rstd"), sem("at_qn"), sem("at_rope")
    root_ready, max_ready, exp_ready, prob_ready = sem("at_root"), sem("at_max"), sem("at_exp"), sem("at_prob")
    dve_own, act_own = sem("at_dve"), sem("at_act")
    with ExitStack() as st:
        wf = sb(st, "at_wf", [P, GT, GW])
        arena = sb(st, "at_arena", [P, 4096])
        Z = arena[:, 0:2048].rearrange("p (h b n) -> p h b n", h=4, b=TB)
        S = arena[:, 0:2048].rearrange("p (h b n) -> p h b n", h=4, b=TB)
        fT = arena[:, 2048:3072].rearrange("p (h n) -> p h n", h=4)
        PT_ = arena[:, 2048:4096].rearrange("p (h k n) -> p h k n", h=4, k=TB)
        qk = sb(st, "at_qk", [P, 6, SEQ])
        qa = sb(st, "at_qa", [P, 6, SEQ])
        qb = sb(st, "at_qb", [P, 6, SEQ])
        vt = sb(st, "at_v", [P, TB, 2, P])
        Pr = sb(st, "at_p", [P, 4, TB, SEQ])
        st8 = sb(st, "at_stat", [P, 4, 8])
        bank = ps(st, "at_bank", [P, 4, 512])
        f6 = lambda a: a.rearrange("p h n -> p (h n)")

        with nc.Block() as block:
            @block.sync
            def _(sp):
                sp.dma_start(wf[:], t["fourier_w"][layer].rearrange("(k p) n -> p k n", p=P)).then_inc(w_in, 16)

            @block.tensor
            def _(pe):
                unit = [0]

                def begin():
                    if unit[0] >= 4:
                        pe.wait_ge(unit_out, unit[0] - 3)
                    return bank[:, unit[0] % 4, :]

                def end(mm):
                    mm.then_inc(unit_mm, 1)
                    unit[0] += 1

                mmul = nc.tensor.matmul
                for h in range(4):
                    o = begin()
                    for b in range(TB):
                        mm = mmul(o[:, b * 256:b * 256 + 256], mixT[:, T_A + h, b * P:b * P + P], c("dft_ch"),
                                  start=(b == 0), stop=True, skip_group_check=True)
                    end(mm)
                pe.wait_ge(unit_out, 4)
                for hp in range(2):
                    o = begin()
                    for e in range(2):
                        for b in range(TB):
                            for part in range(2):
                                at = (b * 2 + part) * SEQ
                                mm = mmul(o[:, e * 256:e * 256 + 256], Z[:, 2 * hp + e, b, part * P:part * P + P],
                                          c("dft_seq", at, at + SEQ), start=(e == 0 and b == 0 and part == 0),
                                          stop=(b == 1 and part == 1), skip_group_check=True)
                    end(mm)
                pe.wait_ge(w_in, 16)
                pe.wait_ge(unit_out, 6)
                for mp in range(2):
                    o = begin()
                    for e in range(2):
                        for k in range(GT):
                            m = 2 * mp + e
                            mm = mmul(o[:, e * 256:e * 256 + 256], wf[:, k, m * P:m * P + P], fT[:, k, :],
                                      start=(e == 0 and k == 0), stop=(k == GT - 1), skip_group_check=True)
                    end(mm)
                pe.wait_ge(sq_ready, 1)
                for g in range(3):
                    o = begin()
                    end(mmul(o, c("ones"), f6(qb)[:, g * 512:g * 512 + 512], start=True, stop=True))
                pe.wait_ge(qn_ready, 1)
                for g in range(3):
                    o = begin()
                    end(mmul(o, c("rot"), f6(qk)[:, g * 512:g * 512 + 512], start=True, stop=True))
                o = begin()
                for g in range(2):
                    for b in range(TB):
                        at = (b * 2 + g) * P
                        mm = nc.tensor.transpose(o[:, at:at + P], mixT[:, T_V + g, b * P:b * P + P], c("ident"))
                end(mm)
                pe.wait_ge(rope_ready, 1)
                for h in range(4):
                    o = begin()
                    for b in range(TB):
                        mm = mmul(o[:, b * 256:b * 256 + 256], qa[:, h, b * P:b * P + P], qa[:, 4 + h // 2, :],
                                  start=(b == 0), stop=True, skip_group_check=True)
                    end(mm)
                pe.wait_ge(prob_ready, 1)
                for h in range(4):
                    o = begin()
                    for k in range(TB):
                        for b in range(TB):
                            at = k * 256 + b * P
                            mm = nc.tensor.transpose(o[:, at:at + P], Pr[:, h, b, k * P:k * P + P], c("ident"))
                    end(mm)
                pe.wait_ge(unit_out, unit[0])
                for hp in range(2):
                    o = begin()
                    for e in range(2):
                        h = 2 * hp + e
                        for k in range(TB):
                            mm = mmul(o[:, e * 256:e * 256 + 256], vt[:, k, h // 2, :], PT_[:, h, k, :],
                                      start=(e == 0 and k == 0), stop=(k == 1), skip_group_check=True)
                    end(mm)

            @block.scalar
            def _(act):
                do = Steps(act, act_own)
                unit = [0]

                def take(dst, func=ACT.Copy, **kw):
                    act.wait_ge(unit_mm, unit[0] + 1)
                    src = bank[:, unit[0] % 4, :]
                    unit[0] += 1
                    do(nc.scalar.activation(dst, src, func, **kw), unit_out)

                for h in range(4):
                    take(Z[:, h].rearrange("p b n -> p (b n)"))
                for hp in range(2):
                    take(f6(fT[:, 2 * hp:2 * hp + 2]))
                for mp in range(2):
                    take(f6(ycT[:, 2 * mp:2 * mp + 2]))
                for g in range(3):
                    take(f6(qa)[:, g * 512:g * 512 + 512], ACT.Sqrt, scale=1.0 / HEAD, bias=c("eps"))
                act.wait_ge(qn_ready, 1)
                for g in range(3):
                    take(f6(qb)[:, g * 512:g * 512 + 512])
                take(vt[:].rearrange("p b g n -> p (b g n)"))
                for h in range(4):
                    take(S[:, h].rearrange("p b n -> p (b n)"))
                act.wait_ge(max_ready, 1)
                for h in range(4):
                    for b in range(TB):
                        i = 2 * h + b
                        do(nc.scalar.activation(Pr[:, h, b, :], S[:, h, b, :], ACT.Exp, scale=SCALE,
                                                bias=st8[:, 1, i:i + 1], accum_out=st8[:, 2, i:i + 1]), exp_ready)
                for h in range(4):
                    take(PT_[:, h].rearrange("p k n -> p (k n)"))
                for hp in range(2):
                    take(f6(ycT[:, 8 + 2 * hp:10 + 2 * hp]))

            @block.vector
            def _(dve):
                do = Steps(dve, dve_own)
                V = nc.vector
                do(V.tensor_tensor(qb[:], mixT[:, T_Q:T_Q + 6, :], mixT[:, T_Q:T_Q + 6, :], ALU.mult), sq_ready)
                dve.wait_ge(unit_out, 11)
                do(V.reciprocal(qa[:], qa[:]))
                for i in range(6):
                    do(V.scalar_tensor_tensor(qk[:, i, :], mixT[:, T_Q + i, :], col("q_norm" if i < 4 else "k_norm"),
                                              qa[:, i, :], ALU.mult, ALU.mult))
                do(V.tensor_tensor(qa[:], qk[:], c("cos").unsqueeze(1).to_broadcast([P, 6, SEQ]), ALU.mult), qn_ready)
                dve.wait_ge(unit_out, 14)
                do(V.tensor_tensor(qb[:], qb[:], c("sin").unsqueeze(1).to_broadcast([P, 6, SEQ]), ALU.mult))
                do(V.tensor_tensor(qa[:], qa[:], qb[:], ALU.add), rope_ready)
                dve.wait_ge(unit_out, 19)
                do(V.tensor_reduce(st8[:, 0], S.rearrange("p h b n -> p (h b) n"), AX.X, ALU.max))
                do(V.tensor_scalar(st8[:, 1], st8[:, 0], -SCALE, None, ALU.mult), max_ready)
                dve.wait_ge(exp_ready, 8)
                do(V.reciprocal(st8[:, 3], st8[:, 2]))
                p8 = Pr[:].rearrange("p h b n -> p (h b) n")
                do(V.tensor_tensor(p8, p8, st8[:, 3].unsqueeze(2).to_broadcast([P, 8, SEQ]), ALU.mult), prob_ready)


def s5_branch(nc, t, layer, sem, sb, ps, c, col, mixT, ycT, s5):
    raw_in, exp_ready, unit_mm, unit_out = sem("s5_raw_in"), sem("s5_exp"), sem("s5_mm"), sem("s5_out")
    c_ready, bu_mm, bu_used, x_ready, y_mm = sem("s5_c"), sem("s5_bu_mm"), sem("s5_bu_used"), sem("s5_x"), sem("s5_y_mm")
    pre_ready, gelu_ready, dve_own, act_own = sem("s5_pre"), sem("s5_gelu"), sem("s5_dve"), sem("s5_act")
    with ExitStack() as st:
        wglu = sb(st, "s5_wglu", [P, GT, GW])
        raw = sb(st, "s5_raw", [P, 4, 512])
        work = sb(st, "s5_work", [P, 6, 1024])
        BT = sb(st, "s5_BT", [P, 2, 8, P])
        CT = sb(st, "s5_CT", [P, 2, 8, P])
        y = sb(st, "s5_y", [P, GT, SEQ])
        bu = ps(st, "s5_bu", [P, 4, 512])
        bank = ps(st, "s5_bank", [P, 3, 512])
        yb = ps(st, "s5_yb", [P, 512])
        bexp = [work[:, i].rearrange("p (q n) -> p q n", q=32) for i in range(2)]
        cexp = [work[:, 2 + i].rearrange("p (q n) -> p q n", q=8) for i in range(2)]
        order = [(ct, d) for ct in range(GT) for d in range(2)]

        with nc.Block() as block:
            @block.sync
            def _(sp):
                for i, name in enumerate(("s5_b_re", "s5_b_im")):
                    sp.dma_start(raw[:, i].rearrange("p (q h) -> p q h", q=32),
                                 t[name][layer].rearrange("d (g e) p h -> (e p) (d g) h", e=2)).then_inc(raw_in, 16)
                for i, name in enumerate(("s5_c_re", "s5_c_im")):
                    sp.dma_start(raw[:, 2 + i].rearrange("p (q n) -> p q n", q=8),
                                 t[name][layer].rearrange("d (q g) h p -> (g h) (d q) p", q=GT)).then_inc(raw_in, 16)
                sp.dma_start(wglu[:], t["s5_w_glu"][layer].rearrange("(k p) n -> p k n", p=P)).then_inc(raw_in, 16)

            @block.tensor
            def _(pe):
                unit = [0]
                pe.wait_ge(raw_in, 80)
                pe.wait_ge(exp_ready, 8)
                for which in range(2):
                    for part in range(2):
                        for d in range(2):
                            if unit[0] >= 3:
                                pe.wait_ge(unit_out, unit[0] - 2)
                            for q in range(4):
                                j = d * 4 + q
                                src = bexp[part][:, 4 * j:4 * j + 4, :].rearrange("p a b -> p (a b)") if which == 0 \
                                    else cexp[part][:, j, :]
                                mm = nc.tensor.transpose(bank[:, unit[0] % 3, q * P:q * P + P], src, c("ident"))
                            mm.then_inc(unit_mm, 1)
                            unit[0] += 1
                pe.wait_ge(unit_out, 8)
                for i in range(len(order) + 1):
                    if i < len(order):
                        ct, d = order[i]
                        if i:
                            pe.wait_ge(bu_used, i)
                        for j in range(4):
                            for part in range(2):
                                mm = nc.tensor.matmul(bu[:, j, part * SEQ:part * SEQ + SEQ],
                                                      BT[32 * j:32 * j + 32, part, d * 4 + ct, :],
                                                      mixT[32 * j:32 * j + 32, T_B + ct, :],
                                                      start=(part == 0), stop=True, skip_group_check=True)
                        mm.then_inc(bu_mm, 1)
                    if i:
                        ct, d = order[i - 1]
                        pe.wait_ge(x_ready, i)
                        pe.wait_ge(c_ready, 1)
                        if ct and d == 0:
                            pe.wait_ge(pre_ready, ct)
                        for j in range(4):
                            for part in range(2):
                                mm = nc.tensor.matmul(yb[32 * j:32 * j + 32, 0:SEQ],
                                                      CT[:, part, d * 4 + ct, 32 * j:32 * j + 32],
                                                      work[:, part, j * SEQ:j * SEQ + SEQ],
                                                      start=(d == 0 and part == 0), stop=(d == 1 and part == 1),
                                                      skip_group_check=True)
                        mm.then_inc(y_mm, 1)
                pe.wait_ge(gelu_ready, GT)
                for mp in range(2):
                    for e in range(2):
                        m = 2 * mp + e
                        for k in range(GT):
                            mm = nc.tensor.matmul(bank[:, mp, e * 256:e * 256 + 256], wglu[:, k, m * P:m * P + P],
                                                  y[:, k, :], start=(e == 0 and k == 0), stop=(k == GT - 1),
                                                  skip_group_check=True)
                    mm.then_inc(unit_mm, 1)

            @block.scalar
            def _(act):
                do = Steps(act, act_own)
                for u in range(8):
                    act.wait_ge(unit_mm, u + 1)
                    which, part, d = u // 4, u // 2 % 2, u % 2
                    dst = (BT, CT)[which][:, part, 4 * d:4 * d + 4, :].rearrange("p q n -> p (q n)")
                    do(nc.scalar.copy(dst, bank[:, u % 3, :]), unit_out)
                for ct in range(GT):
                    act.wait_ge(pre_ready, ct + 1)
                    do(nc.scalar.activation(y[:, ct, :], y[:, ct, :], ACT.Gelu_apprx_tanh), gelu_ready)
                for mp in range(2):
                    act.wait_ge(unit_mm, 9 + mp)
                    do(nc.scalar.activation(raw[:, mp, :], bank[:, mp, :], ACT.Sigmoid), unit_out)

            @block.vector
            def _(dve):
                do = Steps(dve, dve_own)
                V = nc.vector
                for i in range(2):
                    do(V.memset(work[:, i, :], 0.0))
                dve.wait_ge(raw_in, 80)
                for i in range(2):
                    r = raw[:, i].rearrange("p (q h) -> p q h", q=32)
                    do(V.tensor_copy(bexp[i][0:64, :, 0:16], r[0:64]), exp_ready, wait=False)
                    do(V.tensor_copy(bexp[i][64:128, :, 16:32], r[64:128]), exp_ready, wait=False)
                    r = raw[:, 2 + i].rearrange("p (q n) -> p q n", q=8)
                    do(V.tensor_scalar(cexp[i][:, :, 0:64], r, c("even"), None, ALU.mult), exp_ready, wait=False)
                    do(V.tensor_scalar(cexp[i][:, :, 64:128], r, c("odd"), None, ALU.mult), exp_ready, wait=False)
                dve.wait_ge(unit_out, 8)
                v = s5["v"]
                cr = CT[:, 0].rearrange("p q (j n) -> p (q j) n", j=4)
                ci = CT[:, 1].rearrange("p q (j n) -> p (q j) n", j=4)
                kr = v[:, 16].unsqueeze(2).to_broadcast([P, 32, 32])
                ki = v[:, 17].unsqueeze(2).to_broadcast([P, 32, 32])
                w = [work[:, i].rearrange("p (q n) -> p q n", q=32) for i in range(6)]
                do(V.tensor_tensor(w[0], cr, kr, ALU.mult), wait=False)
                do(V.tensor_tensor(w[1], ci, ki, ALU.mult), wait=False)
                do(V.tensor_tensor(w[2], cr, ki, ALU.mult), wait=False)
                do(V.tensor_tensor(w[3], ci, kr, ALU.mult))
                do(V.tensor_tensor(cr, w[0], w[1], ALU.subtract), wait=False)
                do(V.scalar_tensor_tensor(ci, w[2], -1.0, w[3], ALU.mult, ALU.subtract), c_ready)
                for i, (ct, d) in enumerate(order):
                    q0 = d * 16 + ct * 4
                    e = slice(None, None, -1) if d else slice(None)
                    tc, ts = s5["cos"][:, q0:q0 + 4, e], s5["sin"][:, q0:q0 + 4, e]
                    f = [work[:, k].rearrange("p (j s) -> p j s", j=4) for k in range(6)]
                    re, im = bu[:, :, 0:SEQ], bu[:, :, SEQ:2 * SEQ]
                    if i:
                        dve.wait_ge(y_mm, i)
                    dve.wait_ge(bu_mm, i + 1)
                    do(V.tensor_tensor(f[2], re, tc, ALU.mult), wait=False)
                    do(V.tensor_tensor(f[3], im, ts, ALU.mult), wait=False)
                    do(V.tensor_tensor(f[4], im, tc, ALU.mult), wait=False)
                    do(V.tensor_tensor(f[5], re, ts, ALU.mult), bu_used)
                    do(V.tensor_tensor(f[0], f[2], f[3], ALU.add), wait=False)
                    do(V.tensor_tensor(f[1], f[4], f[5], ALU.subtract))
                    for part in range(2):
                        for j in range(4):
                            do(V.tensor_tensor_scan(f[2 + part][:, j, e], v[:, 6, q0 + j:q0 + j + 1].to_broadcast([P, SEQ]),
                                                    f[part][:, j, e], 0.0, ALU.mult, ALU.add), wait=(part == 1 and j == 3))
                    do(V.tensor_tensor(f[4], f[2], tc, ALU.mult), wait=False)
                    do(V.tensor_tensor(f[5], f[3], ts, ALU.mult))
                    do(V.tensor_tensor(f[0], f[4], f[5], ALU.subtract))
                    do(V.tensor_tensor(f[4], f[2], ts, ALU.mult), wait=False)
                    do(V.tensor_tensor(f[5], f[3], tc, ALU.mult))
                    do(V.tensor_tensor(f[1], f[4], f[5], ALU.add), x_ready)
                    if d == 1:
                        dve.wait_ge(y_mm, i + 1)
                        do(V.scalar_tensor_tensor(y[:, ct, :], mixT[:, T_B + ct, :], col("s5_d", ct), yb[:, 0:SEQ],
                                                  ALU.mult, ALU.add), pre_ready)
                dve.wait_ge(unit_out, 10)
                do(V.tensor_tensor(ycT[:, 4:8, :].rearrange("p k s -> p (k s)"), y[:].rearrange("p k s -> p (k s)"),
                                   raw[:, 0:2, :].rearrange("p k s -> p (k s)"), ALU.mult))


def rwkv(nc, t, layer, sem, sb, ps, c, col, mus, rwT, ycT):
    both = lambda *names: [f"{n}{d}" for n in names for d in range(2)]
    PE_EV = (["trV"] + both("pa", "pc", "nn") + ["trA"] + both("vp", "sq2") + ["trB", "trK"]
             + both("sq4", "w2", "w4", "sq8", "w8", "x", "no", "z", "qy", "gh"))
    ACT_EV = ["trV", "trA"] + both("vp", "sq2") + ["trB", "trK"] + both("sq4", "sq8", "x", "no", "gh")
    DVE_EV = both("pa", "pc", "nn", "w2", "w4", "w8", "z", "qy", "gh")

    def at(events, i, name):
        return i * len(events) + events.index(name) + 1

    w_in, low_mm, low_out, z_ready = sem("rw_w_in"), sem("rw_low_mm"), sem("rw_low_out"), sem("rw_z_ready")
    up_mm, up_out, kq_ready, kq_mm, root_out, prepared = [sem("rw_" + n) for n in ("up_mm", "up_out", "kq", "kq_mm",
                                                                                  "kk_root", "prepared")]
    pe_ev, act_ev, dve_ev = sem("rw_pe"), sem("rw_act"), sem("rw_dve")
    state_mm, state_ready, y_ready = sem("rw_state_mm"), sem("rw_state"), sem("rw_y_ready")
    stat_mm, root_ready, sqd_ready = sem("rw_stat_mm"), sem("rw_root"), sem("rw_sqd")
    dve_own, act_own = sem("rw_dve_own"), sem("rw_act_own")
    Q = 2 * GT
    with ExitStack() as st:
        w1 = sb(st, "rw_w1", [P, GT, P])
        g1 = sb(st, "rw_g1", [P, GT, 96])
        w2 = sb(st, "rw_w2", [P, GW])
        g2 = sb(st, "rw_g2", [96, GW])
        low = sb(st, "rw_low", [P, SEQ])
        lowg = sb(st, "rw_lowg", [96, SEQ])
        zs = sb(st, "rw_zs", [P, GT, SEQ])
        diag = zs[:].rearrange("p a s -> p (a s)").rearrange("p (d n k) -> p d n k", d=2, n=NCH)
        keep = sb(st, "rw_keep", [P, GT])
        sr, sk, sv, kk = [sb(st, f"rw_{n}", [P, SEQ]) for n in ("sr", "sk", "sv", "kkn")]
        kq = sb(st, "rw_kq", [P, SEQ])
        kd, kb, Pc, IP, Pe, D1, BH, KH, wend, BTc = [sb(st, f"rw_{n}", [P, 2, SEQ]) for n in
                                                     ("kd", "kb", "pc", "ip", "pe", "d1", "bh", "kh", "wend", "btc")]
        KTc = sb(st, "rw_ktc", [P, 2, SEQ])
        pend = sb(st, "rw_pend", [P, 2, NCH])
        ARs = sb(st, "rw_ar", [P, 2, 2, TB, 2, P])
        R = sb(st, "rw_r", [P, 2, 4, P])
        mats = {n: sb(st, f"rw_{n}", [P, 2, 4, P]) for n in ("NT", "NTo", "Rb", "Aak", "Rk", "N", "N2T", "N2", "W")}
        mats["N4T"], mats["N4"], mats["N8"] = mats["NT"], mats["N"], mats["N2T"]
        Yo = mats["N2"]
        Bt = sb(st, "rw_bt", [P, 2, TB, P])
        Kt = sb(st, "rw_kt", [P, 2, TB, P])
        Vt = sb(st, "rw_vt", [P, TB, P])
        G = sb(st, "rw_G", [P, NCH, Q, RH])
        H = sb(st, "rw_H", [P, NCH, Q, RH])
        QT = sb(st, "rw_QT", [P, Q, SEQ])
        yin = sb(st, "rw_yin", [P, GT, SEQ])
        bonus = sb(st, "rw_bonus", [P, GT, SEQ])
        gt = sb(st, "rw_gt", [P, GT, SEQ])
        S = mats["W"][:].rearrange("p d j k -> p (d j k)").rearrange("p (d q k) -> p d q k", d=2, q=Q)
        bank = ps(st, "rw_bank", [P, 8, 512])
        flat = lambda a: a.rearrange("p a s -> p (a s)")
        big = lambda a, i: a[:].rearrange("p n q k -> p (n q k)")[:, i * 1024:i * 1024 + 1024]
        dlt, sqd = big(G, 0), big(G, 1)
        decay = lambda i: QT[:, 2 * i:2 * i + 2, :]
        rate = lambda i: G[:, 0:4, 2 * i:2 * i + 2, :].rearrange("p n d k -> p d n k")

        with nc.Block() as block:
            @block.sync
            def _(sp):
                for d in range(2):
                    sp.dma_start(w1[:, :, 32 * d:32 * d + 32], t["rwkv_w1"][layer, d].rearrange("(k p) n -> p k n", p=P))\
                        .then_inc(w_in, 16)
                    sp.dma_start(w1[:, :, 64 + 32 * d:96 + 32 * d],
                                 t["rwkv_a1"][layer, d].rearrange("(k p) n -> p k n", p=P)).then_inc(w_in, 16)
                    sp.dma_start(w2[32 * d:32 * d + 32, :], t["rwkv_w2"][layer, d]).then_inc(w_in, 16)
                    sp.dma_start(w2[64 + 32 * d:96 + 32 * d, :], t["rwkv_a2"][layer, d]).then_inc(w_in, 16)
                sp.dma_start(g1[:], t["rwkv_g1"][layer].rearrange("(k p) n -> p k n", p=P)).then_inc(w_in, 16)
                sp.dma_start(g2[:], t["rwkv_g2"][layer]).then_inc(w_in, 16)

            @block.tensor
            def _(pe):
                mmul, tr = nc.tensor.matmul, nc.tensor.transpose
                pe.wait_ge(w_in, 160)
                pe.wait_ge(z_ready, 1)
                for k in range(GT):
                    mmul(bank[:, 0, 0:SEQ], w1[:, k, :], zs[:, k, :], start=(k == 0), stop=(k == GT - 1))
                for k in range(GT):
                    mm = mmul(bank[0:96, 1, 0:SEQ], g1[:, k, :], zs[:, k, :], start=(k == 0), stop=(k == GT - 1))
                mm.then_inc(low_mm, 1)
                pe.wait_ge(low_out, 3)
                for i in range(GT):
                    if i:
                        pe.wait_ge(up_out, 5 * i)
                    for u in range(4):
                        mmul(bank[:, u, 0:SEQ], w2[32 * u:32 * u + 32, i * P:i * P + P], low[32 * u:32 * u + 32, :],
                             start=True, stop=True)
                    mmul(bank[:, 4, 0:SEQ], g2[:, i * P:i * P + P], lowg[:], start=True, stop=True).then_inc(up_mm, 1)

                def head_sums(i, which):
                    pe.wait_ge(kq_ready, 2 * i + which + 1)
                    mmul(bank[:, 6 + which, 0:SEQ], c("heads"), kq[:], start=True, stop=True).then_inc(kq_mm, 1)

                head_sums(0, 0)
                head_sums(0, 1)
                pe.wait_ge(up_out, 20)
                for i in range(GT):
                    AR = ARs[:, i % 2]
                    dve = lambda name: pe.wait_ge(dve_ev, at(DVE_EV, i, name))
                    act = lambda name: pe.wait_ge(act_ev, at(ACT_EV, i, name))
                    ev = lambda mm: mm.then_inc(pe_ev, 1)
                    last = i == GT - 1
                    pe.wait_ge(prepared, i + 1)
                    for b in range(TB):
                        mm = tr(bank[:, 6, b * P:b * P + P], sv[:, b * P:b * P + P], c("ident"))
                    ev(mm)
                    if i:
                        pe.wait_ge(dve_ev, at(DVE_EV, i - 1, "gh1"))
                        pe.wait_ge(act_ev, at(ACT_EV, i - 1, "gh1"))

                    def pairs(d, left, banks):
                        for b in range(TB):
                            for e in range(2):
                                r = slice(RH * e, RH * e + RH)
                                mm = mmul(bank[:, banks[e], b * 256:b * 256 + 256], left[r, d, b * P:b * P + P],
                                          AR[r, d, b, :, :].rearrange("p a s -> p (a s)"), start=(b == 0), stop=True,
                                          skip_group_check=True)
                        ev(mm)

                    def product(d, b, left, right):
                        for j in range(4):
                            mm = mmul(bank[:, b, j * P:j * P + P], left[:, d, j, :], right[:, d, j, :],
                                      start=(j == 0), stop=True, skip_group_check=True)
                        return mm

                    pairs(0, BH, (0, 1))
                    pairs(1, BH, (2, 3))
                    pairs(0, KH, (4, 5))
                    dve("pa0")
                    pairs(1, KH, (0, 1))
                    for d in range(2):
                        dve(("pa1", "pc0")[d])
                        for b in range(TB):
                            for e in range(2):
                                r = slice(RH * e, RH * e + RH)
                                mm = mmul(bank[:, 2 + 2 * d + e, b * P:b * P + P], AR[r, d, b, 0, :], BH[r, d, b * P:b * P + P],
                                          start=(b == 0), stop=True, skip_group_check=True)
                        ev(mm)

                    def turn(n, b0, src):
                        for d in range(2):
                            for b in range(TB):
                                mm = tr(bank[:, b0, (2 * d + b) * P:(2 * d + b + 1) * P], src(d, b), c("ident"))
                        ev(mm)

                    turn("trA", 7, lambda d, b: AR[:, d, b, 0, :])
                    dve("pc1")
                    act("trV")
                    for d in range(2):
                        for j in range(4):
                            e, b = divmod(j, 2)
                            mm = mmul(bank[:, d, j * RH:j * RH + RH], mats["Aak"][:, d, j, :],
                                      Vt[:, b, e * RH:e * RH + RH], start=(j == 0), stop=True, skip_group_check=True)
                        ev(mm)
                    for d in range(2):
                        dve(f"nn{d}")
                        product(d, 2 + 2 * d, mats["N"], mats["NT"])
                        ev(product(d, 3 + 2 * d, mats["NT"], mats["N"]))
                    turn("trB", 6, lambda d, b: BTc[:, d, b * P:b * P + P])
                    act("trA")
                    turn("trK", 7, lambda d, b: KTc[:, d, b * P:b * P + P])
                    for d in range(2):
                        act(f"sq2{d}")
                        product(d, 2 * d, mats["N2"], mats["N2T"])
                        ev(product(d, 2 * d + 1, mats["N2T"], mats["N2"]))
                    for d in range(2):
                        ev(product(d, 4 + d, mats["N2"], mats["W"]))
                    if not last:
                        act("trK")
                        head_sums(i + 1, 0)
                    for d in range(2):
                        act(f"sq4{d}")
                        dve(f"w2{d}")
                        ev(product(d, d, mats["N4"], mats["W"]))
                    for d in range(2):
                        ev(product(d, 2 + d, mats["N4T"], mats["N4"]))
                    if not last:
                        head_sums(i + 1, 1)
                    for d in range(2):
                        act(f"sq8{d}")
                        dve(f"w4{d}")
                        ev(product(d, 4 + d, mats["N8"], mats["W"]))
                    for d in range(2):
                        dve(f"w8{d}")
                        ev(product(d, d, mats["W"], R))
                    for d in range(2):
                        act(f"x{d}")
                        ev(product(d, 2 + d, mats["NTo"], R))
                    for d in range(2):
                        act(f"no{d}")
                        ev(product(d, 4 + d, mats["W"], Yo))
                    for d in range(2):
                        dve(f"z{d}")
                        for b in range(TB):
                            for e in range(2):
                                j, rows = 2 * e + b, slice(RH * e, RH * e + RH)
                                mmul(bank[rows, d, b * P:b * P + P], R[:, d, j, RH:P], mats["Rb"][:, d, j, :],
                                     start=(b == 0), stop=True, skip_group_check=True)
                                mmul(bank[rows, d, 256 + b * P:384 + b * P], R[:, d, j, 0:RH], mats["Rb"][:, d, j, :],
                                     start=False, stop=False, skip_group_check=True)
                                mm = mmul(bank[rows, d, 256 + b * P:384 + b * P], Vt[:, b, e * RH:e * RH + RH],
                                          mats["Rk"][:, d, j, :], start=False, stop=True, skip_group_check=True)
                        ev(mm)
                    act("trK")
                    for d in range(2):
                        if d:
                            dve("gh0")
                            act("gh0")
                        for b in range(TB):
                            for e in range(2):
                                for q in range(CPB):
                                    j, rows, k = 2 * e + b, slice(RH * e, RH * e + RH), slice(CH * q, CH * q + CH)
                                    o = bank[rows, 2 + q, b * P:b * P + P]
                                    mmul(o[:, 0:RH], R[k, d, j, RH:P], Bt[k, d, b, rows], start=(b == 0), stop=True,
                                         skip_group_check=True)
                                    mmul(o[:, RH:P], Bt[k, d, b, rows], R[k, d, j, 0:RH], start=False, stop=False,
                                         skip_group_check=True)
                                    mm = mmul(o[:, RH:P], Kt[k, d, b, rows], Vt[k, b, rows], start=False, stop=True,
                                              skip_group_check=True)
                        ev(mm)
                pe.wait_ge(dve_ev, at(DVE_EV, GT - 1, "gh1"))
                pe.wait_ge(act_ev, at(ACT_EV, GT - 1, "gh1"))
                for n in range(NCH):
                    pe.wait_ge(state_ready, n + 1)
                    for q in range(Q):
                        i, d = divmod(q, 2)
                        ch = n if d == 0 else NCH - 1 - n
                        at_ = i % 2 * SEQ + ch * CH
                        for e in range(2):
                            r = slice(RH * e, RH * e + RH)
                            mm = mmul(bank[r, 2 * d + i // 2, at_:at_ + CH], S[r, n % 2, q, :], QT[r, q, ch * CH:ch * CH + CH],
                                      start=(n == 0 and i % 2 == 0), stop=True, skip_group_check=True)
                    if n < NCH - 1:
                        for q in range(Q):
                            for e in range(2):
                                r = slice(RH * e, RH * e + RH)
                                mm = mmul(bank[r, 4 + n % 2, q * RH:q * RH + RH], G[r, n, q, :], S[r, n % 2, q, :],
                                          start=(q == 0), stop=True, skip_group_check=True)
                    mm.then_inc(state_mm, 1)
                pe.wait_ge(y_ready, 1)
                for g in range(2):
                    mm = mmul(bank[:, 6 + g, :], c("heads"), flat(yin[:])[:, g * 512:g * 512 + 512], start=True, stop=True)
                mm.then_inc(stat_mm, 1)
                pe.wait_ge(sqd_ready, 1)
                for g in range(2):
                    mm = mmul(bank[:, 4 + g, :], c("heads"), sqd[:, g * 512:g * 512 + 512], start=True, stop=True)
                mm.then_inc(stat_mm, 1)

            @block.scalar
            def _(act):
                do = Steps(act, act_own)
                A = nc.scalar
                act.wait_ge(low_mm, 1)
                do(A.activation(low[0:64, :], bank[0:64, 0, 0:SEQ], ACT.Tanh), low_out)
                do(A.copy(low[64:128, :], bank[64:128, 0, 0:SEQ]), low_out)
                do(A.activation(lowg[:], bank[0:96, 1, 0:SEQ], ACT.Sigmoid), low_out)
                for i in range(GT):
                    act.wait_ge(up_mm, i + 1)
                    for d in range(2):
                        do(A.activation(decay(i)[:, d], bank[:, d, 0:SEQ], ACT.Sigmoid, bias=col("w0", 4 * d + i)), up_out)
                        do(A.activation(rate(i)[:, d], bank[:, 2 + d, 0:SEQ].rearrange("p (n k) -> p n k", n=4), ACT.Sigmoid,
                                        bias=col("a0", 4 * d + i)), up_out)
                    do(A.copy(gt[:, i, :], bank[:, 4, 0:SEQ]), up_out)
                q2 = QT[:].rearrange("p q s -> p (q s)")
                do(A.activation(q2, q2, ACT.Exp, scale=-math.exp(-0.5)), up_out)

                def kk_root(i):
                    act.wait_ge(kq_mm, 2 * i + 1)
                    do(A.activation(kk[:], bank[:, 6, 0:SEQ], ACT.Sqrt, bias=c("eps_kk")), root_out)

                kk_root(0)
                for i in range(GT):
                    pe = lambda name: act.wait_ge(pe_ev, at(PE_EV, i, name))
                    jk = lambda a, d: a[:, d].rearrange("p j k -> p (j k)")
                    pe("trV")
                    do(A.copy(flat(Vt[:]), bank[:, 6, 0:256]), act_ev)
                    pe("trA")
                    src = bank[:, 7, :].rearrange("p (d b e k) -> p d b e k", d=2, b=TB, e=2)
                    dst = R[:, :, :, RH:P].rearrange("p d (e b) k -> p d b e k", e=2)
                    do(A.copy(dst[:, 0], src[:, 0]))
                    do(A.copy(dst[:, 1], src[:, 1]), act_ev)
                    for d in range(2):
                        pe(f"vp{d}")
                        do(A.copy(R[:, d, :, 0:RH], bank[:, d, 0:256].rearrange("p (j k) -> p j k", j=4)), act_ev)
                    for d in range(2):
                        pe(f"sq2{d}")
                        do(A.copy(jk(mats["N2T"], d), bank[:, 2 + 2 * d, :]))
                        do(A.copy(jk(mats["N2"], d), bank[:, 3 + 2 * d, :]), act_ev)
                    pe("trB")
                    do(A.copy(Bt[:].rearrange("p d b k -> p (d b k)"), bank[:, 6, :]), act_ev)
                    pe("trK")
                    do(A.copy(Kt[:].rearrange("p d b k -> p (d b k)"), bank[:, 7, :]), act_ev)
                    for d in range(2):
                        pe(f"sq4{d}")
                        do(A.copy(jk(mats["N4T"], d), bank[:, 2 * d, :]))
                        do(A.copy(jk(mats["N4"], d), bank[:, 2 * d + 1, :]), act_ev)
                    if i < GT - 1:
                        kk_root(i + 1)
                    for name, dst, b0 in (("sq8", mats["N8"], 2), ("x", R, 0), ("no", Yo, 2)):
                        for d in range(2):
                            pe(f"{name}{d}")
                            do(A.copy(jk(dst, d), bank[:, b0 + d, :]), act_ev)
                    for d in range(2):
                        act.wait_ge(dve_ev, at(DVE_EV, i, f"gh{d}"))
                        dst = H[:, ::-1, 2 * i + d, :] if d else H[:, :, 2 * i + d, :]
                        src = bank[:, 2:6, 0:256].rearrange("p q (b n) -> p b q n", b=TB)[:, :, :, RH:P]
                        do(A.copy(dst.rearrange("p (b q) k -> p b q k", b=TB), src), act_ev)
                act.wait_ge(stat_mm, 2)
                do(A.activation(sqd, bank[:, 4:6, :].rearrange("p b n -> p (b n)"), ACT.Sqrt, scale=1.0 / RH,
                                bias=c("eps_gn")), root_ready)

            @block.vector
            def _(dve):
                do = Steps(dve, dve_own)
                V = nc.vector

                def shift(dst, kind, i):
                    src = rwT[:, 4 * kind + i, :]
                    do(V.tensor_scalar(dst, src, mus[:, 4 * kind + i:4 * kind + i + 1], None, ALU.mult))
                    do(V.scalar_tensor_tensor(dst[:, 1:], src[:, :-1], col("mu", 8 * kind + i), dst[:, 1:], ALU.mult, ALU.add))
                    do(V.scalar_tensor_tensor(dst[:, :-1], src[:, 1:], col("mu", 8 * kind + 4 + i), dst[:, :-1],
                                              ALU.mult, ALU.add))

                for i in range(GT):
                    shift(zs[:, i, :], 3, i)
                do(V.tensor_scalar(keep[:], col("k_a", 0, 4), -1.0, 1.0, ALU.mult, ALU.add), z_ready)
                do(V.memset(D1[:], 0.0))
                do(V.memset(Pe[:], 1.0))
                on2 = lambda a: a.unsqueeze(1).to_broadcast([P, 2, SEQ])
                n64 = lambda a: a.rearrange("p d (n k) -> p d n k", n=4)
                n32 = lambda a: a.rearrange("p (n s) -> p n s", s=CH)
                s2 = lambda a: a.rearrange("p (b s) -> p b s", b=TB)
                jk = lambda a, d: a[:, d].rearrange("p j k -> p (j k)")

                def prepare_1(i):
                    shift(sr[:], 0, i)
                    shift(sk[:], 1, i)
                    shift(sv[:], 2, i)
                    do(V.scalar_tensor_tensor(kq[:], sk[:], col("k_k", i), sk[:], ALU.mult, ALU.mult))
                    do(V.tensor_scalar(kq[:], kq[:], col("k_k", i), None, ALU.mult), kq_ready)

                def prepare_2(i):
                    if i == 0:
                        dve.wait_ge(up_out, 21)
                    do(V.tensor_scalar(n64(kd[:]), rate(i), col("k_a", i), keep[:, i:i + 1], ALU.mult, ALU.add))
                    do(V.tensor_tensor(kd[:], kd[:], on2(sk[:]), ALU.mult))
                    dve.wait_ge(root_out, i + 1)
                    do(V.tensor_tensor(kq[:], kd[:, 0, :], kd[:, 1, :], ALU.add), wait=False)
                    do(V.reciprocal(kk[:], kk[:]))
                    do(V.scalar_tensor_tensor(kq[:], sr[:], col("r_k", i), kq[:], ALU.mult, ALU.mult), kq_ready, wait=False)
                    do(V.scalar_tensor_tensor(kk[:], sk[:], col("k_k", i), kk[:], ALU.mult, ALU.mult))
                    do(V.tensor_tensor(n64(kb[:]), rate(i), n64(on2(kk[:])), ALU.mult))

                def prepare_3(i):
                    dec = decay(i)
                    for d in range(2):
                        s0 = CH - 1 if d else 0
                        do(V.tensor_copy(D1[:, d, s0::CH], dec[:, d, s0::CH]), wait=(d == 1))
                    for d in range(2):
                        s0 = CH - 1 if d else 0
                        do(V.memset(dec[:, d, s0::CH], 0.0), wait=(d == 1))
                    for d in range(2):
                        o = slice(None, None, -1) if d else slice(None)
                        do(V.tensor_tensor_scan(Pc[:, d, o], dec[:, d, o], D1[:, d, o], 0.0, ALU.mult, ALU.add), wait=(d == 1))
                    do(V.reciprocal(IP[:], Pc[:]), wait=False)
                    do(V.tensor_copy(n32(Pe[:, 0, :])[:, :, 1:], n32(Pc[:, 0, :])[:, :, :-1]), wait=False)
                    do(V.tensor_copy(n32(Pe[:, 1, :])[:, :, :-1], n32(Pc[:, 1, :])[:, :, 1:]), wait=False)
                    do(V.tensor_copy(pend[:, 0, :], Pc[:, 0, CH - 1::CH]), wait=False)
                    do(V.tensor_copy(pend[:, 1, :], Pc[:, 1, 0::CH]))

                def prepare_4(i):
                    AR = ARs[:, i % 2]
                    for d in range(2):
                        do(V.scalar_tensor_tensor(AR[:, d, :, 0, :], s2(Pe[:, d, :]), -1.0, s2(kk[:]), ALU.mult, ALU.mult),
                           wait=False)
                        do(V.tensor_tensor(AR[:, d, :, 1, :], s2(Pc[:, d, :]), s2(sr[:]), ALU.mult), wait=False)
                    do(V.tensor_tensor(KH[:], kd[:], IP[:], ALU.mult), wait=False)
                    do(V.tensor_tensor(BH[:], kb[:], IP[:], ALU.mult), wait=False)
                    nn = lambda a: n32(flat(a[:]))
                    do(V.tensor_tensor(nn(wend), nn(IP), flat(pend[:]).unsqueeze(2).to_broadcast([P, 16, CH]), ALU.mult))
                    do(V.tensor_tensor(BTc[:], kb[:], wend[:], ALU.mult), wait=False)
                    do(V.tensor_tensor(KTc[:], kd[:], wend[:], ALU.mult), wait=False)
                    dve.wait_ge(kq_mm, 2 * i + 2)
                    do(V.tensor_tensor(bonus[:, i, :], bank[:, 7, 0:SEQ], sv[:], ALU.mult), prepared)

                for stage in (prepare_1, prepare_2, prepare_3, prepare_4):
                    stage(0)
                for i in range(GT):
                    AR = ARs[:, i % 2]
                    pe = lambda name: dve.wait_ge(pe_ev, at(PE_EV, i, name))
                    m4 = lambda m: c(m).unsqueeze(1).unsqueeze(1).to_broadcast([P, 2, TB, P])
                    eb = lambda a, d: a[:, d].rearrange("p (e b) k -> p e b k", e=2)

                    def masked(d, b0, half, dst, mask, sem=None, wait=True):
                        src = bank[:, b0:b0 + 2, 256 * 0:512].rearrange("p e (b k) -> p e b k", b=TB)
                        do(V.tensor_tensor(eb(mats[dst], d), src[:, :, :, P * half:P * half + P], m4(mask), ALU.mult), sem,
                           wait=wait)

                    for name, d, b0 in (("pa", 0, 0), ("pa", 1, 2), ("pc", 0, 4), ("pc", 1, 0)):
                        w = "UL"[d]
                        pe(f"{name}{d}")
                        if name == "pa":
                            masked(d, b0, 0, "NT", "m16" + w)
                            masked(d, b0, 0, "NTo", "mX" + w, wait=False)
                            masked(d, b0, 1, "Rb", "m32" + w + "i", dve_ev, wait=False)
                            do(V.tensor_tensor(mats["W"][:, d], mats["NT"][:, d],
                                               c("ident").unsqueeze(1).to_broadcast([P, 4, P]), ALU.add), wait=False)
                        else:
                            masked(d, b0, 0, "Aak", "m32" + w, wait=False)
                            masked(d, b0, 1, "Rk", "m32" + w + "i", dve_ev, wait=False)
                    for d in range(2):
                        pe(f"nn{d}")
                        src = bank[:, 2 + 2 * d:4 + 2 * d, 0:256].rearrange("p e (b k) -> p e b k", b=TB)
                        do(V.tensor_tensor(eb(mats["N"], d), src, m4("m16" + "LU"[d]), ALU.mult), dve_ev, wait=(d == 1))
                    for d in range(2):
                        do(V.tensor_tensor(diag[:, d], c("ident64").unsqueeze(1).to_broadcast([P, NCH, RH]),
                                           pend[:, d, :].unsqueeze(2).to_broadcast([P, NCH, RH]), ALU.mult), wait=(d == 1))

                    def grow(name):
                        for d in range(2):
                            pe(f"{name}{d}")
                            do(V.tensor_tensor(jk(mats["W"], d), bank[:, (0 if name == "w4" else 4) + d, :],
                                               jk(mats["W"], d), ALU.add), dve_ev)

                    more = i < GT - 1
                    if more:
                        prepare_1(i + 1)
                    grow("w2")
                    if more:
                        prepare_2(i + 1)
                    grow("w4")
                    if more:
                        prepare_3(i + 1)
                    grow("w8")
                    if more:
                        prepare_4(i + 1)
                    for d in range(2):
                        pe(f"z{d}")
                        do(V.tensor_tensor(jk(R, d), bank[:, 4 + d, :], jk(R, d), ALU.add), dve_ev)
                    for d in range(2):
                        pe(f"qy{d}")
                        do(V.tensor_tensor(s2(QT[:, 2 * i + d, :]), s2(bank[:, d, 0:SEQ]), AR[:, d, :, 1, :], ALU.add))
                        if d == 0:
                            do(V.tensor_copy(yin[:, i, :], bank[:, d, 256:512]), dve_ev)
                        else:
                            do(V.tensor_tensor(yin[:, i, :], bank[:, d, 256:512], yin[:, i, :], ALU.add), dve_ev)
                    for d in range(2):
                        pe(f"gh{d}")
                        dst = G[:, ::-1, 2 * i + d, :] if d else G[:, :, 2 * i + d, :]
                        src = bank[:, 2:6, 0:256].rearrange("p q (b n) -> p b q n", b=TB)[:, :, :, 0:RH]
                        do(V.tensor_tensor(dst.rearrange("p (b q) k -> p b q k", b=TB), src,
                                           diag[:, d].rearrange("p (b q) k -> p b q k", b=TB), ALU.add), dve_ev)
                do(V.memset(S[:, 0], 0.0), state_ready)
                dve.wait_ge(act_ev, at(ACT_EV, GT - 1, "gh1"))
                for n in range(NCH - 1):
                    dve.wait_ge(state_mm, n + 1)
                    do(V.tensor_tensor(S[:, (n + 1) % 2].rearrange("p q k -> p (q k)"), bank[:, 4 + n % 2, :],
                                       H[:, n].rearrange("p q k -> p (q k)"), ALU.add), state_ready)
                dve.wait_ge(state_mm, NCH)
                y2 = flat(yin[:]).rearrange("p (b n) -> p b n", b=2)
                do(V.tensor_tensor(y2, bank[:, 0:2, :], y2, ALU.add))
                do(V.tensor_tensor(y2, bank[:, 2:4, :], y2, ALU.add), y_ready)
                dve.wait_ge(stat_mm, 1)
                do(V.scalar_tensor_tensor(dlt.rearrange("p (b n) -> p b n", b=2), bank[:, 6:8, :], -1.0 / RH, y2,
                                          ALU.mult, ALU.add))
                do(V.tensor_tensor(sqd, dlt, dlt, ALU.mult), sqd_ready)
                dve.wait_ge(root_ready, 1)
                do(V.reciprocal(sqd, sqd))
                do(V.tensor_tensor(dlt, dlt, sqd, ALU.mult))
                for i in range(GT):
                    y = dlt[:, i * SEQ:i * SEQ + SEQ]
                    do(V.tensor_scalar(y, y, col("ln_w", i), col("ln_b", i), ALU.mult, ALU.add))
                do(V.tensor_tensor(dlt, dlt, flat(bonus[:]), ALU.add))
                do(V.tensor_tensor(flat(ycT[:, 12:16, :]), dlt, flat(gt[:]), ALU.mult))


def route(nc, t, layer, sem, sb, ps, c, col, x, ycT, h2, score):
    slab_in, piece_mm = [sem(f"rt_slab_in{i}") for i in range(WRING)], sem("rt_piece_mm")
    small_in, sq_ready, norm_mm, root_ready = sem("rt_small_in"), sem("rt_sq"), sem("rt_norm_mm"), sem("rt_root")
    ycn_ready, x_added, rms_ready, h2_ready, h2_mm = sem("rt_ycn"), sem("rt_x"), sem("rt_rms"), sem("rt_h2"), sem("rt_h2_mm")
    hT_ready, sk_mm, sk_out, q_out, score_mm, score_out = (sem("rt_hT"), sem("rt_sk_mm"), sem("rt_sk_out"), sem("rt_q_out"),
                                                           sem("rt_score_mm"), sem("rt_score_out"))
    dve_own, act_own = sem("rt_dve"), sem("rt_act")
    with ExitStack() as st:
        slab = sb(st, "rt_slab", [P, 2, HALF_K, GW])
        sq = sb(st, "rt_sq_b", [P, KT, SEQ])
        hT = sb(st, "rt_hT_b", [P, KT, SEQ])
        rstd = sb(st, "rt_rstd", [P, 4, SEQ])
        gain = sb(st, "rt_gain", [P, D])
        qT = sb(st, "rt_qT", [P, PEER_H, SEQ])
        sk = sb(st, "rt_sk", [P, PEER_H, 2, KEYS // 2])
        skT = sb(st, "rt_skT", [P, PEER_H, KEYS])
        ssq = sb(st, "rt_ssq", [P, 8])
        bank = ps(st, "rt_bank", [P, 8, 512])
        NS = 2
        pieces = [("w_out", n, kh) for n in range(4) for kh in range(2)] + \
                 [("peer_w_query", n, kh) for n in range(2) for kh in range(2)]

        with nc.Block() as block:
            @block.sync
            def _(sp):
                for n, (name, g, kh) in enumerate(pieces):
                    if n >= NS:
                        sp.wait_ge(piece_mm, n - NS + 1)
                    sp.dma_start(slab[:, n % NS], t[name][layer][kh * HALF_K * P:(kh + 1) * HALF_K * P, g * GW:(g + 1) * GW]
                                 .rearrange("(k p) n -> p k n", p=P)).then_inc(slab_in[n % NS], 16)
                    if n == 1:
                        sp.dma_start(sk[:], t["peer_sub_keys"][layer].rearrange("h e k d -> k h e d")).then_inc(small_in, 16)
                        sp.dma_start(gain[:], t["norm_ffn"][layer].unsqueeze(0).to_broadcast([P, D])).then_inc(small_in, 16)

            @block.tensor
            def _(pe):
                mmul, tr = nc.tensor.matmul, nc.tensor.transpose
                pe.wait_ge(sq_ready, 1)
                for g in range(4):
                    for k in range(4):
                        mm = mmul(bank[:, g // 2, g % 2 * 256:g % 2 * 256 + 256], c("ones"), sq[:, 4 * g + k, :],
                                  start=(g % 2 == 0 and k == 0), stop=(k == 3), skip_group_check=True)
                mm.then_inc(norm_mm, 1)
                pe.wait_ge(small_in, 32)
                for h in range(PEER_H):
                    mm = tr(bank[:, 6 + h // 4, h % 4 * P:h % 4 * P + P], sk[:, h].rearrange("p e d -> p (e d)"), c("ident"))
                mm.then_inc(sk_mm, 1)
                pe.wait_ge(ycn_ready, KT)
                for n in range(8):
                    g, kh = divmod(n, 2)
                    pe.wait_ge(slab_in[n % NS], 16 * (n // NS + 1))
                    if kh == 0 and g >= 2:
                        pe.wait_ge(x_added, 2 * (g - 1))
                    for b in range(TB):
                        for k in range(HALF_K):
                            mm = mmul(bank[:, 2 + 2 * (g % 2) + b, :], sq[:, kh * HALF_K + k, b * P:b * P + P],
                                      slab[:, n % NS, k, :], start=(kh == 0 and k == 0), stop=(kh == 1 and k == 7),
                                      skip_group_check=True)
                    mm.then_inc(piece_mm, 1)
                pe.wait_ge(sk_out, 2)
                pe.wait_ge(x_added, 8)
                for b in range(TB):
                    pe.wait_ge(h2_ready, b + 1)
                    for k in range(KT):
                        mm = tr(bank[:, 4 * b + k // 4, k % 4 * P:k % 4 * P + P], h2[:, b, k * P:k * P + P], c("ident"))
                        if k % 4 == 3:
                            mm.then_inc(h2_mm, 1)
                pe.wait_ge(hT_ready, 8)
                for n in range(8, 12):
                    g, kh = divmod(n - 8, 2)
                    pe.wait_ge(slab_in[n % NS], 16 * (n // NS + 1))
                    for m in range(4):
                        for k in range(HALF_K):
                            mm = mmul(bank[:, 2 * g + m // 2, m % 2 * SEQ:m % 2 * SEQ + SEQ], slab[:, n % NS, k, m * P:m * P + P],
                                      hT[:, kh * HALF_K + k, :], start=(kh == 0 and k == 0 and m % 2 == 0),
                                      stop=(kh == 1 and k == 7), skip_group_check=True)
                    mm.then_inc(piece_mm, 1)
                pe.wait_ge(q_out, 4)
                for b in range(TB):
                    for e in range(2):
                        for hg in range(2):
                            for h in range(4 * hg, 4 * hg + 4):
                                r = slice(64 * e, 64 * e + 64)
                                mm = mmul(bank[:, 4 * b + 2 * e + hg, h % 4 * P:h % 4 * P + P], qT[r, h, b * P:b * P + P],
                                          skT[r, h, :], start=(h % 4 == 0), stop=True, skip_group_check=True)
                            mm.then_inc(score_mm, 1)

            @block.scalar
            def _(act):
                do = Steps(act, act_own)
                A = nc.scalar
                act.wait_ge(norm_mm, 1)
                do(A.activation(rstd[:].rearrange("p g s -> p (g s)"), bank[:, 0:2, :].rearrange("p b n -> p (b n)"), ACT.Sqrt,
                                scale=1.0 / GW, bias=c("eps")), root_ready)
                act.wait_ge(sk_mm, 1)
                for g in range(2):
                    do(A.copy(skT[:, 4 * g:4 * g + 4].rearrange("p h k -> p (h k)"), bank[:, 6 + g, :]), sk_out)
                act.wait_ge(x_added, 8)
                for b in range(TB):
                    do(A.activation(sq[:, 0:8].rearrange("p k s -> p (k s)"), x[:, b, :], ACT.Square,
                                    accum_out=ssq[:, b:b + 1]))
                    do(A.activation(ssq[:, 2 + b:3 + b], ssq[:, b:b + 1], ACT.Sqrt, scale=1.0 / D, bias=c("eps")), rms_ready)
                for u in range(4):
                    act.wait_ge(piece_mm, 8 + 2 * (u // 2) + 2)
                    do(A.copy(qT[:, 2 * u:2 * u + 2].rearrange("p m s -> p (m s)"), bank[:, u, :]), q_out)
                for b in range(TB):
                    for e in range(2):
                        for hg in range(2):
                            u = 4 * b + 2 * e + hg
                            act.wait_ge(score_mm, u + 1)
                            h = PEER_H * b + 4 * hg
                            do(A.copy(score[:, h:h + 4, e, :], bank[:, u, :].rearrange("p (h k) -> p h k", h=4)), score_out)

            @block.vector
            def _(dve):
                do = Steps(dve, dve_own)
                V = nc.vector
                do(V.tensor_tensor(sq[:], ycT[:], ycT[:], ALU.mult), sq_ready)
                do(V.memset(score[:, TB * PEER_H], 0.0))
                dve.wait_ge(root_ready, 1)
                do(V.reciprocal(rstd[:], rstd[:]))
                for k in range(KT):
                    do(V.scalar_tensor_tensor(sq[:, k, :], ycT[:, k, :], col("branch", k), rstd[:, k // 4, :],
                                              ALU.mult, ALU.mult), ycn_ready)
                for g in range(4):
                    dve.wait_ge(piece_mm, 2 * g + 2)
                    for b in range(TB):
                        xs = x[:, b, g * GW:(g + 1) * GW]
                        do(V.tensor_tensor(xs, bank[:, 2 + 2 * (g % 2) + b, :], xs, ALU.add), x_added)
                for b in range(TB):
                    dve.wait_ge(rms_ready, b + 1)
                    do(V.reciprocal(ssq[:, 4 + b:5 + b], ssq[:, 2 + b:3 + b]))
                    do(V.tensor_scalar(h2[:, b, :], x[:, b, :], ssq[:, 4 + b:5 + b], None, ALU.mult), h2_ready)
                for b in range(TB):
                    for q in range(4):
                        dve.wait_ge(h2_mm, 4 * b + q + 1)
                        do(V.tensor_tensor(hT[:, 4 * q:4 * q + 4, b * P:b * P + P],
                                           bank[:, 4 * b + q, :].rearrange("p (k s) -> p k s", k=4),
                                           col("norm_ffn", 4 * q, 4).unsqueeze(2).to_broadcast([P, 4, P]), ALU.mult), hT_ready)
                dve.wait_ge(small_in, 32)
                for b in range(TB):
                    do(V.tensor_tensor(h2[:, b, :], h2[:, b, :], gain[:], ALU.mult))


def experts(nc, t, layer, sem, sb, c, row_in, x, h2, score, layer_base):
    place_free, place_taken, dots_ready, gelu_ready, weight_ready, rows_ready, best_ready, exp_ready, top = [
        sem("ex_" + n) for n in ("place_free", "place_taken", "dots", "gelu", "weight", "rows", "best", "exp", "top")]
    with ExitStack() as st:
        ring = sb(st, "ex_ring", [P, RING, D])
        rows = sb(st, "ex_rows_b", [P, 2, TOPK], U32)
        dot = sb(st, "ex_dot", [P, 2, TOPK])
        gelu = sb(st, "ex_gelu_b", [P, 2, TOPK])
        gate = sb(st, "ex_gate", [P, 2, TOPK])
        total = sb(st, "ex_total", [P, 2, 2])
        weight = sb(st, "ex_weight_b", [P, 2, TOPK])
        keys = sb(st, "ex_keys", [P, 2, KEYS])
        left = sb(st, "ex_left", [P, 256])
        top_v = sb(st, "ex_top_v", [P, 2, TOPK])
        top_i = sb(st, "ex_top_i", [P, 2, TOPK], U32)
        top_f = sb(st, "ex_top_f", [P, 2, TOPK])
        cand = sb(st, "ex_cand", [P, TOPK, TOPK])
        best = sb(st, "ex_best_b", [P, 2, TOPK])
        pos = sb(st, "ex_pos", [P, TOPK], U32)
        half_u = sb(st, "ex_half_u", [P, 2, TOPK], U32)
        half_f = sb(st, "ex_half_f", [P, 2, TOPK])
        hot = sb(st, "ex_hot", [P, 2, TOPK, TOPK])
        pick = sb(st, "ex_pick", [P, 2, TOPK])
        tables = [t[n].rearrange("l e d -> (l e) d") for n in ("peer_u", "peer_v")]
        PER = 2 * TOPK
        laps = PER // RING

        with nc.Block() as block:
            @block.gpsimd
            def _(pool):
                pool.sem_inc(place_free, RING)
                for b in range(TB):
                    with pool.Fori(0, PEER_H // 2) as pair:
                        for e in range(2):
                            head = pair * 2 + (b * PEER_H + e)
                            pool.wait_ge(rows_ready, head + 1)
                            for s in range(PER):
                                pool.wait_ge(place_free, head * PER + s + 1)
                                pool.sem_inc(place_taken, 1)
                                nc.gpsimd.indirect_dma_start(
                                    out=ring[:, s % RING, :], out_offset=None, in_=tables[s // TOPK][:, :],
                                    in_offset=bass.IndirectOffsetOnAxis(ap=rows[:, e, s % TOPK:s % TOPK + 1], axis=0))\
                                    .then_inc(row_in[s % RING], 16)

            @block.scalar
            def _(act):
                def gates(e, head):
                    act.wait_ge(best_ready, head + 1)
                    nc.scalar.activation(gate[:, e, :], best[:, e, :], ACT.Exp, accum_out=total[:, e, 0:1])\
                        .then_inc(exp_ready, 1)

                gates(0, 0)
                for b in range(TB):
                    with act.Fori(0, PEER_H // 2) as pair:
                        for e in range(2):
                            head = pair * 2 + (b * PEER_H + e)
                            act.wait_ge(dots_ready, head + 1)
                            nc.scalar.activation(gelu[:, e, :], dot[:, e, :], ACT.Gelu).then_inc(gelu_ready, 1)
                            gates(1 - e, head + 1)

            @block.vector
            def _(dve):
                V = nc.vector

                def find(e, head):
                    dve.sem_clear(top)
                    do = Steps(dve, top)

                    def top16(values, out_v, out_i):
                        rest = left[:, 0:values.shape[-1]]
                        do(V.max(out_v[:, 0:8], values))
                        do(V.max_index(out_i[:, 0:8], out_v[:, 0:8], values), wait=False)
                        do(V.match_replace(rest, out_v[:, 0:8], values, -3.0e38))
                        do(V.max(out_v[:, 8:16], rest))
                        do(V.max_index(out_i[:, 8:16], out_v[:, 8:16], rest))

                    src = score[:, head] if isinstance(head, int) else score[:, bass.ds(head, 1)]
                    do(V.tensor_copy(keys[:].rearrange("p e k -> p (e k)"),
                                     src.rearrange("p e k -> p (e k)" if isinstance(head, int) else "p h e k -> p (h e k)")))
                    for i in range(2):
                        top16(keys[:, i, :], top_v[:, i, :], top_i[:, i, :])
                    do(V.tensor_copy(top_f[:], top_i[:]), wait=False)
                    two = [P, TOPK, TOPK]
                    do(V.tensor_tensor(cand[:], top_v[:, 0].unsqueeze(2).to_broadcast(two),
                                       top_v[:, 1].unsqueeze(1).to_broadcast(two), ALU.add))
                    raw = pick[:, 0]
                    top16(cand[:].rearrange("p i j -> p (i j)"), raw, pos[:])
                    do(V.tensor_tensor(best[:, e], raw, raw[:, 0:1].to_broadcast([P, TOPK]), ALU.subtract), best_ready,
                       wait=False)
                    do(V.tensor_scalar(half_u[:, 0], pos[:], 4, None, ALU.logical_shift_right), wait=False)
                    do(V.tensor_scalar(half_u[:, 1], pos[:], 15, None, ALU.bitwise_and))
                    do(V.tensor_copy(half_f[:], half_u[:]))
                    three = [P, 2, TOPK, TOPK]
                    do(V.tensor_tensor(hot[:], half_f[:].unsqueeze(3).to_broadcast(three),
                                       c("iota16").unsqueeze(1).unsqueeze(1).to_broadcast(three), ALU.is_equal))
                    do(V.tensor_tensor(hot[:], hot[:], top_f[:].unsqueeze(2).to_broadcast(three), ALU.mult))
                    do(V.tensor_reduce(pick[:], hot[:], AX.X, ALU.add))
                    do(V.scalar_tensor_tensor(pick[:, 0], pick[:, 0], float(KEYS), pick[:, 1], ALU.mult, ALU.add))
                    do(V.tensor_scalar(rows[:, e], pick[:, 0], layer_base[:], None, ALU.add), rows_ready, wait=False)

                find(0, 0)
                for b in range(TB):
                    with dve.Fori(0, PEER_H // 2) as pair:
                        for e in range(2):
                            head = pair * 2 + (b * PEER_H + e)
                            arrived = (layer * (TB * PEER_H) + head) * (16 * laps)
                            for s in range(TOPK):
                                dve.wait_ge(row_in[s % RING], arrived + 16 * (s // RING + 1))
                                V.tensor_tensor_reduce(out=ring[:, s % RING, :], in0=ring[:, s % RING, :], in1=h2[:, b, :],
                                                       scale=1.0, scalar=0.0, op0=ALU.mult, op1=ALU.add,
                                                       accum_out=dot[:, e, s:s + 1]).then_inc(place_free, 1)
                            dve.wait_ge(place_free, head * PER + TOPK + RING)
                            dve.sem_inc(dots_ready, 1)
                            find(1 - e, head + 1)
                            dve.wait_ge(exp_ready, head + 1)
                            V.reciprocal(total[:, e, 1:2], total[:, e, 0:1]).then_inc(weight_ready, 1)
                            dve.wait_ge(weight_ready, head * 2 + 1)
                            dve.wait_ge(gelu_ready, head + 1)
                            V.scalar_tensor_tensor(weight[:, e, :], gate[:, e, :], total[:, e, 1:2], gelu[:, e, :],
                                                   ALU.mult, ALU.mult).then_inc(weight_ready, 1)
                            dve.wait_ge(weight_ready, head * 2 + 2)
                            for s in range(TOPK, PER):
                                dve.wait_ge(row_in[s % RING], arrived + 16 * (s // RING + 1))
                                dve.wait_ge(place_free, head * PER + s + RING)
                                V.scalar_tensor_tensor(x[:, b, :], ring[:, s % RING, :],
                                                       weight[:, e, s - TOPK:s - TOPK + 1], x[:, b, :], ALU.mult, ALU.add)\
                                    .then_inc(place_free, 1)
                V.tensor_scalar(layer_base[:], layer_base[:], float(EXPERTS), None, ALU.add).then_inc(weight_ready, 1)


_INS = ["x", "norm_mix", "w_in", "fourier_w", "s5_lam_re", "s5_lam_im", "s5_log_step", "s5_b_re", "s5_b_im", "s5_c_re",
        "s5_c_im", "s5_d", "s5_w_glu", "attn_q_norm", "attn_k_norm", "rwkv_mu", "rwkv_w0", "rwkv_w1", "rwkv_w2", "rwkv_a0",
        "rwkv_a1", "rwkv_a2", "rwkv_g1", "rwkv_g2", "rwkv_k_k", "rwkv_k_a", "rwkv_r_k", "rwkv_ln_w", "rwkv_ln_b",
        "branch_norm", "w_out", "norm_ffn", "peer_w_query", "peer_sub_keys", "peer_u", "peer_v"]


def kernel(**inputs):
    import concourse.bacc as bacc
    from concourse.bass_utils import run_bass_kernel_spmd

    nc = bacc.Bacc("TRN2", target_bir_lowering=False, num_devices=1)
    arrays = {f"in_{n}": np.ascontiguousarray(inputs[n]) for n in _INS}
    arrays["in_consts"] = constants()[0]
    t = {n[3:]: nc.dram_tensor(n, a.shape, mybir.dt.from_np(a.dtype), kind="ExternalInput").ap() for n, a in arrays.items()}
    out = nc.dram_tensor("out_x", (1, SEQ, D), F32, kind="ExternalOutput").ap()
    build(nc, t, out)
    r = run_bass_kernel_spmd(nc, [arrays], core_ids=[0])
    return r.results[0]["out_x"]
```

```python
import math
from contextlib import ExitStack

import numpy as np

import concourse.bass as bass
from concourse import mybir

P = 128
F32 = mybir.dt.float32
U32 = mybir.dt.uint32
ALU = mybir.AluOpType
ACT = mybir.ActivationFunctionType
AX = mybir.AxisListType

DEPTH, SEQ, D = 2, 256, 2048
TB = SEQ // P
KT = D // P
GW = 512
GT = GW // P
PROJ = 4096
PT = PROJ // P
NORM_EPS = 1e-6
HEAD = 128
SCALE = HEAD ** -0.5
S5P, S5C, S5G = 64, 16, 32
CH = 32
NCH = SEQ // CH
CPB = P // CH
RH = 64
PEER_H, KEYS, TOPK = 8, 128, 16
EXPERTS = KEYS * KEYS
RING = 8
HALF_K = 8
WRING = 3

T_A, T_B, T_Q, T_K, T_V, T_R, T_RK, T_RV, T_RZ = 0, 4, 8, 12, 14, 16, 20, 24, 28

ROWS = {}
for _name, _n in (("norm_mix", 16), ("norm_ffn", 16), ("mu", 32), ("w0", 8), ("a0", 8), ("k_k", 4), ("k_a", 4),
                  ("r_k", 4), ("ln_w", 4), ("ln_b", 4), ("branch", 16), ("s5_d", 4), ("q_norm", 1), ("k_norm", 1)):
    ROWS[_name] = (sum(n for _, n in ROWS.values()), _n)
NROWS = sum(n for _, n in ROWS.values())
assert NROWS <= P


def constants():
    p = np.arange(P)[:, None]
    q = np.arange(P)[None, :]
    parts = {"ident": p == q, "ones": np.ones((P, P)), "heads": p // RH == q // RH}
    half = HEAD // 2
    parts["rot"] = np.where(p == q + half, -1.0, 0.0) + np.where(p == q - half, 1.0, 0.0)
    t = np.arange(SEQ)
    inv = 10000.0 ** (-np.arange(0, half, 2, dtype=np.float32) / half)
    ang = np.concatenate([(t // 64)[:, None] * inv, (t % 64)[:, None] * inv], axis=-1).astype(np.float32)
    parts["cos"] = np.tile(np.cos(ang).T, (2, 1))
    parts["sin"] = np.tile(np.sin(ang).T, (2, 1))
    ch = 2 * np.pi * p * q / P
    s = 1 / math.sqrt(SEQ * P)
    parts["dft_ch"] = np.concatenate([np.cos(ch), np.sin(ch)], 1) * s
    sq = np.concatenate([2 * np.pi * (p + b * P) * t[None, :] / SEQ for b in range(TB)], 1).reshape(P, TB, SEQ)
    parts["dft_seq"] = np.concatenate([np.cos(sq), -np.sin(sq)], 2).reshape(P, TB * 2 * SEQ)
    s16, s32 = p // 16 == q // 16, p // CH == q // CH
    parts["m16U"], parts["m16L"] = s16 & (q > p), s16 & (q < p)
    parts["mXU"], parts["mXL"] = s32 & ~s16 & (q > p), s32 & ~s16 & (q < p)
    parts["m32U"], parts["m32L"] = s32 & (q > p), s32 & (q < p)
    parts["m32Ui"], parts["m32Li"] = s32 & (q >= p), s32 & (q <= p)
    parts["ident64"] = (p % RH) == np.arange(RH)[None, :]
    parts["iota16"] = np.tile(np.arange(16)[None, :], (P, 1))
    parts["even"] = (p // S5C) % 2 == 0
    parts["odd"] = (p // S5C) % 2 == 1
    parts["eps"] = np.full((P, 1), NORM_EPS)
    parts["eps_kk"] = np.full((P, 1), 1e-12)
    parts["eps_gn"] = np.full((P, 1), 64e-5)
    where, at = {}, 0
    for k, v in parts.items():
        where[k] = (at, at + v.shape[1])
        at += v.shape[1]
    return np.concatenate([np.asarray(v, np.float64) for v in parts.values()], 1).astype(np.float32), where


class Steps:

    def __init__(self, engine, own):
        self.engine, self.own, self.count = engine, own, {}

    def __call__(self, instruction, sem=None, wait=True):
        sem = self.own if sem is None else sem
        instruction.then_inc(sem, 1)
        self.count[sem.name] = self.count.get(sem.name, 0) + 1
        if wait:
            self.engine.wait_ge(sem, self.count[sem.name])


def build(nc, t, out):
    _, where = constants()
    whole = ExitStack()
    with whole:
        first_sem = []

        def sem(name):
            s = whole.enter_context(nc.semaphore(name))
            first_sem.append(s)
            return s

        def sb(stack, name, shape, dt=F32):
            return stack.enter_context(nc.sbuf_tensor(name, shape, dt))

        def ps(stack, name, shape, dt=F32):
            return stack.enter_context(nc.psum_tensor(name, shape, dt))

        x = sb(whole, "x", [P, TB, D])
        consts = sb(whole, "consts", [P, where["eps_gn"][1]])
        pcol = sb(whole, "pcol", [P, NROWS])
        mus = sb(whole, "mus", [P, 16])
        layer_base = sb(whole, "layer_base", [P, 1])

        def c(name, a=None, b=None):
            lo, hi = where[name]
            return consts[:, lo if a is None else lo + a:hi if b is None else lo + b]

        def col(name, i=0, n=1):
            at = ROWS[name][0] + i
            return pcol[:, at:at + n]

        loaded, base_set, stored = sem("loaded"), sem("base_set"), sem("stored")
        with nc.Block() as block:
            @block.sync
            def _(sp):
                sp.dma_start(consts[:], t["consts"]).then_inc(loaded, 16)
                sp.dma_start(x[:], t["x"][0].rearrange("(b p) d -> p b d", p=P)).then_inc(loaded, 16)
                sp.wait_ge(loaded, 32)

            @block.vector
            def _(dve):
                dve.memset(layer_base[:], 0.0).then_inc(base_set, 1)
                dve.wait_ge(base_set, 1)

        row_in = [sem(f"row_in{i}") for i in range(RING)]
        kept = len(first_sem)
        with nc.Fori(0, DEPTH) as layer:
            rw = ExitStack()
            ycT = sb(rw, "ycT", [P, 16, SEQ])
            rwT = sb(rw, "rwT", [P, 16, SEQ])
            mix = ExitStack()
            mixT = sb(mix, "mixT", [P, 16, SEQ])
            mixers(nc, t, layer, sem, sb, ps, c, col, x, pcol, mus, mixT, rwT, ycT)
            mix.close()
            arena = sb(rw, "arena", [P, 9 * 1024])
            bank = ps(rw, "bank", [P, 8, 512])
            out_w = {"place": arena[:, 0:8192].rearrange("p (i k n) -> p i k n", i=2, k=HALF_K),
                     "in": [sem(f"out_w_in{i}") for i in range(2)], "used": sem("out_w_used")}
            rwkv(nc, t, layer, sem, sb, bank, c, col, mus, rwT, ycT, arena, out_w)
            route_kept = ExitStack()
            h2 = rwT[:].rearrange("p k s -> p (k s)").rearrange("p (b d) -> p b d", b=TB)
            score = sb(route_kept, "score", [P, TB * PEER_H, 2, KEYS])
            query = {"w": sb(route_kept, "query_w", [P, WRING, KT, P]), "skT": sb(route_kept, "skT", [P, PEER_H, KEYS]),
                     "gain": sb(route_kept, "gain", [P, D]), "rms": sb(route_kept, "rms", [P, 3, TB]), "w_in": [sem(f"query_in{i}") for i in range(WRING)]}
            hT = [ycT[:, 0:4], ycT[:, 4:8], arena[:, 8192:9216].rearrange("p (k s) -> p k s", k=4), ycT[:, 12:16]]
            route(nc, t, layer, sem, sb, bank, c, col, x, ycT, hT, score, query, out_w)
            experts(nc, t, layer, sem, sb, bank, c, row_in, x, hT, h2, score, query, layer_base, arena)
            route_kept.close()
            rw.close()
            with nc.Block() as block:
                @block.sync
                def _(sp):
                    for s in first_sem[kept:]:
                        sp.sem_clear(s)

        with nc.Block() as block:
            @block.sync
            def _(sp):
                sp.dma_start(out[0].rearrange("(b p) d -> p b d", p=P), x[:]).then_inc(stored, 16)
                sp.wait_ge(stored, 16)


PW = 256
PIECES = [T_B // 2, T_B // 2 + 1] + list(range(T_B // 2)) + list(range(T_B // 2 + 2, T_R // 2)) \
    + [T_RZ // 2, T_RZ // 2 + 1] + list(range(T_R // 2, T_RZ // 2))
PARTS = 4
PARTS_BEFORE = 12
PARTS_BATCH = 5
EL = 16


def mixers(nc, t, layer, sem, sb, ps, c, col, x, pcol, mus, mixT, rwT, ycT):
    rows_in, piece_in = sem("pj_rows_in"), [sem(f"pj_piece_in{i}") for i in range(2)]
    rows_T, cols_ready = sem("pj_rows_T"), sem("pj_cols_ready")
    h_ready, hT_mm, hT_ready = sem("pj_h_ready"), sem("pj_hT_mm"), sem("pj_hT_ready")
    rms_ready, piece_mm, piece_out = sem("pj_rms"), sem("pj_mm"), sem("pj_out")
    ls_ready, s5_act, s5_arg, pool_own = sem("pj_ls_ready"), sem("pj_s5_act"), sem("pj_s5_arg"), sem("pj_pool")
    dve_own, act_own = sem("pj_dve"), sem("pj_act")
    raw_in, wglu_in, exp_ready, turn_mm, turn_out = [sem("s5_" + n) for n in ("raw_in", "wglu_in", "exp", "turn_mm",
                                                                             "turn_out")]
    table_ready, bu_mm, bu_used, x_ready, y_mm = [sem("s5_" + n) for n in ("table", "bu_mm", "bu_used", "x", "y_mm")]
    c_ready, pre_ready, gelu_ready, glu_mm, glu_out = [sem("s5_" + n) for n in ("c", "pre", "gelu", "glu_mm", "glu_out")]
    w_four_in, unit_mm, unit_out, sq_ready = sem("at_w_in"), sem("at_mm"), sem("at_out"), sem("at_sq")
    qn_ready, rope_ready, max_ready, exps_ready, prob_ready = [sem("at_" + n) for n in ("qn", "rope", "max", "exp", "prob")]
    with ExitStack() as st:
        rows = sb(st, "pj_rows", [P, P])
        srow = sb(st, "pj_srow", [96, P])
        ls2 = sb(st, "pj_ls2", [96, 2])
        h = sb(st, "pj_h", [P, D])
        wglu = h[:].rearrange("p (k n) -> p k n", k=GT)
        hT = sb(st, "pj_hT", [P, KT, SEQ])
        piece = sb(st, "pj_piece", [P, 2, KT, PW])
        ssq = sb(st, "pj_ssq", [P, 8])
        v = sb(st, "s5_v", [P, 24, 32])
        work = sb(st, "s5_work", [P, 6, 1024])
        BT = sb(st, "s5_BT", [P, 2, 8, P])
        CT = sb(st, "s5_CT", [P, 2, 8, P])
        table = sb(st, "s5_table", [P, 2, 2, 1024])
        tmp = sb(st, "s5_tmp", [P, 1024])
        factor = sb(st, "s5_factor", [P, 2, 2, 32, EL])
        raw = table[:, 1].rearrange("p a (b n) -> p (a b) n", b=2)
        y = ycT[:, 4:8, :]
        bank = ps(st, "pj_bank", [P, 8, 512])
        bu, yb, turn_bank, pj_bank = bank[:, 0:4, :], bank[:, 4, :], bank[:, 5, :], bank[:, 6:8, :]
        bexp = [work[:, i].rearrange("p (q n) -> p q n", q=32) for i in range(2)]
        cexp = [work[:, 2 + i].rearrange("p (q n) -> p q n", q=8) for i in range(2)]
        order = [(ct, d) for ct in range(GT) for d in range(2)]
        pieces_at = lambda i: (PARTS_BEFORE + PARTS_BATCH * i) // PARTS
        left = pieces_at(8)
        assert PARTS * left == PARTS_BEFORE + PARTS_BATCH * 8 and left == len(PIECES) - 3
        flat = lambda a: a.rearrange("p h n -> p (h n)")
        arena = table[:].rearrange("p b a n -> p (b a n)")
        Z = arena[:, 0:2048].rearrange("p (h b n) -> p h b n", h=4, b=TB)
        S = arena[:, 0:2048].rearrange("p (h b n) -> p h b n", h=4, b=TB)
        fT = arena[:, 2048:3072].rearrange("p (h n) -> p h n", h=4)
        PT_ = arena[:, 2048:4096].rearrange("p (h k n) -> p h k n", h=4, k=TB)
        space = flat(work[:])
        qk, qb, qa = [space[:, o:o + 1536].rearrange("p (h n) -> p h n", h=6) for o in (0, 2048, 3584)]
        vt = space[:, 5120:5632].rearrange("p (b g n) -> p b g n", b=TB, g=2)
        st8 = space[:, 5632:5664].rearrange("p (a n) -> p a n", a=4)
        wf = BT[:].rearrange("p a q n -> p (a q n)").rearrange("p (k n) -> p k n", k=GT)
        Pr = CT[:].rearrange("p a q n -> p (a q n)").rearrange("p (h b n) -> p h b n", h=4, b=TB)
        sig = tmp[:]
        ROW_SRC = [("norm_mix", t["norm_mix"]), ("norm_ffn", t["norm_ffn"]), ("mu", t["rwkv_mu"]), ("w0", t["rwkv_w0"]),
                   ("a0", t["rwkv_a0"]), ("k_k", t["rwkv_k_k"]), ("k_a", t["rwkv_k_a"]), ("r_k", t["rwkv_r_k"]),
                   ("ln_w", t["rwkv_ln_w"]), ("ln_b", t["rwkv_ln_b"]), ("branch", t["branch_norm"]),
                   ("s5_d", t["s5_d"]), ("q_norm", t["attn_q_norm"]), ("k_norm", t["attn_k_norm"])]

        with nc.Block() as block:
            def rows_load(engine, which):
                for name, src in which:
                    a, n = ROWS[name]
                    r = src[layer]
                    r = {1: lambda r: r, 2: lambda r: r.rearrange("a b -> (a b)"),
                         3: lambda r: r.rearrange("a b c -> (a b c)")}[len(r.shape)](r)
                    engine.dma_start(rows[a:a + n, :], r.rearrange("(n p) -> n p", p=P)).then_inc(rows_in, 16)

            @block.sync
            def _(sp):
                rows_load(sp, ROW_SRC)
                for i, name in enumerate(("s5_lam_re", "s5_lam_im")):
                    sp.dma_start(srow[32 * i:32 * i + 32, :],
                                 t[name][layer].rearrange("d (g e) p -> (d g) (e p)", e=2)).then_inc(rows_in, 16)
                sp.dma_start(ls2[64:96, :], t["s5_log_step"][layer].rearrange("d (g e) -> (d g) e", e=2))\
                    .then_inc(rows_in, 16)
                for n, u in enumerate(PIECES):
                    if n == 2:
                        for i, name in enumerate(("s5_b_re", "s5_b_im")):
                            sp.dma_start(raw[:, i].rearrange("p (q h) -> p q h", q=32),
                                         t[name][layer].rearrange("d (g e) p h -> (e p) (d g) h", e=2)).then_inc(raw_in, 16)
                        for i, name in enumerate(("s5_c_re", "s5_c_im")):
                            sp.dma_start(raw[:, 2 + i].rearrange("p (q n) -> p q n", q=8),
                                         t[name][layer].rearrange("d (q g) h p -> (g h) (d q) p", q=GT)).then_inc(raw_in, 16)
                        sp.wait_ge(hT_mm, 8)
                        sp.dma_start(wglu, t["s5_w_glu"][layer].rearrange("(k p) n -> p k n", p=P)).then_inc(wglu_in, 16)
                    if n >= 2:
                        sp.wait_ge(piece_mm, n - 1)
                    sp.dma_start(piece[:, n % 2], t["w_in"][layer][:, u * PW:(u + 1) * PW]
                                 .rearrange("(k p) n -> p k n", p=P)).then_inc(piece_in[n % 2], 16)
                    if n == left + 1:
                        sp.wait_ge(bu_mm, 8)
                        sp.dma_start(wf, t["fourier_w"][layer].rearrange("(k p) n -> p k n", p=P)).then_inc(w_four_in, 16)

            @block.tensor
            def _(pe):
                mmul, tr = nc.tensor.matmul, nc.tensor.transpose
                for b in range(TB):
                    if b == 1:
                        pe.wait_ge(rows_in, 17 * 16)
                        tr(bank[:, 7, 0:NROWS], rows[0:NROWS, :], c("ident")[0:NROWS, 0:NROWS])
                        pe.wait_ge(ls_ready, 1)
                        tr(bank[:, 7, 256:352], srow[:, :], c("ident")[0:96, 0:96]).then_inc(rows_T, 1)
                    pe.wait_ge(h_ready, b + 1)
                    for k in range(KT):
                        if b == 1 and k == 12:
                            pe.wait_ge(cols_ready, 2)
                        mm = tr(bank[:, 4 * b + k // 4, k % 4 * P:k % 4 * P + P], h[:, k * P:k * P + P], c("ident"))
                        if k % 4 == 3:
                            mm.then_inc(hT_mm, 1)
                pe.wait_ge(hT_ready, 8)

                def parts(first, count):
                    for part in range(first, min(first + count, PARTS * len(PIECES))):
                        n, r = divmod(part, PARTS)
                        m, kh = divmod(r, 2)
                        if r == 0:
                            pe.wait_ge(piece_in[n % 2], 16 * (n // 2 + 1))
                            if n >= 2:
                                pe.wait_ge(piece_out, n - 1)
                        for k in range(8 * kh, 8 * kh + 8):
                            mm = mmul(pj_bank[:, n % 2, m * SEQ:m * SEQ + SEQ], piece[:, n % 2, k, m * P:m * P + P],
                                      hT[:, k, :], start=(m == 0 and k == 0), stop=(k == KT - 1), skip_group_check=True)
                        if r == PARTS - 1:
                            mm.then_inc(piece_mm, 1)

                parts(0, 4)
                pe.wait_ge(raw_in, 64)
                pe.wait_ge(exp_ready, 8)
                for u in range(8):
                    which, part, d = u // 4, u // 2 % 2, u % 2
                    if u:
                        pe.wait_ge(turn_out, u)
                    for q in range(4):
                        j = d * 4 + q
                        src = bexp[part][:, 4 * j:4 * j + 4, :].rearrange("p a b -> p (a b)") if which == 0 \
                            else cexp[part][:, j, :]
                        mm = tr(turn_bank[:, q * P:q * P + P], src, c("ident"))
                    mm.then_inc(turn_mm, 1)
                    parts(4 + u, 1)
                pe.wait_ge(piece_out, 2)
                pe.wait_ge(turn_out, 8)
                for i in range(len(order) + 1):
                    if i < len(order):
                        ct, d = order[i]
                        if i:
                            pe.wait_ge(bu_used, i)
                        for j in range(4):
                            for part in range(2):
                                mm = mmul(bu[:, j, part * SEQ:part * SEQ + SEQ], BT[32 * j:32 * j + 32, part, d * 4 + ct, :],
                                          mixT[32 * j:32 * j + 32, T_B + ct, :], start=(part == 0), stop=True,
                                          skip_group_check=True)
                        mm.then_inc(bu_mm, 1)
                    if i:
                        ct, d = order[i - 1]
                        pe.wait_ge(x_ready, i)
                        pe.wait_ge(c_ready, 1)
                        if ct and d == 0:
                            pe.wait_ge(pre_ready, ct)
                        for j in range(4):
                            for part in range(2):
                                mm = mmul(yb[32 * j:32 * j + 32, 0:SEQ], CT[:, part, d * 4 + ct, 32 * j:32 * j + 32],
                                          work[:, part, j * SEQ:j * SEQ + SEQ], start=(d == 0 and part == 0),
                                          stop=(d == 1 and part == 1), skip_group_check=True)
                        mm.then_inc(y_mm, 1)
                    if i < len(order):
                        parts(PARTS_BEFORE + PARTS_BATCH * i, PARTS_BATCH)

                unit = [0]

                def begin():
                    if unit[0] >= 4:
                        pe.wait_ge(unit_out, unit[0] - 3)
                    return bank[:, unit[0] % 4, :]

                def end(mm):
                    mm.then_inc(unit_mm, 1)
                    unit[0] += 1

                pe.wait_ge(sq_ready, 1)
                for g in range(3):
                    o = begin()
                    end(mmul(o, c("ones"), flat(qb)[:, g * 512:g * 512 + 512], start=True, stop=True))
                for h_ in range(4):
                    o = begin()
                    for b in range(TB):
                        mm = mmul(o[:, b * 256:b * 256 + 256], mixT[:, T_A + h_, b * P:b * P + P], c("dft_ch"),
                                  start=(b == 0), stop=True, skip_group_check=True)
                    end(mm)
                parts(PARTS * left, PARTS)
                pe.wait_ge(qn_ready, 1)
                for g in range(3):
                    o = begin()
                    end(mmul(o, c("rot"), flat(qk)[:, g * 512:g * 512 + 512], start=True, stop=True))
                o = begin()
                for g in range(2):
                    for b in range(TB):
                        at = (b * 2 + g) * P
                        mm = tr(o[:, at:at + P], mixT[:, T_V + g, b * P:b * P + P], c("ident"))
                end(mm)
                pe.wait_ge(unit_out, 7)
                for hp in range(2):
                    o = begin()
                    for e in range(2):
                        for b in range(TB):
                            for part in range(2):
                                at = (b * 2 + part) * SEQ
                                mm = mmul(o[:, e * 256:e * 256 + 256], Z[:, 2 * hp + e, b, part * P:part * P + P],
                                          c("dft_seq", at, at + SEQ), start=(e == 0 and b == 0 and part == 0),
                                          stop=(b == 1 and part == 1), skip_group_check=True)
                    end(mm)
                pe.wait_ge(rope_ready, 1)
                for h_ in range(4):
                    o = begin()
                    for b in range(TB):
                        mm = mmul(o[:, b * 256:b * 256 + 256], qa[:, h_, b * P:b * P + P], qa[:, 4 + h_ // 2, :],
                                  start=(b == 0), stop=True, skip_group_check=True)
                    end(mm)
                pe.wait_ge(w_four_in, 16)
                pe.wait_ge(unit_out, 13)
                for mp in range(2):
                    o = begin()
                    for e in range(2):
                        for k in range(GT):
                            m = 2 * mp + e
                            mm = mmul(o[:, e * 256:e * 256 + 256], wf[:, k, m * P:m * P + P], fT[:, k, :],
                                      start=(e == 0 and k == 0), stop=(k == GT - 1), skip_group_check=True)
                    end(mm)
                parts(PARTS * left + PARTS, PARTS)
                pe.wait_ge(prob_ready, 1)
                for h_ in range(4):
                    o = begin()
                    for k in range(TB):
                        for b in range(TB):
                            at = k * 256 + b * P
                            mm = tr(o[:, at:at + P], Pr[:, h_, b, k * P:k * P + P], c("ident"))
                    end(mm)
                pe.wait_ge(wglu_in, 16)
                pe.wait_ge(gelu_ready, GT)
                for mp in range(2):
                    for e in range(2):
                        m = 2 * mp + e
                        for k in range(GT):
                            mm = mmul(bank[:, 4 + mp, e * 256:e * 256 + 256], wglu[:, k, m * P:m * P + P], y[:, k, :],
                                      start=(e == 0 and k == 0), stop=(k == GT - 1), skip_group_check=True)
                    mm.then_inc(glu_mm, 1)
                pe.wait_ge(unit_out, 23)
                for hp in range(2):
                    o = begin()
                    for e in range(2):
                        h_ = 2 * hp + e
                        for k in range(TB):
                            mm = mmul(o[:, e * 256:e * 256 + 256], vt[:, k, h_ // 2, :], PT_[:, h_, k, :],
                                      start=(e == 0 and k == 0), stop=(k == 1), skip_group_check=True)
                    end(mm)
                parts(PARTS * left + 2 * PARTS, PARTS)

            @block.scalar
            def _(act):
                do = Steps(act, act_own)
                A = nc.scalar
                for b in range(TB):
                    do(A.activation(work[:, 0:2, :].rearrange("p a n -> p (a n)"), x[:, b, :], ACT.Square,
                                    accum_out=ssq[:, b:b + 1]))
                    do(A.activation(ssq[:, 2 + b:3 + b], ssq[:, b:b + 1], ACT.Sqrt, scale=1.0 / D, bias=c("eps")), rms_ready)

                def pieces(first, last):
                    for n in range(first, last):
                        act.wait_ge(piece_mm, n + 1)
                        u = PIECES[n]
                        dst = mixT[:, 2 * u:2 * u + 2] if u < 8 else rwT[:, 2 * u - 16:2 * u - 14]
                        do(A.copy(dst, pj_bank[:, n % 2, :].rearrange("p (m s) -> p m s", m=2)), piece_out)

                act.wait_ge(s5_arg, 1)
                do(A.activation(v[:, 3], v[:, 2], ACT.Exp), s5_act)
                act.wait_ge(s5_arg, 2)
                do(A.activation(v[:, 6], v[:, 4], ACT.Exp), s5_act)
                do(A.activation(v[:, 8], v[:, 7], ACT.Sin), s5_act)
                do(A.activation(v[:, 10], v[:, 9], ACT.Sin), s5_act)
                pieces(0, 1)
                for u in range(8):
                    act.wait_ge(turn_mm, u + 1)
                    which, part, d = u // 4, u // 2 % 2, u % 2
                    dst = (BT, CT)[which][:, part, 4 * d:4 * d + 4, :].rearrange("p q n -> p (q n)")
                    do(A.copy(dst, turn_bank), turn_out)
                    if u == 3:
                        pieces(1, 2)
                pieces(2, pieces_at(0))
                for i in range(1, 9):
                    pieces(pieces_at(i - 1), pieces_at(i))
                    if i % 2 == 0:
                        ct = i // 2 - 1
                        act.wait_ge(pre_ready, ct + 1)
                        do(A.activation(y[:, ct, :], y[:, ct, :], ACT.Gelu_apprx_tanh), gelu_ready)
                unit = [0]

                def take(dst, func=ACT.Copy, **kw):
                    act.wait_ge(unit_mm, unit[0] + 1)
                    src = bank[:, unit[0] % 4, :]
                    unit[0] += 1
                    do(A.activation(dst, src, func, **kw), unit_out)

                for g in range(3):
                    take(flat(qa)[:, g * 512:g * 512 + 512], ACT.Sqrt, scale=1.0 / HEAD, bias=c("eps"))
                for h_ in range(4):
                    take(Z[:, h_].rearrange("p b n -> p (b n)"))
                pieces(left, left + 1)
                for g in range(3):
                    take(flat(qb)[:, g * 512:g * 512 + 512])
                take(vt.rearrange("p b g n -> p (b g n)"))
                for hp in range(2):
                    take(flat(fT[:, 2 * hp:2 * hp + 2]))
                for h_ in range(4):
                    take(S[:, h_].rearrange("p b n -> p (b n)"))
                act.wait_ge(max_ready, 1)
                for h_ in range(4):
                    for b in range(TB):
                        i = 2 * h_ + b
                        do(A.activation(Pr[:, h_, b, :], S[:, h_, b, :], ACT.Exp, scale=SCALE,
                                        bias=st8[:, 1, i:i + 1], accum_out=st8[:, 2, i:i + 1]), exps_ready, wait=False)
                for mp in range(2):
                    take(flat(ycT[:, 2 * mp:2 * mp + 2]))
                pieces(left + 1, left + 2)
                for h_ in range(4):
                    take(PT_[:, h_].rearrange("p k n -> p (k n)"))
                for mp in range(2):
                    act.wait_ge(glu_mm, 1 + mp)
                    do(A.activation(sig[:, mp * 512:mp * 512 + 512], bank[:, 4 + mp, :], ACT.Sigmoid), glu_out)
                for hp in range(2):
                    take(flat(ycT[:, 8 + 2 * hp:10 + 2 * hp]))
                pieces(left + 2, left + 3)

            @block.gpsimd
            def _(pool):
                do = Steps(pool, pool_own)
                G = nc.gpsimd
                pool.wait_ge(s5_act, 4)
                pool.wait_ge(exp_ready, 8)
                pool.wait_ge(cols_ready, 4)
                wr, wi, wr2, wi2 = v[:, 18], v[:, 19], v[:, 20], v[:, 21]
                do(G.tensor_copy(wr, v[:, 10]), wait=False)
                do(G.tensor_copy(wi, v[:, 8]))
                for f in range(2):
                    Ec, Es = factor[:, f, 0], factor[:, f, 1]
                    n = 1
                    while n < EL:
                        a = tmp[:, 0:32 * n].rearrange("p (g n) -> p g n", g=32)
                        b_ = tmp[:, 512:512 + 32 * n].rearrange("p (g n) -> p g n", g=32)
                        br, bi = wr.unsqueeze(2).to_broadcast([P, 32, n]), wi.unsqueeze(2).to_broadcast([P, 32, n])
                        do(G.tensor_tensor(a, Ec[:, :, 0:n], br, ALU.mult), wait=False)
                        do(G.tensor_tensor(b_, Es[:, :, 0:n], bi, ALU.mult))
                        do(G.tensor_tensor(Ec[:, :, n:2 * n], a, b_, ALU.subtract))
                        do(G.tensor_tensor(a, Es[:, :, 0:n], br, ALU.mult), wait=False)
                        do(G.tensor_tensor(b_, Ec[:, :, 0:n], bi, ALU.mult))
                        do(G.tensor_tensor(Es[:, :, n:2 * n], a, b_, ALU.add), wait=False)
                        do(G.tensor_tensor(v[:, 22], wi, wi, ALU.mult), wait=False)
                        do(G.tensor_tensor(wr2, wr, wr, ALU.mult), wait=False)
                        do(G.tensor_tensor(wi2, wr, wi, ALU.mult))
                        do(G.tensor_tensor(wr, wr2, v[:, 22], ALU.subtract), wait=False)
                        do(G.tensor_tensor(wi, wi2, wi2, ALU.add))
                        n *= 2
                for i, (ct, d) in enumerate(order):
                    q0 = d * 16 + ct * 4
                    lo = lambda k: factor[:, 0, k, q0:q0 + 4].unsqueeze(2).to_broadcast([P, 4, EL, EL])
                    hi = lambda k: factor[:, 1, k, q0:q0 + 4].unsqueeze(3).to_broadcast([P, 4, EL, EL])
                    q4 = lambda a: a.rearrange("p (j m n) -> p j m n", j=4, m=EL)
                    if i >= 2:
                        pool.wait_ge(x_ready, i - 1)
                    Tc, Ts = q4(table[:, i % 2, 0]), q4(table[:, i % 2, 1])
                    do(G.tensor_tensor(Tc, lo(0), hi(0), ALU.mult), wait=False)
                    do(G.tensor_tensor(q4(tmp[:]), lo(1), hi(1), ALU.mult))
                    do(G.tensor_tensor(Tc, Tc, q4(tmp[:]), ALU.subtract))
                    do(G.tensor_tensor(Ts, lo(1), hi(0), ALU.mult), wait=False)
                    do(G.tensor_tensor(q4(tmp[:]), lo(0), hi(1), ALU.mult))
                    do(G.tensor_tensor(Ts, Ts, q4(tmp[:]), ALU.add), table_ready)

            @block.vector
            def _(dve):
                do = Steps(dve, dve_own)
                V = nc.vector
                for b in range(TB):
                    dve.wait_ge(rms_ready, b + 1)
                    do(V.reciprocal(ssq[:, 4 + b:5 + b], ssq[:, 2 + b:3 + b]))
                    if b:
                        dve.wait_ge(hT_mm, 4)
                    do(V.tensor_scalar(h[:], x[:, b, :], ssq[:, 4 + b:5 + b], None, ALU.mult), h_ready)
                    if b == 0:
                        dve.wait_ge(rows_in, 17 * 16)
                        do(V.tensor_copy(srow[64:96, :].rearrange("q (e p) -> q e p", e=2),
                                         ls2[64:96, :].unsqueeze(2).to_broadcast([32, 2, S5P])), ls_ready)
                dve.wait_ge(rows_T, 1)
                do(V.tensor_copy(pcol[:], bank[:, 7, 0:NROWS]), cols_ready)
                do(V.tensor_copy(v[:, 0:3], bank[:, 7, 256:352].rearrange("p (a b) -> p a b", a=3)), cols_ready)
                for b in range(TB):
                    for q in range(4):
                        dve.wait_ge(hT_mm, 4 * b + q + 1)
                        do(V.tensor_tensor(hT[:, 4 * q:4 * q + 4, b * P:b * P + P],
                                           bank[:, 4 * b + q, :].rearrange("p (k s) -> p k s", k=4),
                                           col("norm_mix", 4 * q, 4).unsqueeze(2).to_broadcast([P, 4, P]), ALU.mult),
                           hT_ready, wait=False)
                do(V.tensor_copy(v[:, 23], v[:, 2]), s5_arg)
                for f in range(2):
                    do(V.memset(factor[:, f, 0, :, 0:1], 1.0), wait=False)
                    do(V.memset(factor[:, f, 1, :, 0:1], 0.0), cols_ready, wait=False)
                mu = col("mu", 0, 32).rearrange("p (i s g) -> p i s g", i=4, s=2)
                m4 = mus[:].rearrange("p (i g) -> p i g", i=4)
                do(V.tensor_tensor(m4, mu[:, :, 0, :], mu[:, :, 1, :], ALU.add))
                do(V.tensor_scalar(mus[:], mus[:], -1.0, 1.0, ALU.mult, ALU.add), wait=False)
                dve.wait_ge(s5_act, 1)
                re, im, step = v[:, 0], v[:, 1], v[:, 3]
                do(V.tensor_tensor(v[:, 4], re, step, ALU.mult))
                do(V.tensor_tensor(v[:, 5], im, step, ALU.mult))
                big = 1.5 * 2.0 ** 23
                do(V.tensor_scalar(v[:, 11], v[:, 5], 1.0 / (2 * math.pi), big, ALU.mult, ALU.add))
                do(V.tensor_scalar(v[:, 11], v[:, 11], big, None, ALU.subtract))
                do(V.scalar_tensor_tensor(v[:, 12], v[:, 11], -6.28125, v[:, 5], ALU.mult, ALU.add))
                do(V.scalar_tensor_tensor(v[:, 12], v[:, 11], -(2 * math.pi - 6.28125), v[:, 12], ALU.mult, ALU.add))
                do(V.tensor_scalar(v[:, 7], v[:, 12], 3.1415925, -3.1415925, ALU.min, ALU.max))
                do(V.scalar_tensor_tensor(v[:, 12], v[:, 7], -1.0, v[:, 7], ALU.mult, ALU.max))
                do(V.tensor_scalar(v[:, 9], v[:, 12], -1.0, math.pi / 2, ALU.mult, ALU.add), s5_arg)
                for i in range(2):
                    do(V.memset(work[:, i, :], 0.0))
                dve.wait_ge(raw_in, 64)
                for i in range(2):
                    r = raw[:, i].rearrange("p (q h) -> p q h", q=32)
                    do(V.tensor_copy(bexp[i][0:64, :, 0:16], r[0:64]), exp_ready, wait=False)
                    do(V.tensor_copy(bexp[i][64:128, :, 16:32], r[64:128]), exp_ready, wait=False)
                    r = raw[:, 2 + i].rearrange("p (q n) -> p q n", q=8)
                    do(V.tensor_scalar(cexp[i][:, :, 0:64], r, c("even"), None, ALU.mult), exp_ready, wait=False)
                    do(V.tensor_scalar(cexp[i][:, :, 64:128], r, c("odd"), None, ALU.mult), exp_ready, wait=False)
                dve.wait_ge(s5_act, 4)
                rho, sn, cs = v[:, 6], v[:, 8], v[:, 10]
                do(V.tensor_tensor(v[:, 11], rho, cs, ALU.mult))
                do(V.tensor_scalar(v[:, 11], v[:, 11], -1.0, None, ALU.add))
                do(V.tensor_tensor(v[:, 12], rho, sn, ALU.mult))
                do(V.tensor_tensor(v[:, 13], re, re, ALU.mult))
                do(V.tensor_tensor(v[:, 14], im, im, ALU.mult))
                do(V.tensor_tensor(v[:, 13], v[:, 13], v[:, 14], ALU.add))
                do(V.reciprocal(v[:, 13], v[:, 13]))
                do(V.tensor_tensor(v[:, 14], v[:, 11], re, ALU.mult))
                do(V.tensor_tensor(v[:, 15], v[:, 12], im, ALU.mult))
                do(V.tensor_tensor(v[:, 14], v[:, 14], v[:, 15], ALU.add))
                do(V.tensor_tensor(v[:, 16], v[:, 14], v[:, 13], ALU.mult))
                do(V.tensor_tensor(v[:, 14], v[:, 12], re, ALU.mult))
                do(V.tensor_tensor(v[:, 15], v[:, 11], im, ALU.mult))
                do(V.tensor_tensor(v[:, 14], v[:, 14], v[:, 15], ALU.subtract))
                do(V.tensor_tensor(v[:, 17], v[:, 14], v[:, 13], ALU.mult))
                dve.wait_ge(turn_out, 8)
                cr = CT[:, 0].rearrange("p q (j n) -> p (q j) n", j=4)
                ci = CT[:, 1].rearrange("p q (j n) -> p (q j) n", j=4)
                kr = v[:, 16].unsqueeze(2).to_broadcast([P, 32, 32])
                ki = v[:, 17].unsqueeze(2).to_broadcast([P, 32, 32])
                w = [work[:, i].rearrange("p (q n) -> p q n", q=32) for i in range(6)]
                do(V.tensor_tensor(w[0], cr, kr, ALU.mult), wait=False)
                do(V.tensor_tensor(w[1], ci, ki, ALU.mult), wait=False)
                do(V.tensor_tensor(w[2], cr, ki, ALU.mult), wait=False)
                do(V.tensor_tensor(w[3], ci, kr, ALU.mult))
                do(V.tensor_tensor(cr, w[0], w[1], ALU.subtract), wait=False)
                do(V.scalar_tensor_tensor(ci, w[2], -1.0, w[3], ALU.mult, ALU.subtract), c_ready)

                def finish(i):
                    ct = order[i][0]
                    do(V.scalar_tensor_tensor(y[:, ct, :], mixT[:, T_B + ct, :], col("s5_d", ct), yb[:, 0:SEQ],
                                              ALU.mult, ALU.add), pre_ready)

                for i, (ct, d) in enumerate(order):
                    q0 = d * 16 + ct * 4
                    e = slice(None, None, -1) if d else slice(None)
                    tc, ts = [table[:, i % 2, k].rearrange("p (j s) -> p j s", j=4)[:, :, e] for k in range(2)]
                    f = [work[:, k].rearrange("p (j s) -> p j s", j=4) for k in range(6)]
                    re, im = bu[:, :, 0:SEQ], bu[:, :, SEQ:2 * SEQ]
                    dve.wait_ge(table_ready, i + 1)
                    dve.wait_ge(bu_mm, i + 1)
                    do(V.tensor_tensor(f[2], re, tc, ALU.mult), wait=False)
                    do(V.tensor_tensor(f[3], im, ts, ALU.mult), wait=False)
                    do(V.tensor_tensor(f[4], im, tc, ALU.mult), wait=False)
                    do(V.tensor_tensor(f[5], re, ts, ALU.mult), bu_used)
                    if i:
                        dve.wait_ge(y_mm, i)
                        if d == 0:
                            finish(i - 1)
                    do(V.tensor_tensor(f[0], f[2], f[3], ALU.add), wait=False)
                    do(V.tensor_tensor(f[1], f[4], f[5], ALU.subtract))
                    for part in range(2):
                        for j in range(4):
                            do(V.tensor_tensor_scan(f[2 + part][:, j, e], v[:, 6, q0 + j:q0 + j + 1].to_broadcast([P, SEQ]),
                                                    f[part][:, j, e], 0.0, ALU.mult, ALU.add), wait=(part == 1 and j == 3))
                    do(V.tensor_tensor(f[4], f[2], tc, ALU.mult), wait=False)
                    do(V.tensor_tensor(f[5], f[3], ts, ALU.mult))
                    do(V.tensor_tensor(f[0], f[4], f[5], ALU.subtract))
                    do(V.tensor_tensor(f[4], f[2], ts, ALU.mult), wait=False)
                    do(V.tensor_tensor(f[5], f[3], tc, ALU.mult))
                    do(V.tensor_tensor(f[1], f[4], f[5], ALU.add), x_ready)
                do(V.tensor_tensor(qb, mixT[:, T_Q:T_Q + 6, :], mixT[:, T_Q:T_Q + 6, :], ALU.mult), sq_ready)
                dve.wait_ge(y_mm, len(order))
                finish(len(order) - 1)
                dve.wait_ge(unit_out, 3)
                do(V.reciprocal(qa, qa))
                for i in range(6):
                    do(V.scalar_tensor_tensor(qk[:, i, :], mixT[:, T_Q + i, :], col("q_norm" if i < 4 else "k_norm"),
                                              qa[:, i, :], ALU.mult, ALU.mult), wait=(i == 5))
                dve.sem_inc(qn_ready, 1)
                do(V.tensor_tensor(qa, qk, c("cos").unsqueeze(1).to_broadcast([P, 6, SEQ]), ALU.mult))
                dve.wait_ge(unit_out, 10)
                do(V.tensor_tensor(qb, qb, c("sin").unsqueeze(1).to_broadcast([P, 6, SEQ]), ALU.mult))
                do(V.tensor_tensor(qa, qa, qb, ALU.add), rope_ready)
                dve.wait_ge(unit_out, 17)
                do(V.tensor_reduce(st8[:, 0], S.rearrange("p h b n -> p (h b) n"), AX.X, ALU.max))
                do(V.tensor_scalar(st8[:, 1], st8[:, 0], -SCALE, None, ALU.mult), max_ready)
                dve.wait_ge(exps_ready, 8)
                do(V.reciprocal(st8[:, 3], st8[:, 2]))
                p8 = Pr.rearrange("p h b n -> p (h b) n")
                do(V.tensor_tensor(p8, p8, st8[:, 3].unsqueeze(2).to_broadcast([P, 8, SEQ]), ALU.mult), prob_ready)
                for i in range(GT):
                    token_shift(nc, do, col, mus, rwT, ycT[:, 12 + i, :], 3, i)
                dve.wait_ge(glu_out, 2)
                do(V.tensor_tensor(flat(y), flat(y), sig, ALU.mult))


def token_shift(nc, do, col, mus, rwT, dst, kind, i):
    V, src = nc.vector, rwT[:, 4 * kind + i, :]
    do(V.tensor_scalar(dst, src, mus[:, 4 * kind + i:4 * kind + i + 1], None, ALU.mult))
    do(V.scalar_tensor_tensor(dst[:, 1:], src[:, :-1], col("mu", 8 * kind + i), dst[:, 1:], ALU.mult, ALU.add))
    do(V.scalar_tensor_tensor(dst[:, :-1], src[:, 1:], col("mu", 8 * kind + 4 + i), dst[:, :-1], ALU.mult, ALU.add))


OUT_PIECES = [(n, kh) for kh in range(2) for n in range(4)]
EARLY = 3


def out_bank(n):
    return (6, 0, 2, 4)[n]


def out_piece(nc, t, layer, out_w, engine, i):
    n, kh = OUT_PIECES[i]
    engine.dma_start(out_w["place"][:, i % 2], t["w_out"][layer][kh * HALF_K * P:(kh + 1) * HALF_K * P, n * GW:(n + 1) * GW]
                     .rearrange("(k p) n -> p k n", p=P)).then_inc(out_w["in"][i % 2], 16)


def out_products(nc, out_w, bank, pe, ycT, i, first, last):
    n, kh = OUT_PIECES[i]
    if first == 0:
        pe.wait_ge(out_w["in"][i % 2], 16 * (i // 2 + 1))
    for j in range(first, last):
        b, k = divmod(j, HALF_K)
        mm = nc.tensor.matmul(bank[:, out_bank(n) + b, :], ycT[:, kh * HALF_K + k, b * P:b * P + P], out_w["place"][:, i % 2, k, :],
                              start=(kh == 0 and k == 0), stop=(kh == 1 and k == HALF_K - 1), skip_group_check=True)
    if last == TB * HALF_K:
        mm.then_inc(out_w["used"], 1)


def rwkv(nc, t, layer, sem, sb, bank, c, col, mus, rwT, ycT, arena, out_w):
    both = lambda *names: [f"{n}{d}" for n in names for d in range(2)]
    PE_EV = (["trV"] + both("pa", "pc", "nn") + ["trA"] + both("vp", "sq2") + ["trB", "trK"]
             + both("sq4", "w2", "w4", "sq8", "w8", "x", "no", "z", "qy", "gh"))
    ACT_EV = ["trV", "trA"] + both("vp", "sq2") + ["trB", "trK"] + both("sq4", "sq8", "x", "no", "gh")
    DVE_EV = both("pa", "pc", "nn", "w2", "w4", "w8", "z", "qy", "gh")

    def at(events, i, name):
        return i * len(events) + events.index(name) + 1

    w_in, up_in, low_mm, low_out = sem("rw_w_in"), sem("rw_up_in"), sem("rw_low_mm"), sem("rw_low_out")
    up_mm, up_out, kq_ready, kq_mm, root_out, prepared = [sem("rw_" + n) for n in ("up_mm", "up_out", "kq", "kq_mm",
                                                                                  "kk_root", "prepared")]
    pe_ev, act_ev, dve_ev = sem("rw_pe"), sem("rw_act"), sem("rw_dve")
    state_mm, out_mm, state_ready, y_ready = sem("rw_state_mm"), sem("rw_out_mm"), sem("rw_state"), sem("rw_y_ready")
    norm_sq, norm_mm, norm_root = sem("rw_norm_sq"), sem("rw_norm_mm"), sem("rw_norm_root")
    stat_mm, root_ready, sqd_ready = sem("rw_stat_mm"), sem("rw_root"), sem("rw_sqd")
    dve_own, act_own, sq_d_ready = sem("rw_dve_own"), sem("rw_act_own"), sem("rw_sq_d")
    Q = 2 * GT
    with ExitStack() as st:
        w1 = sb(st, "rw_w1", [P, GT, P])
        g1 = sb(st, "rw_g1", [P, GT, 96])
        w2 = sb(st, "rw_w2", [P, GW])
        g2 = sb(st, "rw_g2", [96, GW])
        low = sb(st, "rw_low", [P, SEQ])
        lowg = sb(st, "rw_lowg", [96, SEQ])
        zs = ycT[:, 12:16, :]
        spare = sb(st, "rw_diag", [P, GT, SEQ])
        H = sb(st, "rw_H", [P, NCH, Q, RH])
        h_flat = H[:].rearrange("p n q k -> p (n q k)")
        sq = h_flat[:, 0:3072].rearrange("p (k s) -> p k s", k=12)
        rstd = h_flat[:, 3072:3840].rearrange("p (g s) -> p g s", g=3)
        diag = spare[:].rearrange("p a s -> p (a s)").rearrange("p (d n k) -> p d n k", d=2, n=NCH)
        keep = sb(st, "rw_keep", [P, GT])
        sr, sk, sv, kk = [sb(st, f"rw_{n}", [P, SEQ]) for n in ("sr", "sk", "sv", "kkn")]
        kq = sb(st, "rw_kq", [P, SEQ])
        kd, kb, Pc, IP, Pe, D1, BH, KH, wend, BTc = [sb(st, f"rw_{n}", [P, 2, SEQ]) for n in
                                                     ("kd", "kb", "pc", "ip", "pe", "d1", "bh", "kh", "wend", "btc")]
        KTc = sb(st, "rw_ktc", [P, 2, SEQ])
        pend = sb(st, "rw_pend", [P, 2, NCH])
        ARs = sb(st, "rw_ar", [P, 2, 2, TB, 2, P])
        R = sb(st, "rw_r", [P, 2, 4, P])
        mats = {n: arena[:, 1024 * i:1024 * i + 1024].rearrange("p (d j k) -> p d j k", d=2, j=4)
                for i, n in enumerate(("NT", "NTo", "Rb", "Aak", "Rk", "N", "N2T", "N2", "W"))}
        mats["N4T"], mats["N4"], mats["N8"] = mats["NT"], mats["N"], mats["N2T"]
        Yo = mats["N2"]
        Bt = sb(st, "rw_bt", [P, 2, TB, P])
        Kt = sb(st, "rw_kt", [P, 2, TB, P])
        Vt = sb(st, "rw_vt", [P, TB, P])
        G = sb(st, "rw_G", [P, NCH, Q, RH])
        QT = sb(st, "rw_QT", [P, Q, SEQ])
        yin = sb(st, "rw_yin", [P, GT, SEQ])
        bonus = sb(st, "rw_bonus", [P, GT, SEQ])
        gt = sb(st, "rw_gt", [P, GT, SEQ])
        S = arena[:, 8192:9216].rearrange("p (d q k) -> p d q k", d=2, q=Q)
        sq_d, rstd_d = spare, kq
        flat = lambda a: a.rearrange("p a s -> p (a s)")
        big = lambda a, i: a[:].rearrange("p n q k -> p (n q k)")[:, i * 1024:i * 1024 + 1024]
        dlt, sqd = big(G, 0), big(G, 1)
        decay = lambda i: QT[:, 2 * i:2 * i + 2, :]
        rate = lambda i: G[:, 0:4, 2 * i:2 * i + 2, :].rearrange("p n d k -> p d n k")

        with nc.Block() as block:
            @block.sync
            def _(sp):
                for d in range(2):
                    sp.dma_start(w1[:, :, 32 * d:32 * d + 32], t["rwkv_w1"][layer, d].rearrange("(k p) n -> p k n", p=P))\
                        .then_inc(w_in, 16)
                    sp.dma_start(w1[:, :, 64 + 32 * d:96 + 32 * d],
                                 t["rwkv_a1"][layer, d].rearrange("(k p) n -> p k n", p=P)).then_inc(w_in, 16)
                sp.dma_start(g1[:], t["rwkv_g1"][layer].rearrange("(k p) n -> p k n", p=P)).then_inc(w_in, 16)
                for d in range(2):
                    sp.dma_start(w2[32 * d:32 * d + 32, :], t["rwkv_w2"][layer, d]).then_inc(up_in, 16)
                    sp.dma_start(w2[64 + 32 * d:96 + 32 * d, :], t["rwkv_a2"][layer, d]).then_inc(up_in, 16)
                sp.dma_start(g2[:], t["rwkv_g2"][layer]).then_inc(up_in, 16)
                sp.wait_ge(pe_ev, at(PE_EV, GT - 1, "gh1"))
                for i in range(EARLY + 2):
                    if i >= 2:
                        sp.wait_ge(out_w["used"], i - 1)
                    out_piece(nc, t, layer, out_w, sp, i)

            @block.tensor
            def _(pe):
                mmul, tr = nc.tensor.matmul, nc.tensor.transpose
                pe.wait_ge(w_in, 80)
                for k in range(GT):
                    mmul(bank[:, 0, 0:SEQ], w1[:, k, :], zs[:, k, :], start=(k == 0), stop=(k == GT - 1))
                for k in range(GT):
                    mm = mmul(bank[0:96, 1, 0:SEQ], g1[:, k, :], zs[:, k, :], start=(k == 0), stop=(k == GT - 1))
                mm.then_inc(low_mm, 1)

                def head_sums(i, which):
                    pe.wait_ge(kq_ready, 2 * i + which + 1)
                    mmul(bank[:, 6 + which, 0:SEQ], c("heads"), kq[:], start=True, stop=True).then_inc(kq_mm, 1)

                pe.wait_ge(low_out, 3)
                pe.wait_ge(up_in, 80)
                for i in range(GT):
                    if i == 1:
                        pe.wait_ge(norm_sq, 1)
                        for g in range(3):
                            for k in range(4):
                                mm = mmul(bank[:, 5 + g // 2 * 2, g % 2 * 256:g % 2 * 256 + 256], c("ones"), sq[:, 4 * g + k, :],
                                          start=(g % 2 == 0 and k == 0), stop=(k == 3), skip_group_check=True)
                        mm.then_inc(norm_mm, 1)
                        head_sums(0, 0)
                    if i:
                        pe.wait_ge(up_out, 5 * i + (i > 1))
                    for u in range(4):
                        mmul(bank[:, u, 0:SEQ], w2[32 * u:32 * u + 32, i * P:i * P + P], low[32 * u:32 * u + 32, :],
                             start=True, stop=True)
                    mmul(bank[:, 4, 0:SEQ], g2[:, i * P:i * P + P], lowg[:], start=True, stop=True).then_inc(up_mm, 1)

                pe.wait_ge(norm_root, 2)
                head_sums(0, 1)
                pe.wait_ge(up_out, 21)
                for i in range(GT):
                    AR = ARs[:, i % 2]
                    dve = lambda name: pe.wait_ge(dve_ev, at(DVE_EV, i, name))
                    act = lambda name: pe.wait_ge(act_ev, at(ACT_EV, i, name))
                    ev = lambda mm: mm.then_inc(pe_ev, 1)
                    last = i == GT - 1
                    pe.wait_ge(prepared, i + 1)
                    for b in range(TB):
                        mm = tr(bank[:, 6, b * P:b * P + P], sv[:, b * P:b * P + P], c("ident"))
                    ev(mm)
                    if i:
                        pe.wait_ge(dve_ev, at(DVE_EV, i - 1, "gh1"))
                        pe.wait_ge(act_ev, at(ACT_EV, i - 1, "gh1"))

                    def pairs(d, left, banks):
                        for b in range(TB):
                            for e in range(2):
                                r = slice(RH * e, RH * e + RH)
                                mm = mmul(bank[:, banks[e], b * 256:b * 256 + 256], left[r, d, b * P:b * P + P],
                                          AR[r, d, b, :, :].rearrange("p a s -> p (a s)"), start=(b == 0), stop=True,
                                          skip_group_check=True)
                        ev(mm)

                    def product(d, b, left, right):
                        for j in range(4):
                            mm = mmul(bank[:, b, j * P:j * P + P], left[:, d, j, :], right[:, d, j, :],
                                      start=(j == 0), stop=True, skip_group_check=True)
                        return mm

                    pairs(0, BH, (0, 1))
                    pairs(1, BH, (2, 3))
                    pairs(0, KH, (4, 5))
                    dve("pa0")
                    pairs(1, KH, (0, 1))
                    for d in range(2):
                        dve(("pa1", "pc0")[d])
                        for b in range(TB):
                            for e in range(2):
                                r = slice(RH * e, RH * e + RH)
                                mm = mmul(bank[:, 2 + 2 * d + e, b * P:b * P + P], AR[r, d, b, 0, :], BH[r, d, b * P:b * P + P],
                                          start=(b == 0), stop=True, skip_group_check=True)
                        ev(mm)

                    def turn(n, b0, src):
                        for d in range(2):
                            for b in range(TB):
                                mm = tr(bank[:, b0, (2 * d + b) * P:(2 * d + b + 1) * P], src(d, b), c("ident"))
                        ev(mm)

                    turn("trA", 7, lambda d, b: AR[:, d, b, 0, :])
                    dve("pc1")
                    act("trV")
                    for d in range(2):
                        for j in range(4):
                            e, b = divmod(j, 2)
                            mm = mmul(bank[:, d, j * RH:j * RH + RH], mats["Aak"][:, d, j, :],
                                      Vt[:, b, e * RH:e * RH + RH], start=(j == 0), stop=True, skip_group_check=True)
                        ev(mm)
                    for d in range(2):
                        dve(f"nn{d}")
                        product(d, 2 + 2 * d, mats["N"], mats["NT"])
                        ev(product(d, 3 + 2 * d, mats["NT"], mats["N"]))
                    turn("trB", 6, lambda d, b: BTc[:, d, b * P:b * P + P])
                    act("trA")
                    turn("trK", 7, lambda d, b: KTc[:, d, b * P:b * P + P])
                    for d in range(2):
                        act(f"sq2{d}")
                        product(d, 2 * d, mats["N2"], mats["N2T"])
                        ev(product(d, 2 * d + 1, mats["N2T"], mats["N2"]))
                    for d in range(2):
                        ev(product(d, 4 + d, mats["N2"], mats["W"]))
                    if not last:
                        act("trK")
                        head_sums(i + 1, 0)
                    for d in range(2):
                        act(f"sq4{d}")
                        dve(f"w2{d}")
                        ev(product(d, d, mats["N4"], mats["W"]))
                    for d in range(2):
                        ev(product(d, 2 + d, mats["N4T"], mats["N4"]))
                    for d in range(2):
                        act(f"sq8{d}")
                        dve(f"w4{d}")
                        ev(product(d, 4 + d, mats["N8"], mats["W"]))
                    for d in range(2):
                        dve(f"w8{d}")
                        ev(product(d, d, mats["W"], R))
                    for d in range(2):
                        act(f"x{d}")
                        ev(product(d, 2 + d, mats["NTo"], R))
                    for d in range(2):
                        act(f"no{d}")
                        ev(product(d, 4 + d, mats["W"], Yo))
                    if not last:
                        head_sums(i + 1, 1)
                    for d in range(2):
                        dve(f"z{d}")
                        for b in range(TB):
                            for e in range(2):
                                j, rows = 2 * e + b, slice(RH * e, RH * e + RH)
                                mmul(bank[rows, d, b * P:b * P + P], R[:, d, j, RH:P], mats["Rb"][:, d, j, :],
                                     start=(b == 0), stop=True, skip_group_check=True)
                                mmul(bank[rows, d, 256 + b * P:384 + b * P], R[:, d, j, 0:RH], mats["Rb"][:, d, j, :],
                                     start=False, stop=False, skip_group_check=True)
                                mm = mmul(bank[rows, d, 256 + b * P:384 + b * P], Vt[:, b, e * RH:e * RH + RH],
                                          mats["Rk"][:, d, j, :], start=False, stop=True, skip_group_check=True)
                        ev(mm)
                    act("trK")
                    for d in range(2):
                        if d:
                            dve("gh0")
                            act("gh0")
                        for b in range(TB):
                            for e in range(2):
                                rows = slice(RH * e, RH * e + RH)
                                for step in ("G", "H: U", "H: V"):
                                    for q in range(CPB):
                                        j, k = 2 * e + b, slice(CH * q, CH * q + CH)
                                        o = bank[rows, 2 + q, b * P:b * P + P]
                                        if step == "G":
                                            mmul(o[:, 0:RH], R[k, d, j, RH:P], Bt[k, d, b, rows], start=(b == 0), stop=True,
                                                 skip_group_check=True)
                                        elif step == "H: U":
                                            mmul(o[:, RH:P], Bt[k, d, b, rows], R[k, d, j, 0:RH], start=False, stop=False,
                                                 skip_group_check=True)
                                        else:
                                            mm = mmul(o[:, RH:P], Kt[k, d, b, rows], Vt[k, b, rows], start=False, stop=True,
                                                      skip_group_check=True)
                        ev(mm)
                pe.wait_ge(dve_ev, at(DVE_EV, GT - 1, "gh1"))
                pe.wait_ge(act_ev, at(ACT_EV, GT - 1, "gh1"))
                for n in range(NCH):
                    pe.wait_ge(state_ready, n + 1)
                    if n < NCH - 1:
                        for q in range(Q):
                            for e in range(2):
                                r = slice(RH * e, RH * e + RH)
                                mm = mmul(bank[r, 4 + n % 2, q * RH:q * RH + RH], G[r, n, q, :], S[r, n % 2, q, :],
                                          start=(q == 0), stop=True, skip_group_check=True)
                        mm.then_inc(state_mm, 1)
                    for q in range(Q):
                        i, d = divmod(q, 2)
                        ch = n if d == 0 else NCH - 1 - n
                        at_ = i % 2 * SEQ + ch * CH
                        for e in range(2):
                            r = slice(RH * e, RH * e + RH)
                            mm = mmul(bank[r, 2 * d + i // 2, at_:at_ + CH], S[r, n % 2, q, :], QT[r, q, ch * CH:ch * CH + CH],
                                      start=(n == 0 and i % 2 == 0), stop=True, skip_group_check=True)
                    mm.then_inc(out_mm, 1)
                wo = lambda i, first, last: out_products(nc, out_w, bank, pe, ycT, i, first, last)
                wo(0, 0, 3)
                pe.wait_ge(y_ready, 1)
                for g in range(2):
                    mm = mmul(bank[:, 4 + g, :], c("heads"), flat(yin[:])[:, g * 512:g * 512 + 512], start=True, stop=True)
                mm.then_inc(stat_mm, 1)
                wo(0, 3, 6)
                pe.wait_ge(sqd_ready, 1)
                for g in range(2):
                    mm = mmul(bank[:, 4 + g, :], c("heads"), sqd[:, g * 512:g * 512 + 512], start=True, stop=True)
                mm.then_inc(stat_mm, 1)
                wo(0, 6, 16)
                wo(1, 0, 6)
                pe.wait_ge(sq_d_ready, 1)
                for k in range(GT):
                    mm = mmul(bank[:, 4, 0:SEQ], c("ones"), sq_d[:, k, :], start=(k == 0), stop=(k == GT - 1))
                mm.then_inc(stat_mm, 1)
                wo(1, 6, 16)
                wo(2, 0, 16)

            @block.scalar
            def _(act):
                do = Steps(act, act_own)
                A = nc.scalar
                act.wait_ge(low_mm, 1)
                do(A.activation(low[0:64, :], bank[0:64, 0, 0:SEQ], ACT.Tanh), low_out)
                do(A.copy(low[64:128, :], bank[64:128, 0, 0:SEQ]), low_out)
                do(A.activation(lowg[:], bank[0:96, 1, 0:SEQ], ACT.Sigmoid), low_out)

                def kk_root(i):
                    act.wait_ge(kq_mm, 2 * i + 1)
                    do(A.activation(kk[:], bank[:, 6, 0:SEQ], ACT.Sqrt, bias=c("eps_kk")), root_out)

                for i in range(GT):
                    act.wait_ge(up_mm, i + 1)
                    for d in range(2):
                        do(A.activation(decay(i)[:, d], bank[:, d, 0:SEQ], ACT.Sigmoid, bias=col("w0", 4 * d + i)), up_out, wait=False)
                        do(A.activation(rate(i)[:, d], bank[:, 2 + d, 0:SEQ].rearrange("p (n k) -> p n k", n=4), ACT.Sigmoid,
                                        bias=col("a0", 4 * d + i)), up_out, wait=False)
                    do(A.copy(gt[:, i, :], bank[:, 4, 0:SEQ]), up_out, wait=False)
                    if i in (0, GT - 1):
                        q2 = QT[:, 0:2] if i == 0 else QT[:, 2:]
                        q2 = q2.rearrange("p q s -> p (q s)")
                        act.wait_ge(up_out, 5 if i == 0 else 21)
                        do(A.activation(q2, q2, ACT.Exp, scale=-math.exp(-0.5)), up_out, wait=False)
                    if i == 0:
                        kk_root(0)
                        act.wait_ge(norm_mm, 1)
                        for a, b in ((0, 5), (2, 7)):
                            n = 2 if a == 0 else 1
                            do(A.activation(rstd[:, a:a + n].rearrange("p g s -> p (g s)"), bank[:, b, 0:n * SEQ], ACT.Sqrt,
                                            scale=1.0 / GW, bias=c("eps")), norm_root)

                for i in range(GT):
                    pe = lambda name: act.wait_ge(pe_ev, at(PE_EV, i, name))
                    jk = lambda a, d: a[:, d].rearrange("p j k -> p (j k)")
                    pe("trV")
                    do(A.copy(flat(Vt[:]), bank[:, 6, 0:256]), act_ev, wait=False)
                    pe("trA")
                    src = bank[:, 7, :].rearrange("p (d b e k) -> p d b e k", d=2, b=TB, e=2)
                    dst = R[:, :, :, RH:P].rearrange("p d (e b) k -> p d b e k", e=2)
                    do(A.copy(dst[:, 0], src[:, 0]), wait=False)
                    do(A.copy(dst[:, 1], src[:, 1]), act_ev, wait=False)
                    for d in range(2):
                        pe(f"vp{d}")
                        do(A.copy(R[:, d, :, 0:RH], bank[:, d, 0:256].rearrange("p (j k) -> p j k", j=4)), act_ev, wait=False)
                    for d in range(2):
                        pe(f"sq2{d}")
                        do(A.copy(jk(mats["N2T"], d), bank[:, 2 + 2 * d, :]), wait=False)
                        do(A.copy(jk(mats["N2"], d), bank[:, 3 + 2 * d, :]), act_ev, wait=False)
                    pe("trB")
                    do(A.copy(Bt[:].rearrange("p d b k -> p (d b k)"), bank[:, 6, :]), act_ev, wait=False)
                    pe("trK")
                    do(A.copy(Kt[:].rearrange("p d b k -> p (d b k)"), bank[:, 7, :]), act_ev, wait=False)
                    for d in range(2):
                        pe(f"sq4{d}")
                        do(A.copy(jk(mats["N4T"], d), bank[:, 2 * d, :]), wait=False)
                        do(A.copy(jk(mats["N4"], d), bank[:, 2 * d + 1, :]), act_ev, wait=False)
                    if i < GT - 1:
                        kk_root(i + 1)
                    for name, dst, b0 in (("sq8", mats["N8"], 2), ("x", R, 0), ("no", Yo, 2)):
                        for d in range(2):
                            pe(f"{name}{d}")
                            do(A.copy(jk(dst, d), bank[:, b0 + d, :]), act_ev, wait=False)
                    for d in range(2):
                        act.wait_ge(dve_ev, at(DVE_EV, i, f"gh{d}"))
                        dst = H[:, ::-1, 2 * i + d, :] if d else H[:, :, 2 * i + d, :]
                        src = bank[:, 2:6, 0:256].rearrange("p q (b n) -> p b q n", b=TB)[:, :, :, RH:P]
                        do(A.copy(dst.rearrange("p (b q) k -> p b q k", b=TB), src), act_ev, wait=False)
                act.wait_ge(stat_mm, 2)
                do(A.activation(sqd, bank[:, 4:6, :].rearrange("p b n -> p (b n)"), ACT.Sqrt, scale=1.0 / RH,
                                bias=c("eps_gn")), root_ready)
                act.wait_ge(stat_mm, 3)
                do(A.activation(rstd_d[:], bank[:, 4, 0:SEQ], ACT.Sqrt, scale=1.0 / GW, bias=c("eps")), root_ready)

            @block.vector
            def _(dve):
                do = Steps(dve, dve_own)
                V = nc.vector

                shift = lambda dst, kind, i: token_shift(nc, do, col, mus, rwT, dst, kind, i)
                do(V.tensor_scalar(keep[:], col("k_a", 0, 4), -1.0, 1.0, ALU.mult, ALU.add), wait=False)
                do(V.memset(D1[:], 0.0))
                do(V.memset(Pe[:], 1.0))
                on2 = lambda a: a.unsqueeze(1).to_broadcast([P, 2, SEQ])
                n64 = lambda a: a.rearrange("p d (n k) -> p d n k", n=4)
                n32 = lambda a: a.rearrange("p (n s) -> p n s", s=CH)
                s2 = lambda a: a.rearrange("p (b s) -> p b s", b=TB)
                jk = lambda a, d: a[:, d].rearrange("p j k -> p (j k)")

                def prepare_1(i):
                    shift(sr[:], 0, i)
                    shift(sk[:], 1, i)
                    shift(sv[:], 2, i)
                    do(V.scalar_tensor_tensor(kq[:], sk[:], col("k_k", i), sk[:], ALU.mult, ALU.mult))
                    do(V.tensor_scalar(kq[:], kq[:], col("k_k", i), None, ALU.mult), kq_ready)

                def prepare_3(i):
                    if i == 0:
                        dve.wait_ge(up_out, 5)
                    do(V.tensor_scalar(n64(kd[:]), rate(i), col("k_a", i), keep[:, i:i + 1], ALU.mult, ALU.add))
                    do(V.tensor_tensor(kd[:], kd[:], on2(sk[:]), ALU.mult))
                    dve.wait_ge(root_out, i + 1)
                    do(V.tensor_tensor(kq[:], kd[:, 0, :], kd[:, 1, :], ALU.add), wait=False)
                    do(V.reciprocal(kk[:], kk[:]))
                    do(V.scalar_tensor_tensor(kq[:], sr[:], col("r_k", i), kq[:], ALU.mult, ALU.mult), kq_ready, wait=False)
                    do(V.scalar_tensor_tensor(kk[:], sk[:], col("k_k", i), kk[:], ALU.mult, ALU.mult))
                    do(V.tensor_tensor(n64(kb[:]), rate(i), n64(on2(kk[:])), ALU.mult))

                def prepare_2(i):
                    dec = decay(i)
                    if i < 2:
                        dve.wait_ge(up_out, 22 if i else 6)
                    for d in range(2):
                        s0 = CH - 1 if d else 0
                        do(V.tensor_copy(D1[:, d, s0::CH], dec[:, d, s0::CH]), wait=(d == 1))
                    for d in range(2):
                        s0 = CH - 1 if d else 0
                        do(V.memset(dec[:, d, s0::CH], 0.0), wait=(d == 1))
                    for d in range(2):
                        o = slice(None, None, -1) if d else slice(None)
                        do(V.tensor_tensor_scan(Pc[:, d, o], dec[:, d, o], D1[:, d, o], 0.0, ALU.mult, ALU.add), wait=(d == 1))
                    do(V.reciprocal(IP[:], Pc[:]), wait=False)
                    do(V.tensor_copy(n32(Pe[:, 0, :])[:, :, 1:], n32(Pc[:, 0, :])[:, :, :-1]), wait=False)
                    do(V.tensor_copy(n32(Pe[:, 1, :])[:, :, :-1], n32(Pc[:, 1, :])[:, :, 1:]), wait=False)
                    do(V.tensor_copy(pend[:, 0, :], Pc[:, 0, CH - 1::CH]), wait=False)
                    do(V.tensor_copy(pend[:, 1, :], Pc[:, 1, 0::CH]))

                def prepare_4(i):
                    AR = ARs[:, i % 2]
                    for d in range(2):
                        do(V.scalar_tensor_tensor(AR[:, d, :, 0, :], s2(Pe[:, d, :]), -1.0, s2(kk[:]), ALU.mult, ALU.mult),
                           wait=False)
                        do(V.tensor_tensor(AR[:, d, :, 1, :], s2(Pc[:, d, :]), s2(sr[:]), ALU.mult), wait=False)
                    do(V.tensor_tensor(KH[:], kd[:], IP[:], ALU.mult), wait=False)
                    do(V.tensor_tensor(BH[:], kb[:], IP[:], ALU.mult), wait=False)

                def prepare_5(i):
                    nn = lambda a: n32(flat(a[:]))
                    do(V.tensor_tensor(nn(wend), nn(IP), flat(pend[:]).unsqueeze(2).to_broadcast([P, 16, CH]), ALU.mult))
                    do(V.tensor_tensor(BTc[:], kb[:], wend[:], ALU.mult), wait=False)
                    do(V.tensor_tensor(KTc[:], kd[:], wend[:], ALU.mult), wait=False)
                    dve.wait_ge(kq_mm, 2 * i + 2)
                    do(V.tensor_tensor(bonus[:, i, :], bank[:, 7, 0:SEQ], sv[:], ALU.mult), prepared)

                prepare_1(0)
                do(V.tensor_tensor(sq, ycT[:, 0:12, :], ycT[:, 0:12, :], ALU.mult), norm_sq)
                prepare_3(0)
                prepare_2(0)
                prepare_4(0)
                prepare_5(0)
                dve.wait_ge(norm_root, 2)
                do(V.reciprocal(rstd, rstd))
                for k in range(12):
                    do(V.scalar_tensor_tensor(ycT[:, k, :], ycT[:, k, :], col("branch", k), rstd[:, k // 4, :],
                                              ALU.mult, ALU.mult), wait=(k == 11))
                for i in range(GT):
                    AR = ARs[:, i % 2]
                    pe = lambda name: dve.wait_ge(pe_ev, at(PE_EV, i, name))
                    m4 = lambda m: c(m).unsqueeze(1).unsqueeze(1).to_broadcast([P, 2, TB, P])
                    eb = lambda a, d: a[:, d].rearrange("p (e b) k -> p e b k", e=2)

                    def masked(d, b0, half, dst, mask, sem=None, wait=True):
                        src = bank[:, b0:b0 + 2, 256 * 0:512].rearrange("p e (b k) -> p e b k", b=TB)
                        do(V.tensor_tensor(eb(mats[dst], d), src[:, :, :, P * half:P * half + P], m4(mask), ALU.mult), sem,
                           wait=wait)

                    for name, d, b0 in (("pa", 0, 0), ("pa", 1, 2), ("pc", 0, 4), ("pc", 1, 0)):
                        w = "UL"[d]
                        pe(f"{name}{d}")
                        if name == "pa":
                            masked(d, b0, 1, "Rb", "m32" + w + "i", wait=False)
                            masked(d, b0, 0, "NT", "m16" + w, wait=False)
                            masked(d, b0, 0, "NTo", "mX" + w, dve_ev)
                            do(V.tensor_tensor(mats["W"][:, d], mats["NT"][:, d],
                                               c("ident").unsqueeze(1).to_broadcast([P, 4, P]), ALU.add), wait=False)
                        else:
                            masked(d, b0, 0, "Aak", "m32" + w, wait=False)
                            masked(d, b0, 1, "Rk", "m32" + w + "i", dve_ev, wait=False)
                    for d in range(2):
                        pe(f"nn{d}")
                        src = bank[:, 2 + 2 * d:4 + 2 * d, 0:256].rearrange("p e (b k) -> p e b k", b=TB)
                        do(V.tensor_tensor(eb(mats["N"], d), src, m4("m16" + "LU"[d]), ALU.mult), dve_ev, wait=(d == 1))
                    for d in range(2):
                        do(V.tensor_tensor(diag[:, d], c("ident64").unsqueeze(1).to_broadcast([P, NCH, RH]),
                                           pend[:, d, :].unsqueeze(2).to_broadcast([P, NCH, RH]), ALU.mult), wait=(d == 1))

                    def grow(name):
                        for d in range(2):
                            pe(f"{name}{d}")
                            do(V.tensor_tensor(jk(mats["W"], d), bank[:, (0 if name == "w4" else 4) + d, :],
                                               jk(mats["W"], d), ALU.add), dve_ev, wait=False)

                    more = i < GT - 1
                    if more:
                        prepare_1(i + 1)
                        prepare_2(i + 1)
                    grow("w2")
                    grow("w4")
                    grow("w8")
                    if more:
                        prepare_3(i + 1)
                    for d in range(2):
                        pe(f"z{d}")
                        do(V.tensor_tensor(jk(R, d), bank[:, 4 + d, :], jk(R, d), ALU.add), dve_ev, wait=False)
                    if more:
                        prepare_4(i + 1)
                    for d in range(2):
                        pe(f"qy{d}")
                        do(V.tensor_tensor(s2(QT[:, 2 * i + d, :]), s2(bank[:, d, 0:SEQ]), AR[:, d, :, 1, :], ALU.add),
                           wait=False)
                        if d == 0:
                            do(V.tensor_copy(yin[:, i, :], bank[:, d, 256:512]), dve_ev)
                        else:
                            do(V.tensor_tensor(yin[:, i, :], bank[:, d, 256:512], yin[:, i, :], ALU.add), dve_ev)
                    if more:
                        prepare_5(i + 1)
                    for d in range(2):
                        pe(f"gh{d}")
                        dst = G[:, ::-1, 2 * i + d, :] if d else G[:, :, 2 * i + d, :]
                        src = bank[:, 2:6, 0:256].rearrange("p q (b n) -> p b q n", b=TB)[:, :, :, 0:RH]
                        do(V.tensor_tensor(dst.rearrange("p (b q) k -> p b q k", b=TB), src,
                                           diag[:, d].rearrange("p (b q) k -> p b q k", b=TB), ALU.add), dve_ev, wait=False)
                do(V.memset(S[:, 0], 0.0), state_ready)
                dve.wait_ge(act_ev, at(ACT_EV, GT - 1, "gh1"))
                for n in range(NCH - 1):
                    dve.wait_ge(state_mm, n + 1)
                    if n:
                        dve.wait_ge(out_mm, n)
                    do(V.tensor_tensor(S[:, (n + 1) % 2].rearrange("p q k -> p (q k)"), bank[:, 4 + n % 2, :],
                                       H[:, n].rearrange("p q k -> p (q k)"), ALU.add), state_ready)
                dve.wait_ge(out_mm, NCH)
                y2 = flat(yin[:]).rearrange("p (b n) -> p b n", b=2)
                do(V.tensor_tensor(y2, bank[:, 0:2, :], y2, ALU.add))
                do(V.tensor_tensor(y2, bank[:, 2:4, :], y2, ALU.add), y_ready)
                dve.wait_ge(stat_mm, 1)
                do(V.scalar_tensor_tensor(dlt.rearrange("p (b n) -> p b n", b=2), bank[:, 4:6, :], -1.0 / RH, y2,
                                          ALU.mult, ALU.add))
                do(V.tensor_tensor(sqd, dlt, dlt, ALU.mult), sqd_ready)
                dve.wait_ge(root_ready, 1)
                do(V.reciprocal(sqd, sqd))
                do(V.tensor_tensor(dlt, dlt, sqd, ALU.mult))
                for i in range(GT):
                    y = dlt[:, i * SEQ:i * SEQ + SEQ]
                    do(V.tensor_scalar(y, y, col("ln_w", i), col("ln_b", i), ALU.mult, ALU.add))
                do(V.tensor_tensor(dlt, dlt, flat(bonus[:]), ALU.add))
                do(V.tensor_tensor(flat(ycT[:, 12:16, :]), dlt, flat(gt[:]), ALU.mult))
                do(V.tensor_tensor(sq_d[:], ycT[:, 12:16, :], ycT[:, 12:16, :], ALU.mult), sq_d_ready)
                dve.wait_ge(root_ready, 2)
                do(V.reciprocal(rstd_d[:], rstd_d[:]))
                for k in range(12, KT):
                    do(V.scalar_tensor_tensor(ycT[:, k, :], ycT[:, k, :], col("branch", k), rstd_d[:], ALU.mult, ALU.mult),
                       wait=(k == KT - 1))


def query_piece(nc, t, layer, query, engine, h):
    engine.dma_start(query["w"][:, h % WRING], t["peer_w_query"][layer][:, h * P:(h + 1) * P]
                     .rearrange("(k p) n -> p k n", p=P)).then_inc(query["w_in"][h % WRING], 16)


def query_products(nc, query, bank, hT, h, first, last):
    for k in range(first, last):
        mm = nc.tensor.matmul(bank[:, h % 2, 0:SEQ], query["w"][:, h % WRING, k, :], hT[k // 4][:, k % 4, :], start=(k == 0),
                              stop=(k == KT - 1), skip_group_check=True)
    return mm


def route(nc, t, layer, sem, sb, bank, c, col, x, ycT, hT, score, query, out_w):
    small_in, x_added, turn_mm = sem("rt_small_in"), sem("rt_x"), sem("rt_turn_mm")
    sums_ready, sum_ready, rms_ready = sem("rt_sums"), sem("rt_sum"), sem("rt_rms")
    hT_ready, sk_mm, sk_out = sem("rt_hT"), sem("rt_sk_mm"), sem("rt_sk_out")
    dve_own, act_own = sem("rt_dve"), sem("rt_act")
    with ExitStack() as st:
        gain, skT, rms = query["gain"], query["skT"], query["rms"]
        sk = sb(st, "rt_sk", [P, PEER_H, 2, KEYS // 2])
        ssq = sb(st, "rt_ssq", [P, 2, 4])
        squares = sb(st, "rt_squares", [P, GW])

        with nc.Block() as block:
            @block.sync
            def _(sp):
                sp.dma_start(sk[:], t["peer_sub_keys"][layer].rearrange("h e k d -> k h e d")).then_inc(small_in, 16)
                sp.dma_start(gain[:], t["norm_ffn"][layer].unsqueeze(0).to_broadcast([P, D])).then_inc(small_in, 16)
                for i in range(EARLY + 2, len(OUT_PIECES)):
                    sp.wait_ge(out_w["used"], i - 1)
                    out_piece(nc, t, layer, out_w, sp, i)
                for h in range(WRING):
                    query_piece(nc, t, layer, query, sp, h)

            @block.tensor
            def _(pe):
                tr = nc.tensor.transpose

                def turn(g):
                    pe.wait_ge(x_added, 2 * g + 2)
                    a = 6 if g == 3 else out_bank(g)
                    for b in range(TB):
                        for k in range(4):
                            mm = tr(bank[:, a + b, k * P:k * P + P], x[:, b, (4 * g + k) * P:(4 * g + k + 1) * P], c("ident"))
                    mm.then_inc(turn_mm, 1)

                for i in range(EARLY, len(OUT_PIECES)):
                    if i == len(OUT_PIECES) - 2:
                        pe.wait_ge(small_in, 32)
                        pe.wait_ge(x_added, 2)
                        for h in range(PEER_H):
                            mm = tr(bank[:, 6 + h // 4, h % 4 * P:h % 4 * P + P], sk[:, h].rearrange("p e d -> p (e d)"),
                                    c("ident"))
                        mm.then_inc(sk_mm, 1)
                    if i == len(OUT_PIECES) - 1:
                        pe.wait_ge(sk_out, 2)
                        turn(0)
                        turn(1)
                    out_products(nc, out_w, bank, pe, ycT, i, 0, TB * HALF_K)
                turn(2)
                pe.wait_ge(query["w_in"][0], 16)
                pe.wait_ge(hT_ready, 2)
                query_products(nc, query, bank, hT, 0, 0, 8)
                turn(3)
                pe.wait_ge(hT_ready, 3)
                query_products(nc, query, bank, hT, 0, 8, 12)

            @block.scalar
            def _(act):
                do = Steps(act, act_own)
                A = nc.scalar
                for g in range(4):
                    if g == 2:
                        act.wait_ge(sk_mm, 1)
                        for i in range(2):
                            do(A.copy(skT[:, 4 * i:4 * i + 4].rearrange("p h k -> p (h k)"), bank[:, 6 + i, :]), sk_out)
                    for b in range(TB):
                        act.wait_ge(x_added, 2 * g + b + 1)
                        do(A.activation(squares[:], x[:, b, g * GW:(g + 1) * GW], ACT.Square,
                                        accum_out=ssq[:, b, g:g + 1]), sums_ready)
                act.wait_ge(sum_ready, 1)
                do(A.activation(rms[:, 1], rms[:, 0], ACT.Sqrt, scale=1.0 / D, bias=c("eps")), rms_ready)

            @block.vector
            def _(dve):
                do = Steps(dve, dve_own)
                V = nc.vector

                def turned(g):
                    dve.wait_ge(turn_mm, g + 1)
                    a = 6 if g == 3 else out_bank(g)
                    do(V.tensor_tensor(hT[g].rearrange("p k (b s) -> p b k s", b=TB),
                                       bank[:, a:a + 2, :].rearrange("p b (k s) -> p b k s", k=4),
                                       col("norm_ffn", 4 * g, 4).unsqueeze(1).unsqueeze(3).to_broadcast([P, TB, 4, P]),
                                       ALU.mult), hT_ready)

                for g in range(4):
                    if g == 3:
                        turned(0)
                        turned(1)
                    dve.wait_ge(out_w["used"], 5 + g)
                    for b in range(TB):
                        xs = x[:, b, g * GW:(g + 1) * GW]
                        do(V.tensor_tensor(xs, bank[:, out_bank(g) + b, :], xs, ALU.add), x_added)
                turned(2)
                turned(3)
                dve.wait_ge(sums_ready, 8)
                do(V.tensor_reduce(rms[:, 0], ssq[:], AX.X, ALU.add), sum_ready)
                dve.wait_ge(rms_ready, 1)
                do(V.reciprocal(rms[:, 2], rms[:, 1]))
                dve.wait_ge(small_in, 32)


def experts(nc, t, layer, sem, sb, bank, c, row_in, x, hT, h2, score, query, layer_base, arena):
    place_free, place_taken, dots_ready, gelu_ready, weight_ready, rows_ready, best_ready, exp_ready, top = [
        sem("ex_" + n) for n in ("place_free", "place_taken", "dots", "gelu", "weight", "rows", "best", "exp", "top")]
    q_mm, q_out, score_mm, score_out = [sem("ex_" + n) for n in ("q_mm", "q_out", "score_mm", "score_out")]
    with ExitStack() as st:
        h2_ready = sem("ex_h2")
        qT = sb(st, "ex_qT", [P, 2, SEQ])
        ring_2 = sb(st, "ex_ring", [P, RING - 4, D])
        place = lambda s: arena[:, s % RING * D:s % RING * D + D] if s % RING < 4 else ring_2[:, s % RING - 4, :]
        rows = sb(st, "ex_rows_b", [P, 2, TOPK], U32)
        dot = sb(st, "ex_dot", [P, 2, TOPK])
        gelu = sb(st, "ex_gelu_b", [P, 2, TOPK])
        gate = sb(st, "ex_gate", [P, 2, TOPK])
        total = sb(st, "ex_total", [P, 2, 2])
        weight = sb(st, "ex_weight_b", [P, 2, TOPK])
        keys = sb(st, "ex_keys", [P, 2, KEYS])
        left = sb(st, "ex_left", [P, 256])
        top_v = sb(st, "ex_top_v", [P, 2, TOPK])
        top_i = sb(st, "ex_top_i", [P, 2, TOPK], U32)
        top_f = sb(st, "ex_top_f", [P, 2, TOPK])
        cand = sb(st, "ex_cand", [P, TOPK, TOPK])
        best = sb(st, "ex_best_b", [P, 2, TOPK])
        pos = sb(st, "ex_pos", [P, TOPK], U32)
        half_u = sb(st, "ex_half_u", [P, 2, TOPK], U32)
        half_f = sb(st, "ex_half_f", [P, 2, TOPK])
        hot = sb(st, "ex_hot", [P, 2, TOPK, TOPK])
        pick = sb(st, "ex_pick", [P, 2, TOPK])
        tables = [t[n].rearrange("l e d -> (l e) d") for n in ("peer_u", "peer_v")]
        PER = 2 * TOPK
        laps = PER // RING

        with nc.Block() as block:
            @block.sync
            def _(sp):
                for h in range(WRING, PEER_H):
                    sp.wait_ge(q_mm, h - WRING + 1)
                    query_piece(nc, t, layer, query, sp, h)

            @block.tensor
            def _(pe):
                mmul = nc.tensor.matmul

                def scores(h):
                    pe.wait_ge(q_out, h + 1)
                    if h:
                        pe.wait_ge(score_out, 2 * h)
                    for b in range(TB):
                        for e in range(2):
                            r = slice(64 * e, 64 * e + 64)
                            mm = mmul(bank[:, 2 + e, b * P:b * P + P], qT[r, h % 2, b * P:b * P + P],
                                      query["skT"][r, h, :], start=(b == 0), stop=True, skip_group_check=True)
                    mm.then_inc(score_mm, 1)

                for h in range(PEER_H):
                    pe.wait_ge(query["w_in"][h % WRING], 16 * (h // WRING + 1))
                    query_products(nc, query, bank, hT, h, 0 if h else 12, KT).then_inc(q_mm, 1)
                    if h != 1:
                        scores(max(h - 1, 0))
                scores(PEER_H - 1)

            @block.gpsimd
            def _(pool):
                pool.sem_inc(place_free, RING)
                for b in range(TB):
                    with pool.Fori(0, PEER_H // 2) as pair:
                        for e in range(2):
                            head = pair * 2 + (b * PEER_H + e)
                            pool.wait_ge(rows_ready, head + 1)
                            for s in range(PER):
                                pool.wait_ge(place_free, head * PER + s + 1)
                                pool.sem_inc(place_taken, 1)
                                nc.gpsimd.indirect_dma_start(
                                    out=place(s), out_offset=None, in_=tables[s // TOPK][:, :],
                                    in_offset=bass.IndirectOffsetOnAxis(ap=rows[:, e, s % TOPK:s % TOPK + 1], axis=0))\
                                    .then_inc(row_in[s % RING], 16)

            @block.scalar
            def _(act):
                def gates(e, head):
                    act.wait_ge(best_ready, head + 1)
                    nc.scalar.activation(gate[:, e, :], best[:, e, :], ACT.Exp, accum_out=total[:, e, 0:1])\
                        .then_inc(exp_ready, 1)

                def scores_out(h):
                    act.wait_ge(score_mm, h + 1)
                    for b in range(TB):
                        nc.scalar.activation(score[:, b * PEER_H + h], bank[:, 2:4, b * P:b * P + P], ACT.Copy,
                                             scale=query["rms"][:, 2, b:b + 1]).then_inc(score_out, 1)

                for h in range(PEER_H):
                    act.wait_ge(q_mm, h + 1)
                    nc.scalar.copy(qT[:, h % 2, :], bank[:, h % 2, 0:SEQ]).then_inc(q_out, 1)
                    if h != 1:
                        scores_out(max(h - 1, 0))
                    if h == 2:
                        gates(0, 0)
                scores_out(PEER_H - 1)

                def weigh(e, head, last=False):
                    act.wait_ge(dots_ready, head + 1)
                    nc.scalar.activation(gelu[:, e, :], dot[:, e, :], ACT.Gelu).then_inc(gelu_ready, 1)
                    if not last:
                        gates(1 - e, head + 1)

                for b in range(TB):
                    with act.Fori(0, PEER_H // 2 - (b == TB - 1)) as pair:
                        for e in range(2):
                            weigh(e, pair * 2 + (b * PEER_H + e))
                for e in range(2):
                    weigh(e, TB * PEER_H - 2 + e, last=(e == 1))

            @block.vector
            def _(dve):
                V = nc.vector

                def find(e, head):
                    dve.sem_clear(top)
                    do = Steps(dve, top)

                    def top16(values, out_v, out_i):
                        rest = left[:, 0:values.shape[-1]]
                        do(V.max(out_v[:, 0:8], values))
                        do(V.max_index(out_i[:, 0:8], out_v[:, 0:8], values), wait=False)
                        do(V.match_replace(rest, out_v[:, 0:8], values, -3.0e38))
                        do(V.max(out_v[:, 8:16], rest))
                        do(V.max_index(out_i[:, 8:16], out_v[:, 8:16], rest))

                    src = score[:, head] if isinstance(head, int) else score[:, bass.ds(head, 1)]
                    do(V.tensor_copy(keys[:].rearrange("p e k -> p (e k)"),
                                     src.rearrange("p e k -> p (e k)" if isinstance(head, int) else "p h e k -> p (h e k)")))
                    for i in range(2):
                        top16(keys[:, i, :], top_v[:, i, :], top_i[:, i, :])
                    do(V.tensor_copy(top_f[:], top_i[:]), wait=False)
                    two = [P, TOPK, TOPK]
                    do(V.tensor_tensor(cand[:], top_v[:, 0].unsqueeze(2).to_broadcast(two),
                                       top_v[:, 1].unsqueeze(1).to_broadcast(two), ALU.add))
                    raw = pick[:, 0]
                    top16(cand[:].rearrange("p i j -> p (i j)"), raw, pos[:])
                    do(V.tensor_tensor(best[:, e], raw, raw[:, 0:1].to_broadcast([P, TOPK]), ALU.subtract), best_ready,
                       wait=False)
                    do(V.tensor_scalar(half_u[:, 0], pos[:], 4, None, ALU.logical_shift_right), wait=False)
                    do(V.tensor_scalar(half_u[:, 1], pos[:], 15, None, ALU.bitwise_and))
                    do(V.tensor_copy(half_f[:], half_u[:]))
                    three = [P, 2, TOPK, TOPK]
                    do(V.tensor_tensor(hot[:], half_f[:].unsqueeze(3).to_broadcast(three),
                                       c("iota16").unsqueeze(1).unsqueeze(1).to_broadcast(three), ALU.is_equal))
                    do(V.tensor_tensor(hot[:], hot[:], top_f[:].unsqueeze(2).to_broadcast(three), ALU.mult))
                    do(V.tensor_reduce(pick[:], hot[:], AX.X, ALU.add))
                    do(V.scalar_tensor_tensor(pick[:, 0], pick[:, 0], float(KEYS), pick[:, 1], ALU.mult, ALU.add))
                    do(V.tensor_scalar(rows[:, e], pick[:, 0], layer_base[:], None, ALU.add), rows_ready, wait=False)

                for b in range(TB):
                    V.scalar_tensor_tensor(h2[:, b, :], x[:, b, :], query["rms"][:, 2, b:b + 1], query["gain"][:],
                                           ALU.mult, ALU.mult).then_inc(h2_ready, 1)
                dve.wait_ge(score_out, 2)
                find(0, 0)
                dve.wait_ge(h2_ready, TB)

                def serve(b, e, head, last=False):
                    arrived = (layer * (TB * PEER_H) + head) * (16 * laps)
                    for s in range(TOPK):
                        dve.wait_ge(row_in[s % RING], arrived + 16 * (s // RING + 1))
                        V.tensor_tensor_reduce(out=place(s), in0=place(s), in1=h2[:, b, :],
                                               scale=1.0, scalar=0.0, op0=ALU.mult, op1=ALU.add,
                                               accum_out=dot[:, e, s:s + 1]).then_inc(place_free, 1)
                    dve.wait_ge(place_free, head * PER + TOPK + RING)
                    dve.sem_inc(dots_ready, 1)
                    if not last:
                        dve.wait_ge(score_out, 2 * PEER_H)
                        find(1 - e, head + 1)
                    dve.wait_ge(exp_ready, head + 1)
                    V.reciprocal(total[:, e, 1:2], total[:, e, 0:1]).then_inc(weight_ready, 1)
                    dve.wait_ge(weight_ready, head * 2 + 1)
                    dve.wait_ge(gelu_ready, head + 1)
                    V.scalar_tensor_tensor(weight[:, e, :], gate[:, e, :], total[:, e, 1:2], gelu[:, e, :],
                                           ALU.mult, ALU.mult).then_inc(weight_ready, 1)
                    dve.wait_ge(weight_ready, head * 2 + 2)
                    for s in range(TOPK, PER):
                        dve.wait_ge(row_in[s % RING], arrived + 16 * (s // RING + 1))
                        dve.wait_ge(place_free, head * PER + s + RING)
                        V.scalar_tensor_tensor(x[:, b, :], place(s),
                                               weight[:, e, s - TOPK:s - TOPK + 1], x[:, b, :], ALU.mult, ALU.add)\
                            .then_inc(place_free, 1)

                for b in range(TB):
                    with dve.Fori(0, PEER_H // 2 - (b == TB - 1)) as pair:
                        for e in range(2):
                            serve(b, e, pair * 2 + (b * PEER_H + e))
                for e in range(2):
                    serve(TB - 1, e, TB * PEER_H - 2 + e, last=(e == 1))
                V.tensor_scalar(layer_base[:], layer_base[:], float(EXPERTS), None, ALU.add).then_inc(weight_ready, 1)


_INS = ["x", "norm_mix", "w_in", "fourier_w", "s5_lam_re", "s5_lam_im", "s5_log_step", "s5_b_re", "s5_b_im", "s5_c_re",
        "s5_c_im", "s5_d", "s5_w_glu", "attn_q_norm", "attn_k_norm", "rwkv_mu", "rwkv_w0", "rwkv_w1", "rwkv_w2", "rwkv_a0",
        "rwkv_a1", "rwkv_a2", "rwkv_g1", "rwkv_g2", "rwkv_k_k", "rwkv_k_a", "rwkv_r_k", "rwkv_ln_w", "rwkv_ln_b",
        "branch_norm", "w_out", "norm_ffn", "peer_w_query", "peer_sub_keys", "peer_u", "peer_v"]


def kernel(**inputs):
    import concourse.bacc as bacc
    from concourse.bass_utils import run_bass_kernel_spmd

    nc = bacc.Bacc("TRN2", target_bir_lowering=False, num_devices=1)
    arrays = {f"in_{n}": np.ascontiguousarray(inputs[n]) for n in _INS}
    arrays["in_consts"] = constants()[0]
    t = {n[3:]: nc.dram_tensor(n, a.shape, mybir.dt.from_np(a.dtype), kind="ExternalInput").ap() for n, a in arrays.items()}
    out = nc.dram_tensor("out_x", (1, SEQ, D), F32, kind="ExternalOutput").ap()
    build(nc, t, out)
    r = run_bass_kernel_spmd(nc, [arrays], core_ids=[0])
    return r.results[0]["out_x"]
```
